# Optimizing a Trainium2 kernel written in Bass

```python
import math
import jax, jax.numpy as jnp
from jax import lax
import numpy as np

D_MODEL = 1024
BATCH = 1
SEQ = 256
DEPTH = 2

HEAD_DIM = 64
N_MIX_HEADS = D_MODEL // HEAD_DIM
CONV_WIDTH = D_MODEL // 4
CONV_GROUPS = CONV_WIDTH // HEAD_DIM
RET_HEADS = (N_MIX_HEADS - CONV_GROUPS) // 2
MOBA_HEADS = N_MIX_HEADS - CONV_GROUPS - RET_HEADS
RET_WIDTH = RET_HEADS * HEAD_DIM
MOBA_WIDTH = MOBA_HEADS * HEAD_DIM
IN_COLS = 4 * RET_WIDTH + 3 * MOBA_WIDTH + 3 * CONV_WIDTH
CONV_K = 3
RET_CHUNK = 128
MOBA_BLOCK = 256
MOBA_TOPK = 3
MOBA_Q_CHUNK = 16
REL_BUCKETS = 32
REL_MAX_DIST = 128
ROPE_BASE = 10000.0
D_FF = 256 * ((8 * D_MODEL // 3 + 255) // 256)
DN_ALPHA = (2.0 * DEPTH) ** 0.25
DN_BETA = (8.0 * DEPTH) ** -0.25
LN_EPS = 1e-5


F32 = jnp.float32

def layer_norm(x, g, b):
    xf = x.astype(F32)
    mu = jnp.mean(xf, axis=-1, keepdims=True)
    var = jnp.mean(jnp.square(xf - mu), axis=-1, keepdims=True)
    y = (xf - mu) * lax.rsqrt(var + LN_EPS)
    return (y * g.astype(F32) + b.astype(F32)).astype(x.dtype)

def causal_dwconv(x, w):
    K = w.shape[0]
    S = x.shape[1]
    xp = jnp.pad(x, ((0, 0), (K - 1, 0), (0, 0)))
    y = xp[:, 0:S] * w[0]
    for i in range(1, K):
        y = y + xp[:, i:i + S] * w[i]
    return y

def split_heads(t, n_heads):
    B, S, _ = t.shape
    return t.reshape(B, S, n_heads, HEAD_DIM).transpose(0, 2, 1, 3)

def merge_heads(t):
    B, H, S, dh = t.shape
    return t.transpose(0, 2, 1, 3).reshape(B, S, H * dh)

def rotary(t):
    S, dh = t.shape[2], t.shape[3]
    inv = ROPE_BASE ** (-jnp.arange(0, dh, 2, dtype=F32) / dh)
    ang = jnp.arange(S, dtype=F32)[:, None] * inv[None, :]
    cos, sin = jnp.cos(ang), jnp.sin(ang)
    t1, t2 = t[..., : dh // 2], t[..., dh // 2:]
    return jnp.concatenate([t1 * cos - t2 * sin, t1 * sin + t2 * cos], axis=-1)

def retention(q, k, v):
    B, H, S, dh = q.shape
    C = RET_CHUNK
    n = S // C
    log_g = jnp.log(1.0 - 2.0 ** (-5.0 - jnp.arange(H, dtype=F32)))
    idx = jnp.arange(C, dtype=F32)
    diff = idx[:, None] - idx[None, :]
    decay = jnp.where(diff >= 0, jnp.exp(jnp.maximum(diff, 0.0)[None] * log_g[:, None, None]), 0.0)
    xi = jnp.exp((idx + 1.0)[None, :] * log_g[:, None])
    zeta = jnp.exp((C - 1.0 - idx)[None, :] * log_g[:, None])
    g_chunk = jnp.exp(C * log_g)

    def to_chunks(t):
        return t.reshape(B, H, n, C, dh).transpose(2, 0, 1, 3, 4)

    def step(state, qkv):
        qc, kc, vc = qkv
        scores = jnp.einsum('bhcd,bhed->bhce', qc, kc) * decay[None]
        inner = jnp.einsum('bhce,bhev->bhcv', scores, vc)
        cross = jnp.einsum('bhcd,bhdv->bhcv', qc, state) * xi[None, :, :, None]
        state = state * g_chunk[None, :, None, None] + jnp.einsum(
            'bhcd,bhcv->bhdv', kc * zeta[None, :, :, None], vc)
        return state, inner + cross

    state0 = jnp.zeros((B, H, dh, dh), F32)
    _, out = lax.scan(step, state0, (to_chunks(q), to_chunks(k), to_chunks(v)))
    return out.transpose(1, 2, 0, 3, 4).reshape(B, H, S, dh)

def t5_bucket(dist):
    n = jnp.maximum(dist, 0)
    max_exact = REL_BUCKETS // 2
    nf = jnp.maximum(n, 1).astype(F32)
    large = max_exact + (jnp.log(nf / max_exact) / math.log(REL_MAX_DIST / max_exact)
                         * (REL_BUCKETS - max_exact)).astype(jnp.int32)
    large = jnp.minimum(large, REL_BUCKETS - 1)
    return jnp.where(n < max_exact, n, large)

def moba_attention(q, k, v, rel_bias):
    B, H, S, dh = q.shape
    L = MOBA_BLOCK
    nb = -(-S // L)
    pad = nb * L - S
    kp = jnp.pad(k, ((0, 0), (0, 0), (0, pad), (0, 0))).reshape(B, H, nb, L, dh)
    vp = jnp.pad(v, ((0, 0), (0, 0), (0, pad), (0, 0))).reshape(B, H, nb, L, dh)
    k_mean = jnp.mean(kp, axis=3)
    topk = min(MOBA_TOPK, nb)
    scale = dh ** -0.5
    rel_t = rel_bias.T.astype(F32)
    bi = jnp.arange(B)[:, None, None, None]
    hi = jnp.arange(H)[None, :, None, None]
    Qc = MOBA_Q_CHUNK
    nc = S // Qc
    q_chunks = q.reshape(B, H, nc, Qc, dh).transpose(2, 0, 1, 3, 4)

    def attend(args):
        qi, ci = args
        q_pos = ci * Qc + jnp.arange(Qc, dtype=jnp.int32)
        own = (ci * Qc) // L
        gate = jnp.einsum('bhqd,bhnd->bhqn', qi, k_mean)
        gate = jnp.where(jnp.arange(nb) < own, gate, -jnp.inf)
        _, sel = lax.top_k(gate, topk)
        sel_valid = jnp.arange(topk) < own
        kg = kp[bi, hi, sel]
        vg = vp[bi, hi, sel]
        k_pos_sel = sel[..., None] * L + jnp.arange(L, dtype=jnp.int32)
        b_sel = rel_t[hi[..., None], t5_bucket(q_pos[:, None, None] - k_pos_sel)]
        s_sel = jnp.einsum('bhqd,bhqjld->bhqjl', qi, kg) * scale + b_sel
        s_sel = jnp.where(sel_valid[:, None], s_sel, -jnp.inf)
        k_own = lax.dynamic_index_in_dim(kp, own, axis=2, keepdims=False)
        v_own = lax.dynamic_index_in_dim(vp, own, axis=2, keepdims=False)
        k_pos_own = own * L + jnp.arange(L, dtype=jnp.int32)
        dist_own = q_pos[:, None] - k_pos_own[None, :]
        b_own = rel_t[:, t5_bucket(dist_own)]
        s_own = jnp.einsum('bhqd,bhld->bhql', qi, k_own) * scale + b_own[None]
        s_own = jnp.where(dist_own >= 0, s_own, -jnp.inf)
        logits = jnp.concatenate([s_sel.reshape(B, H, Qc, topk * L), s_own], axis=-1)
        p = jax.nn.softmax(logits, axis=-1)
        p_sel = p[..., : topk * L].reshape(B, H, Qc, topk, L)
        p_own = p[..., topk * L:]
        return (jnp.einsum('bhqjl,bhqjld->bhqd', p_sel, vg)
                + jnp.einsum('bhql,bhld->bhqd', p_own, v_own))

    out = lax.map(attend, (q_chunks, jnp.arange(nc, dtype=jnp.int32)))
    return out.transpose(1, 2, 0, 3, 4).reshape(B, H, S, dh)

def head_group_norm(t):
    mu = jnp.mean(t, axis=-1, keepdims=True)
    var = jnp.mean(jnp.square(t - mu), axis=-1, keepdims=True)
    return (t - mu) * lax.rsqrt(var + LN_EPS)

def hybrid_mixer(h, w_in, conv_w, w_out, rel_bias):
    proj = h @ w_in
    o = np.cumsum([0, RET_WIDTH, RET_WIDTH, RET_WIDTH, RET_WIDTH,
                   MOBA_WIDTH, MOBA_WIDTH, MOBA_WIDTH, CONV_WIDTH, CONV_WIDTH, CONV_WIDTH])
    parts = [proj[..., int(o[i]):int(o[i + 1])] for i in range(10)]
    rq, rk, rv, rg, mq, mk, mv, cb, cc, ch = parts
    scale = HEAD_DIM ** -0.5
    q_r = rotary(split_heads(rq, RET_HEADS).astype(F32))
    k_r = rotary(split_heads(rk, RET_HEADS).astype(F32)) * scale
    v_r = split_heads(rv, RET_HEADS).astype(F32)
    y_ret = merge_heads(head_group_norm(retention(q_r, k_r, v_r))) * jax.nn.silu(rg.astype(F32))
    y_moba = merge_heads(moba_attention(split_heads(mq, MOBA_HEADS).astype(F32),
                                        split_heads(mk, MOBA_HEADS).astype(F32),
                                        split_heads(mv, MOBA_HEADS).astype(F32), rel_bias))
    y_conv = cb.astype(F32) * causal_dwconv(cc.astype(F32) * ch.astype(F32), conv_w.astype(F32))
    cat = jnp.concatenate([y_ret, y_moba, y_conv], axis=-1).astype(h.dtype)
    return cat @ w_out

def conv_ffn(h, w_up, ffn_conv_w, w_down):
    u = h @ w_up
    a, b = u[..., :D_FF], u[..., D_FF:]
    a = causal_dwconv(a, ffn_conv_w)
    return (jax.nn.gelu(a.astype(F32), approximate=False) * b.astype(F32)).astype(h.dtype) @ w_down

def first_inputs(seed: int = 0) -> dict:
    key = jax.random.key(seed)
    ks = jax.random.split(key, 12)
    nrm = jax.random.normal
    x = nrm(ks[0], (BATCH, SEQ, D_MODEL), F32)
    w_in = nrm(ks[1], (DEPTH, D_MODEL, IN_COLS), F32) * D_MODEL ** -0.5
    conv_w = nrm(ks[2], (DEPTH, CONV_K, CONV_WIDTH), F32) * CONV_K ** -0.5
    w_out = nrm(ks[3], (DEPTH, D_MODEL, D_MODEL), F32) * (D_MODEL ** -0.5 * DN_BETA)
    ln1_g = 1.0 + 0.02 * nrm(ks[4], (DEPTH, D_MODEL), F32)
    ln1_b = 0.02 * nrm(ks[5], (DEPTH, D_MODEL), F32)
    w_up = nrm(ks[6], (DEPTH, D_MODEL, 2 * D_FF), F32) * D_MODEL ** -0.5
    ffn_conv_w = nrm(ks[7], (DEPTH, CONV_K, D_FF), F32) * CONV_K ** -0.5
    w_down = nrm(ks[8], (DEPTH, D_FF, D_MODEL), F32) * (D_FF ** -0.5 * DN_BETA)
    ln2_g = 1.0 + 0.02 * nrm(ks[9], (DEPTH, D_MODEL), F32)
    ln2_b = 0.02 * nrm(ks[10], (DEPTH, D_MODEL), F32)
    rel_bias = 0.2 * nrm(ks[11], (REL_BUCKETS, MOBA_HEADS), F32)
    return {"x": x, "w_in": w_in, "conv_w": conv_w, "w_out": w_out,
            "ln1_g": ln1_g, "ln1_b": ln1_b, "w_up": w_up, "ffn_conv_w": ffn_conv_w,
            "w_down": w_down, "ln2_g": ln2_g, "ln2_b": ln2_b, "rel_bias": rel_bias}

def first_block(x, w_in, conv_w, w_out, ln1_g, ln1_b, w_up, ffn_conv_w, w_down, ln2_g, ln2_b, rel_bias):
    for l in range(DEPTH):
        mix = hybrid_mixer(x, w_in[l], conv_w[l], w_out[l], rel_bias)
        x = layer_norm(DN_ALPHA * x + mix, ln1_g[l], ln1_b[l])
        f = conv_ffn(x, w_up[l], ffn_conv_w[l], w_down[l])
        x = layer_norm(DN_ALPHA * x + f, ln2_g[l], ln2_b[l])
    return x


CTX_LEN = 256
GRID_W = 64
N_Q_HEADS = 8
N_KV_HEADS = 2
GQA_GROUP = N_Q_HEADS // N_KV_HEADS
Q_WIDTH = N_Q_HEADS * HEAD_DIM
KV_WIDTH = N_KV_HEADS * HEAD_DIM
CONV_WIDTH_2 = D_MODEL - Q_WIDTH
CONV_KERNEL = 31
IN_COLS_2 = Q_WIDTH + 2 * KV_WIDTH + 2 * CONV_WIDTH_2
Q_BLOCK = 128
ROPE_THETA = 10000.0
ATTN_SCALE = HEAD_DIM ** -0.5
PEER_HEADS = 8
PEER_KEYS = 128
PEER_N = PEER_KEYS * PEER_KEYS
PEER_QDIM = 128
PEER_HALF = PEER_QDIM // 2
PEER_TOPK = 16
PEER_CHUNK = 128
EPS = 1e-6


def rms(x):
    xf = x.astype(jnp.float32)
    return (xf * lax.rsqrt(jnp.mean(xf * xf, axis=-1, keepdims=True) + EPS)).astype(x.dtype)

def layer_norm_2(x, g, b):
    xf = x.astype(jnp.float32)
    mu = jnp.mean(xf, axis=-1, keepdims=True)
    var = jnp.mean(jnp.square(xf - mu), axis=-1, keepdims=True)
    return ((xf - mu) * lax.rsqrt(var + 1e-5)).astype(x.dtype) * g + b

def modulate(x, shift, scale):
    return rms(x) * (1 + scale) + shift

def rope_tables(row, col):
    n = HEAD_DIM // 4
    inv = ROPE_THETA ** (-jnp.arange(n, dtype=jnp.float32) / n)
    ang = jnp.concatenate([row.astype(jnp.float32)[:, None] * inv,
                           col.astype(jnp.float32)[:, None] * inv], axis=-1)
    return jnp.cos(ang), jnp.sin(ang)

def apply_rope(x, cos, sin):
    half = HEAD_DIM // 2
    x1, x2 = x[..., :half], x[..., half:]
    c = cos[None, :, None, :].astype(x.dtype)
    s = sin[None, :, None, :].astype(x.dtype)
    return jnp.concatenate([x1 * c - x2 * s, x1 * s + x2 * c], axis=-1)

def split_cols(p):
    return jnp.split(p, [Q_WIDTH, Q_WIDTH + KV_WIDTH, Q_WIDTH + 2 * KV_WIDTH], axis=-1)

def gqa_core(q, k, v):
    s = jnp.einsum('bqhgd,bkhd->bhgqk', q, k).astype(jnp.float32) * ATTN_SCALE
    p = jax.nn.softmax(s, axis=-1).astype(v.dtype)
    return jnp.einsum('bhgqk,bkhd->bqhgd', p, v)

def attend_latent(q, k_all, v_all):
    B, S = q.shape[:2]
    nb = S // Q_BLOCK
    qb = q.reshape(B, nb, Q_BLOCK, N_KV_HEADS, GQA_GROUP, HEAD_DIM).transpose(1, 0, 2, 3, 4, 5)
    o = lax.map(lambda qi: gqa_core(qi, k_all, v_all), qb)
    return o.transpose(1, 0, 2, 3, 4, 5).reshape(B, S, Q_WIDTH)

def attend_context(q, k, v):
    B, L = q.shape[:2]
    o = gqa_core(q.reshape(B, L, N_KV_HEADS, GQA_GROUP, HEAD_DIM), k, v)
    return o.reshape(B, L, Q_WIDTH)

def conformer_conv(u, conv_w, conv_b, ln_g, ln_b):
    a, gate = jnp.split(u, 2, axis=-1)
    g = a * jax.nn.sigmoid(gate)
    y = lax.conv_general_dilated(
        g, conv_w[:, None, :], window_strides=(1,),
        padding=[(CONV_KERNEL // 2, CONV_KERNEL // 2)],
        dimension_numbers=('NWC', 'WIO', 'NWC'),
        feature_group_count=CONV_WIDTH_2) + conv_b
    return jax.nn.silu(layer_norm_2(y, ln_g, ln_b))

def merge_groups(o_attn, o_conv, beta_attn, beta_conv, w_o):
    o = jnp.concatenate([rms(o_attn) * beta_attn, rms(o_conv) * beta_conv], axis=-1)
    return o @ w_o

def peer(h, w_pq, sub_keys, u_tab, v_tab):
    B, T, D = h.shape
    q = (h @ w_pq).reshape(B, T, PEER_HEADS, 2, PEER_HALF)
    s = jnp.einsum('bthcd,hckd->bthck', q, sub_keys).astype(jnp.float32)
    top_s, top_i = lax.top_k(s, PEER_TOPK)
    cand = top_s[..., 0, :, None] + top_s[..., 1, None, :]
    best_s, best_j = lax.top_k(cand.reshape(B, T, PEER_HEADS, PEER_TOPK * PEER_TOPK), PEER_TOPK)
    i1 = jnp.take_along_axis(top_i[..., 0, :], best_j // PEER_TOPK, axis=-1)
    i2 = jnp.take_along_axis(top_i[..., 1, :], best_j % PEER_TOPK, axis=-1)
    expert = i1 * PEER_KEYS + i2
    w = jax.nn.softmax(best_s, axis=-1)
    n_chunks = (B * T) // PEER_CHUNK
    hx = h.reshape(n_chunks, PEER_CHUNK, D)
    ex = expert.reshape(n_chunks, PEER_CHUNK, PEER_HEADS * PEER_TOPK)
    wx = w.reshape(n_chunks, PEER_CHUNK, PEER_HEADS * PEER_TOPK)

    def chunk(args):
        hc, ec, wc = args
        u = jnp.take(u_tab, ec, axis=0)
        act = jax.nn.gelu(jnp.einsum('cd,ced->ce', hc, u), approximate=False)
        v = jnp.take(v_tab, ec, axis=0)
        return jnp.einsum('ce,ced->cd', (act * wc).astype(h.dtype), v)

    return lax.map(chunk, (hx, ex, wx)).reshape(B, T, D)

def second_inputs(seed: int = 0) -> dict:
    key = jax.random.key(seed)
    ks = jax.random.split(key, 22)
    D = D_MODEL

    def nrm(k, shape, s):
        return jax.random.normal(k, shape, jnp.float32) * s

    return {
        "x": nrm(ks[0], (BATCH, SEQ, D), 1.0),
        "c": nrm(ks[1], (BATCH, D), 1.0),
        "ctx": nrm(ks[2], (BATCH, CTX_LEN, D), 1.0),
        "c_ctx": nrm(ks[3], (D,), 1.0),
        "w_mod": nrm(ks[4], (DEPTH, D, 6 * D), 0.5 * D ** -0.5),
        "b_mod": nrm(ks[5], (DEPTH, 6 * D), 0.02),
        "w_in": nrm(ks[6], (DEPTH, D, IN_COLS_2), D ** -0.5),
        "q_gain": 1.0 + nrm(ks[7], (DEPTH, HEAD_DIM), 0.02),
        "k_gain": 1.0 + nrm(ks[8], (DEPTH, HEAD_DIM), 0.02),
        "conv_w": nrm(ks[9], (DEPTH, CONV_KERNEL, CONV_WIDTH_2), CONV_KERNEL ** -0.5),
        "conv_b": nrm(ks[10], (DEPTH, CONV_WIDTH_2), 0.02),
        "ln_g": 1.0 + nrm(ks[11], (DEPTH, CONV_WIDTH_2), 0.02),
        "ln_b": nrm(ks[12], (DEPTH, CONV_WIDTH_2), 0.02),
        "beta_attn": 1.0 + nrm(ks[13], (DEPTH, Q_WIDTH), 0.02),
        "beta_conv": 1.0 + nrm(ks[14], (DEPTH, CONV_WIDTH_2), 0.02),
        "w_o": nrm(ks[15], (DEPTH, D, D), D ** -0.5),
        "peer_wq": nrm(ks[16], (DEPTH, D, PEER_HEADS * PEER_QDIM), D ** -0.5),
        "peer_keys": nrm(ks[17], (DEPTH, PEER_HEADS, 2, PEER_KEYS, PEER_HALF), PEER_HALF ** -0.5),
        "peer_u": nrm(ks[18], (DEPTH, PEER_N, D), D ** -0.5),
        "peer_v": nrm(ks[19], (DEPTH, PEER_N, D), 0.5),
        "final_g": 1.0 + nrm(ks[20], (D,), 0.02),
    }

def second_block(x, c, ctx, c_ctx, w_mod, b_mod, w_in, q_gain, k_gain, conv_w, conv_b, ln_g, ln_b,
              beta_attn, beta_conv, w_o, peer_wq, peer_keys, peer_u, peer_v, final_g):
    B, S, D = x.shape
    L = ctx.shape[1]
    ROWS = S // GRID_W
    row = jnp.repeat(jnp.arange(ROWS), GRID_W)
    col = jnp.tile(jnp.arange(GRID_W), ROWS)
    cos, sin = rope_tables(row, col)
    sc = jax.nn.silu(c)
    sc_ctx = jax.nn.silu(c_ctx)
    h_ctx = ctx
    for l in range(DEPTH):
        last = l == DEPTH - 1
        sh1, s1, g1, sh2, s2, g2 = jnp.split((sc @ w_mod[l] + b_mod[l])[:, None, :], 6, axis=-1)
        csh1, cs1, cg1, csh2, cs2, cg2 = jnp.split(sc_ctx @ w_mod[l] + b_mod[l], 6, axis=-1)

        hc = modulate(h_ctx, csh1, cs1)
        if last:
            kc, vc = jnp.split(hc @ w_in[l][:, Q_WIDTH:Q_WIDTH + 2 * KV_WIDTH], 2, axis=-1)
        else:
            qc, kc, vc, uc = split_cols(hc @ w_in[l])
            qc = rms(qc.reshape(B, L, N_Q_HEADS, HEAD_DIM)) * q_gain[l]
        kc = rms(kc.reshape(B, L, N_KV_HEADS, HEAD_DIM)) * k_gain[l]
        vc = vc.reshape(B, L, N_KV_HEADS, HEAD_DIM)

        hx = modulate(x, sh1, s1)
        q, k, v, u = split_cols(hx @ w_in[l])
        q = apply_rope(rms(q.reshape(B, S, N_Q_HEADS, HEAD_DIM)) * q_gain[l], cos, sin)
        k = apply_rope(rms(k.reshape(B, S, N_KV_HEADS, HEAD_DIM)) * k_gain[l], cos, sin)
        v = v.reshape(B, S, N_KV_HEADS, HEAD_DIM)
        o_attn = attend_latent(q, jnp.concatenate([kc, k], axis=1), jnp.concatenate([vc, v], axis=1))
        o_conv = conformer_conv(u, conv_w[l], conv_b[l], ln_g[l], ln_b[l])
        x = x + g1 * merge_groups(o_attn, o_conv, beta_attn[l], beta_conv[l], w_o[l])

        x = x + g2 * peer(modulate(x, sh2, s2), peer_wq[l], peer_keys[l], peer_u[l], peer_v[l])

        if not last:
            oc_attn = attend_context(qc, kc, vc)
            oc_conv = conformer_conv(uc, conv_w[l], conv_b[l], ln_g[l], ln_b[l])
            h_ctx = h_ctx + cg1 * merge_groups(oc_attn, oc_conv, beta_attn[l], beta_conv[l], w_o[l])
            h_ctx = h_ctx + cg2 * peer(modulate(h_ctx, csh2, cs2), peer_wq[l], peer_keys[l], peer_u[l], peer_v[l])

    return rms(x) * final_g


def setup_inputs(seed=0):
    out = dict(first_inputs(seed))
    for name, value in second_inputs(seed + 1).items():
        if name != "x":
            out[name + "_2"] = value
    return out


def reference(
    x, w_in, conv_w, w_out, ln1_g, ln1_b, w_up, ffn_conv_w, w_down, ln2_g, ln2_b, rel_bias, c_2,
    ctx_2, c_ctx_2, w_mod_2, b_mod_2, w_in_2, q_gain_2, k_gain_2, conv_w_2, conv_b_2, ln_g_2,
    ln_b_2, beta_attn_2, beta_conv_2, w_o_2, peer_wq_2, peer_keys_2, peer_u_2, peer_v_2,
    final_g_2,
):
    x = first_block(
        x, w_in, conv_w, w_out, ln1_g, ln1_b, w_up, ffn_conv_w, w_down, ln2_g, ln2_b, rel_bias,
    )
    return second_block(
        x, c_2, ctx_2, c_ctx_2, w_mod_2, b_mod_2, w_in_2, q_gain_2, k_gain_2, conv_w_2,
        conv_b_2, ln_g_2, ln_b_2, beta_attn_2, beta_conv_2, w_o_2, peer_wq_2, peer_keys_2,
        peer_u_2, peer_v_2, final_g_2,
    )


_drawn_inputs = setup_inputs


def setup_inputs(seed=0):
    import zlib

    import numpy as np

    out = dict(_drawn_inputs(seed))
    spreads = {}
    factors = {'rel_bias': 3.522,
     'q_gain_2': 8.0,
     'k_gain_2': 8.0,
     'conv_b_2': 3.861,
     'ln_g_2': 4.602,
     'ln_b_2': 5.14,
     'beta_attn_2': 5.265,
     'beta_conv_2': 5.383,
     'final_g_2': 2.825}
    for name, (base, spread) in spreads.items():
        noise = np.random.default_rng([zlib.crc32(name.encode()), seed]).standard_normal(out[name].shape)
        drawn = base * np.exp(spread * noise) if base else spread * noise
        out[name] = __import__('jax').numpy.asarray(drawn.astype(out[name].dtype))
    for name, factor in factors.items():
        out[name] = (out[name] * factor).astype(out[name].dtype)
    return out
```

```python
from contextlib import ExitStack

import concourse.bass as bass
import numpy as np
from concourse import mybir

F32 = mybir.dt.float32
I32 = mybir.dt.int32
U32 = mybir.dt.uint32
ALU = mybir.AluOpType
ACT = mybir.ActivationFunctionType
AX = mybir.AxisListType.X

P = 128
D = 1024
S = 256
TT = S // P
DK = D // P
L = 2
HD = 64

RET_H, MOBA_H = 6, 6
RW, MW, CW1 = 384, 384, 256
QKV1 = 4 * RW + 3 * MW
FF = 2816
FT = FF // P
ALPHA = (2.0 * L) ** 0.25
LN_EPS = 1e-5
REL_BUCKETS, REL_MAX = 32, 128
MASKED = -1.0e30

QH, KVH = 8, 2
QW, KVW = QH * HD, KVH * HD
CW2, TAPS2 = 512, 31
HALO = TAPS2 // 2
QKV2 = QW + 2 * KVW
RMS_EPS = 1e-6
EH, EK, TOPK = 8, 128, 16
PICKS = EH * TOPK
N_EXP = EK * EK
LOW = -3.0e38

RING = 8
WS = 4
WCOL = 4096

C_ID, C_FLIP, C_IOTA = 0, P, 2 * P
C_COS1, C_SIN1 = C_IOTA + 16, C_IOTA + 16 + TT * 32
C_COS2, C_SIN2 = C_SIN1 + TT * 32, C_SIN1 + 2 * TT * 32
C_END = C_SIN2 + TT * 32


class Groups:

    def __init__(self):
        self.n, self.at = 0, {}

    def mark(self, *name):
        self.n += 1
        self.at[name] = self.n
        return 1

    def of(self, *name):
        return self.at[name]


class Banks:

    def __init__(self, pe, banks):
        self.pe, self.banks, self.i, self.read_out = pe, banks, 0, {}

    def take(self, sem, value):
        b = self.banks[self.i % len(self.banks)]
        self.i += 1
        self.hold(b, sem, value)
        return b

    def hold(self, b, sem, value):
        if b in self.read_out:
            self.pe.wait_ge(*self.read_out[b])
        self.read_out[b] = (sem, value)


class Count:

    def __init__(self):
        self.n, self.reg, self.per = 0, 0, 0

    def next(self, step=1):
        self.n += step
        return self.value()

    def value(self):
        return self.n if self.per == 0 else self.n + self.reg * self.per

    def enter(self, reg, per):
        self.reg, self.per, self.start = reg, per, self.n

    def leave(self, rounds):
        assert self.n - self.start == self.per, (self.n - self.start, self.per)
        self.n = self.start + self.per * rounds
        self.per = 0


def program(nc, A, out):
    with ExitStack() as ctx:
        sems, named = [], {}

        def sem(name):
            sems.append(ctx.enter_context(nc.semaphore(name)))
            return sems[-1]

        def sbuf(name, shape, dt=F32, at=None):
            named[name] = named.get(name, 0) + 1
            name += f"_{named[name]}" if named[name] > 1 else ""
            return (at or ctx).enter_context(nc.sbuf_tensor(name, shape, dt))

        mod_stored = [sem(f"mod_stored{i}") for i in range(2)]
        row_landed = [sem(f"row_landed{i}") for i in range(RING)]
        sems.clear()
        consts_loaded = sem("consts_loaded")
        inputs_loaded = sem("inputs_loaded")
        rows_loaded = sem("rows_loaded")
        late_rows_loaded = sem("late_rows_loaded")
        weights_loaded = [sem(f"weights_loaded{i}") for i in range(WS)]
        stored = sem("stored")
        groups_done = sem("groups_done")
        dve_step = sem("dve_step")
        act_step = sem("act_step")
        silu_ready = sem("silu_ready")
        mod_read = sem("mod_read")
        stat_ready = sem("stat_ready")
        root_ready = sem("root_ready")
        norm_ready = sem("norm_ready")
        xT_ready = sem("xT_ready")
        cols_ready = sem("cols_ready")
        proj_ready = sem("proj_ready")
        conv_in_ready = sem("conv_in_ready")
        rot_ready = sem("rot_ready")
        qkT_ready = sem("qkT_ready")
        max_ready = sem("max_ready")
        probs_ready = sem("probs_ready")
        probsT_ready = sem("probsT_ready")
        ret_ready = sem("ret_ready")
        attn_ready = sem("attn_ready")
        conv_ready = sem("conv_ready")
        conv_read = sem("conv_read")
        act_in_ready = sem("act_in_ready")
        act_out_ready = sem("act_out_ready")
        merged_ready = sem("merged_ready")
        catT_ready = sem("catT_ready")
        mix_read = sem("mix_read")
        h_ready = sem("h_ready")
        picksT_ready = sem("picksT_ready")
        keysT_ready = sem("keysT_ready")
        score_read = sem("score_read")
        topk_free = sem("topk_free")
        up_loaded = [sem(f"up_loaded{i}") for i in range(2)]
        down_loaded = [sem(f"down_loaded{i}") for i in range(2)]
        up_read = sem("up_read")
        conv_done = sem("conv_done")
        gelu_done = sem("gelu_done")
        hidden_ready = sem("hidden_ready")
        picks_ready = sem("picks_ready")
        idx_copied = sem("idx_copied")
        gather_issued = sem("gather_issued")
        rows_used = sem("rows_used")
        dots_ready = sem("dots_ready")
        gelu_ready = sem("gelu_ready")
        coef_ready = sem("coef_ready")

        def phase_end():
            nc.all_engine_barrier(sems_to_clear=range(sems[0].num, sems[-1].num + 1))

        mod_dram = nc.dram_tensor("mod_dram", (L, 2, 6 * D), F32, kind="Internal").ap()
        rel_dram = nc.dram_tensor("rel_dram", (MOBA_H, 2 * S - 1), F32, kind="Internal")
        bias_dram = nc.dram_tensor("bias_dram", (P, MOBA_H * 3 * P), F32, kind="Internal").ap()

        cx_dram = nc.dram_tensor("cx_dram", (P, TT * D), F32, kind="Internal").ap()

        C = sbuf("C", [P, C_END])
        ident = C[:, C_ID:C_ID + P]
        flip = C[:, C_FLIP:C_FLIP + P]
        iota16 = C[:, C_IOTA:C_IOTA + TOPK]

        def angles(c0):
            return C[:, c0:c0 + TT * 32].rearrange("p (t o d) -> p t o d", t=TT, o=1)

        eps = sbuf("eps", [P, 2])
        X = sbuf("X", [P, TT, D])
        W = sbuf("W", [P, WS, WCOL])
        XT = sbuf("XT", [P, DK, S])
        CT = sbuf("CT", [P, DK, S])
        ROWS = sbuf("ROWS", [P, RING, D])
        H = sbuf("H", [P, TT, D])
        ACC = sbuf("ACC", [P, TT, D])
        PROD = sbuf("PROD", [P, D])
        G2ROW = XT[:].rearrange("p k s -> p (k s)")[:, 0:D]
        IDX = sbuf("IDX", [P, TT, PICKS], I32)
        IDXS = sbuf("IDXS", [P, 2, RING], I32)
        WGT = sbuf("WGT", [P, TT, PICKS])
        DOT = sbuf("DOT", [P, TT, PICKS])
        DOT8 = sbuf("DOT8", [P, 2, RING])
        COEF = sbuf("COEF", [P, TT, PICKS])
        BASE = sbuf("BASE", [P, 1])
        KTC = sbuf("KTC", [P, L, KVH, S])
        VC = sbuf("VC", [P, L, TT, KVW])
        st = sbuf("st", [P, 2, 16])
        rt = sbuf("rt", [P, 2, 16])
        ri = sbuf("ri", [P, 2, 16])
        PS = ctx.enter_context(nc.psum_tensor("PS", [P, 8, 512], F32))

        x_dram = A["x"].rearrange("o (t p) d -> p (o t) d", p=P)
        ctx_dram = A["ctx_2"].rearrange("o (t p) d -> p (o t) d", p=P)
        out_dram = out.rearrange("o (t p) d -> p (o t) d", p=P)
        tables = {n: A[n].rearrange("l n d -> (l n) d") for n in ("peer_u_2", "peer_v_2")}

        def wview(name, l):
            return A[name].rearrange("l (k p) n -> l p k n", p=P)[l]

        def wslot(s, k, n):
            return W[:, s, 0:k * n].rearrange("p (k n) -> p k n", k=k)

        def dve_chain(dve):
            count = Count()

            def link(ins):
                ins.then_inc(dve_step, 1)
                dve.wait_ge(dve_step, count.next())

            link.count = count
            return link


        def transposes(pe, banks, groups, name, src, n_k, sem_, base, width=P):
            for j in range(0, n_k, 2):
                b = banks.take(sem_, base + j // 2 + 1)
                for k in range(j, min(j + 2, n_k)):
                    for t in range(TT):
                        o = ((k - j) * TT + t) * P
                        ins = nc.tensor.transpose(PS[:, b, o:o + P], src(t, k), ident)
                ins.then_inc(groups_done, groups.mark(name, j // 2))
                groups.at[name, j // 2, "bank"] = b

        def matmul_rows(pe, b, cols, lhs, rhs, n_k, start=True, stop=True):
            for k in range(n_k):
                ins = nc.tensor.matmul(PS[:, b, cols[0]:cols[1]], lhs(k), rhs(k),
                                       start=start and k == 0, stop=stop and k == n_k - 1)
            return ins

        def weights_in(pe, chunk):
            pe.wait_ge(weights_loaded[chunk % WS], 16 * (chunk // WS + 1))

        def gather_rows(pool, table, src, rounds, n0):
            with pool.Fori(0, PICKS // (2 * RING)) as e:
                for half in range(2):
                    pool.wait_ge(rows_used, e * 2 * RING + n0 + half * RING + 1)
                    nc.gpsimd.tensor_copy(IDXS[:, half, :], src(e * 2 + half)).then_inc(idx_copied, 1)
                    for k in range(RING):
                        pool.wait_ge(rows_used, e * 2 * RING + n0 + half * RING + k + 1)
                        pool.sem_inc(gather_issued, 1)
                        if k == 0:
                            pool.wait_ge(idx_copied, e * 2 + n0 // RING + half + 1)
                            pool.sem_inc(gather_issued, 1)
                        nc.gpsimd.indirect_dma_start(
                            ROWS[:, k, :], None, tables[table],
                            bass.IndirectOffsetOnAxis(IDXS[:, half, k:k + 1], 0),
                        ).then_inc(row_landed[k], 16)

        def dot_steps(dve, h, dots, n8, before, link):
            for k in range(RING):
                dve.wait_ge(row_landed[k], (n8 + before) * 16 + 16)
                nc.vector.tensor_tensor_reduce(ROWS[:, k, :], ROWS[:, k, :], h, 1.0, 0.0, ALU.mult, ALU.add,
                                               DOT8[:, 0, k:k + 1]).then_inc(rows_used, 1)
            dve.wait_ge(rows_used, n8 * RING + 2 * RING)
            link(nc.vector.tensor_copy(dots, DOT8[:, 0, :]))

        def sum_steps(dve, acc, coef, n8, before):
            for k in range(RING):
                dve.wait_ge(row_landed[k], (n8 + before) * 16 + 16)
                dve.wait_ge(rows_used, n8 * RING + RING + k)
                nc.vector.scalar_tensor_tensor(acc, ROWS[:, k, :], coef(k), acc, ALU.mult,
                                               ALU.add).then_inc(rows_used, 1)

        with ExitStack() as ph:
            SCR = sbuf("SCR", [16, P], at=ph)
            SCS = sbuf("SCS", [16, P], at=ph)
            SC = sbuf("SC", [P, 16], at=ph)
            BM = ROWS[:].rearrange("p k d -> p (k d)")
            ONE = sbuf("ONE", [64, 2], at=ph)
            MODS = sbuf("MODS", [2, 2, 512], at=ph)
            REL = sbuf("REL", [REL_BUCKETS + 1, MOBA_H], at=ph)
            BUCK = sbuf("BUCK", [REL_BUCKETS + 1, 2 * S - 1], at=ph)
            RELT = sbuf("RELT", [MOBA_H, 2 * S - 1], at=ph)
            HANK = sbuf("HANK", [P, MOBA_H, 3 * P], at=ph)
            BIAS = sbuf("BIASS", [P, MOBA_H, 3 * P], at=ph)
            NMOD = L * 12
            with nc.Block() as block:
                groups = Groups()

                @block.tensor
                def _(pe):
                    banks = Banks(pe, list(range(8)))
                    pe.wait_ge(consts_loaded, 16)
                    pe.wait_ge(silu_ready, 1)
                    b = banks.take(cols_ready, 1)
                    nc.tensor.transpose(PS[:, b, 0:16], SCS[:], ident[0:16, 0:16]).then_inc(
                        groups_done, groups.mark("sc"))
                    pe.wait_ge(inputs_loaded, 6 * 16)
                    pe.wait_ge(dve_step, 3)
                    b = banks.take(act_step, 1)
                    nc.tensor.matmul(PS[0:MOBA_H, b, 0:2 * S - 1], REL[:], BUCK[:], start=True,
                                     stop=True).then_inc(groups_done, groups.mark("rel"))
                    pe.wait_ge(cols_ready, 1)
                    for c in range(NMOD):
                        weights_in(pe, c)
                        b = banks.take(mod_read, c + 1)
                        for k in range(DK):
                            nc.tensor.matmul(PS[0:2, b, :], SC[:, k:k + 9:8], wslot(c % WS, DK, 512)[:, k, :],
                                             start=(k == 0), stop=False)
                        q = 32 * (c // 12)
                        nc.tensor.matmul(PS[0:2, b, :], ONE[q:q + 1, :], BM[q:q + 1, (c % 12) * 512:(c % 12 + 1) * 512],
                                         start=False, stop=True).then_inc(groups_done, groups.mark("mod", c))
                    pe.wait_ge(late_rows_loaded, 12 * 16)
                    for h in range(MOBA_H):
                        b = banks.take(score_read, h + 1)
                        nc.tensor.matmul(PS[:, b, 0:3 * P], flip, HANK[:, h, :], start=True,
                                         stop=True).then_inc(groups_done, groups.mark("bias", h))

                @block.sync
                def _(sp):
                    sp.dma_start(SCR[0:8, :], A["c_2"].rearrange("o (k p) -> (o k) p", p=P)).then_inc(inputs_loaded, 16)
                    sp.dma_start(SCR[8:16, :], A["c_ctx_2"].rearrange("(k p) -> k p", p=P)).then_inc(inputs_loaded, 16)
                    sp.dma_start(C[:], A["consts"]).then_inc(consts_loaded, 16)
                    for l in range(L):
                        sp.dma_start(BM[32 * l:32 * l + 1, 0:6 * D], A["b_mod_2"][l:l + 1, :]).then_inc(inputs_loaded, 16)
                    sp.dma_start(REL[0:REL_BUCKETS, :], A["rel_bias"]).then_inc(inputs_loaded, 16)
                    sp.dma_start(BUCK[:], A["buckets"]).then_inc(inputs_loaded, 16)
                    sp.dma_start(X[:], x_dram).then_inc(rows_loaded, 16)
                    for c in range(NMOD):
                        if c >= WS:
                            sp.wait_ge(groups_done, groups.of("mod", c - WS))
                        sp.dma_start(wslot(c % WS, DK, 512), wview("w_mod_2", c // 12)[:, :, (c % 12) * 512:(c % 12 + 1) * 512]
                                     ).then_inc(weights_loaded[c % WS], 16)
                    sp.wait_ge(rows_loaded, 16)

                @block.scalar
                def _(act):
                    act.wait_ge(inputs_loaded, 6 * 16)
                    nc.scalar.activation(SCS[:], SCR[:], ACT.Silu).then_inc(silu_ready, 1)
                    act.wait_ge(groups_done, groups.of("rel"))
                    nc.scalar.copy(RELT[:], PS[0:MOBA_H, 1, 0:2 * S - 1]).then_inc(act_step, 1)
                    act.wait_ge(act_step, 1)
                    act.dma_start(rel_dram.ap(), RELT[:]).then_inc(stored, 16)
                    act.wait_ge(stored, 16)
                    for h in range(MOBA_H):
                        for first, n, o in ((P, P, 0), (0, 2 * P, P)):
                            src = bass.AP(rel_dram, h * (2 * S - 1) + first, [[1, P], [1, n]])
                            act.dma_start(HANK[:, h, o:o + n], src).then_inc(late_rows_loaded, 16)
                    for h in range(MOBA_H):
                        act.wait_ge(groups_done, groups.of("bias", h))
                        nc.scalar.copy(BIAS[:, h, :], PS[:, (2 + NMOD + h) % 8, 0:3 * P]).then_inc(score_read, 1)
                    act.wait_ge(score_read, MOBA_H)
                    act.dma_start(bias_dram, BIAS[:].rearrange("p h n -> p (h n)")).then_inc(stored, 16)
                    act.wait_ge(stored, 32)

                @block.vector
                def _(dve):
                    link = dve_chain(dve)
                    link(nc.vector.memset(ONE[:], 1.0))
                    link(nc.vector.memset(REL[REL_BUCKETS:REL_BUCKETS + 1, :], 1.0))
                    link(nc.vector.memset(eps[:, 0:1], LN_EPS))
                    nc.vector.memset(eps[:, 1:2], RMS_EPS)
                    nc.vector.memset(BASE[:], 0.0)
                    dve.wait_ge(groups_done, groups.of("sc"))
                    nc.vector.tensor_copy(SC[:], PS[:, 0, 0:16]).then_inc(cols_ready, 1)
                    for c in range(NMOD):
                        dve.wait_ge(groups_done, groups.of("mod", c))
                        if c >= 2:
                            dve.wait_ge(mod_stored[c % 2], 16 * (c // 2))
                        nc.vector.tensor_copy(MODS[:, c % 2, :], PS[0:2, (2 + c) % 8, :]).then_inc(mod_read, 1)

                @block.gpsimd
                def _(pool):
                    for c in range(NMOD):
                        pool.wait_ge(mod_read, c + 1)
                        pool.dma_start(mod_dram[c // 12, :, (c % 12) * 512:(c % 12 + 1) * 512], MODS[:, c % 2, :]
                                       ).then_inc(mod_stored[c % 2], 16)
                    for i in range(2):
                        pool.wait_ge(mod_stored[i], 16 * NMOD // 2)
            phase_end()


        def stream_buffers(ph, latent):
            B = {}
            B["PROJ"] = sbuf("PROJ2", [P, TT, QKV2], at=ph)
            B["QR"] = sbuf("QR", [P, TT, QW + 2 * KVW], at=ph)
            B["T1"] = PROD[:, 0:TT * 320].rearrange("p (t n) -> p t n", t=TT)
            B["T2"] = sbuf("T2", [P, TT, 10 * 32], at=ph)
            B["QT"] = sbuf("QT", [P, QH // 2, S], at=ph)
            B["KT"] = sbuf("KT", [P, KVH, 2 * S], at=ph)
            B["V"] = sbuf("V", [P, 2 * TT, KVW], at=ph)
            B["GAIN"] = sbuf("GAIN", [P, 2, HD], at=ph)
            B["COLR"] = sbuf("COLR", [TAPS2 + 3, CW2], at=ph)
            B["COLC"] = sbuf("COLC", [P, CW2 // P, TAPS2 + 3], at=ph)
            B["MODR"] = sbuf("MODR", [16, P], at=ph)
            B["MODC"] = sbuf("MODC", [P, 16], at=ph)
            B["LNR"] = sbuf("LNR", [P, 2, CW2], at=ph)
            B["ROW"] = [ACC[:, 0, :], ACC[:, 1, :], sbuf("ROW", [P, D], at=ph)[:]]
            AR = ROWS[:].rearrange("p k d -> p (k d)")
            B["U"] = AR[:, 0:2048].rearrange("p (j s) -> p j s", j=8)
            B["PAD"] = AR[:, 2048:2048 + 4 * (S + 2 * HALO)].rearrange("p (j s) -> p j s", j=4)
            B["PR"] = AR[:, 4096:5120].rearrange("p (i n) -> p i n", i=2)
            B["PT"] = AR[:, 5120:6144].rearrange("p (i n) -> p i n", i=2)
            B["O"] = AR[:, 6144:7168].rearrange("p (t n) -> p t n", t=TT)
            B["Y"] = AR[:, 7168:8192].rearrange("p (t n) -> p t n", t=TT)
            B["SC"] = AR[:, 0:2048]
            B["CAND"] = AR[:, 2048:4096]
            B["HOT"] = AR[:, 4096:6144]
            B["QPT"] = AR[:, 6144:8192].rearrange("p (h s) -> p h s", h=EH)
            B["KPT"] = B["QR"][:].rearrange("p t n -> p (t n)")[:, 0:1024].rearrange("p (h k) -> p h k", h=EH)
            B["KEYS"] = B["PROJ"][:].rearrange("p t n -> p (t n)")[:, 0:1024]
            B["TV"] = sbuf("TV", [P, 2 * EH, TOPK], at=ph)
            B["TI"] = sbuf("TI", [P, 2 * EH, TOPK], U32, at=ph)
            B["TF"] = sbuf("TF", [P, 2 * EH, TOPK], at=ph)
            B["BV"] = sbuf("BV", [P, EH, TOPK], at=ph)
            B["BJ"] = sbuf("BJ", [P, EH, TOPK], U32, at=ph)
            B["J"] = sbuf("J", [P, 2, PICKS], U32, at=ph)
            B["JF"] = sbuf("JF", [P, 2, PICKS], at=ph)
            B["EI"] = sbuf("EI", [P, 3, PICKS], at=ph)
            B["SUM"] = sbuf("SUM", [P, 2, TT * QH], at=ph)
            B["NMAX"] = sbuf("NMAX", [P, TT * QH], at=ph)
            B["BN"] = sbuf("BN", [P, TT, 8], at=ph)
            return B

        CHUNKS2 = [("w_in_2", 0, 512), ("w_in_2", 512, 256), ("w_in_2", 768, 512), ("w_in_2", 1280, 512),
                   ("w_o_2", 0, 512), ("w_o_2", 512, 512), ("peer_wq_2", 0, 512), ("peer_wq_2", 512, 512)]

        def stream_pe(pe, groups, B, latent):
            banks = Banks(pe, [0, 1, 2, 3, 4, 5])
            nk = 2 * S if latent else S
            pe.wait_ge(rows_loaded, 16 * 6)
            b = banks.take(cols_ready, 1)
            for j in range(CW2 // P):
                nc.tensor.transpose(PS[:, b, j * 34:j * 34 + 34], B["COLR"][:, j * P:(j + 1) * P], ident[0:34, 0:34])
            nc.tensor.transpose(PS[:, b, 136:152], B["MODR"][:], ident[0:16, 0:16]).then_inc(
                groups_done, groups.mark("cols"))
            pe.wait_ge(norm_ready, TT)
            transposes(pe, banks, groups, "xT", lambda t, k: CT_tok(B)[:, t, k * P:(k + 1) * P], DK, xT_ready, 0)
            pe.wait_ge(xT_ready, 4)
            for c, (o, n) in enumerate(((0, 512), (512, 256))):
                weights_in(pe, c)
                for t in range(TT):
                    b = banks.take(proj_ready, c * TT + t + 1)
                    matmul_rows(pe, b, (0, n), lambda k: XT[:, k, t * P:(t + 1) * P],
                                lambda k: wslot(c, DK, n)[:, k, :], DK).then_inc(
                        groups_done, groups.mark("proj", c, t))
                    groups.at["proj", c, t, "bank"] = b
            for j in range(8):
                c = 2 + j // 4
                if j % 4 == 0:
                    weights_in(pe, c)
                b = banks.take(conv_in_ready, j + 1)
                matmul_rows(pe, b, (0, S), lambda k: wslot(c, DK, 512)[:, k, (j % 4) * P:(j % 4 + 1) * P],
                            lambda k: XT[:, k, :], DK).then_inc(groups_done, groups.mark("u", j))
                groups.at["u", j, "bank"] = b
            pe.wait_ge(rot_ready, 1)
            transposes(pe, banks, groups, "qk", lambda t, k: B["QR"][:, t, k * P:(k + 1) * P], 6, qkT_ready, 0)
            pe.wait_ge(qkT_ready, 3)
            n = TT * QH
            nb = nk // P
            for i in range(n + 2):
                if i < n:
                    t, h = divmod(i, QH)
                    q0 = HD * (h % 2)
                    b = banks.take(probs_ready, i + 1)
                    nc.tensor.matmul(PS[:, b, 0:nk], B["QT"][q0:q0 + HD, h // 2, t * P:(t + 1) * P],
                                     B["KT"][q0:q0 + HD, h // (QH // KVH), 0:nk], start=True, stop=True
                                     ).then_inc(groups_done, groups.mark("score", i))
                    groups.at["score", i, "bank"] = b
                if 1 <= i <= n:
                    j = i - 1
                    pe.wait_ge(probs_ready, j + 1)
                    b = banks.take(probsT_ready, j + 1)
                    for kb in range(nb):
                        ins = nc.tensor.transpose(PS[:, b, kb * P:(kb + 1) * P], B["PR"][:, j % 2, kb * P:(kb + 1) * P], ident)
                    ins.then_inc(groups_done, groups.mark("pT", j))
                    groups.at["pT", j, "bank"] = b
                if i >= 2:
                    j = i - 2
                    t, h = divmod(j, QH)
                    pe.wait_ge(probsT_ready, j + 1)
                    kv = h // (QH // KVH)
                    for kb in range(nb):
                        ins = nc.tensor.matmul(PS[:, 6 + t, h * HD:(h + 1) * HD], B["PT"][:, j % 2, kb * P:(kb + 1) * P],
                                               B["V"][:, kb, kv * HD:(kv + 1) * HD], start=(kb == 0), stop=(kb == nb - 1))
                    ins.then_inc(groups_done, groups.mark("pv", j))
            pe.wait_ge(conv_ready, 1)
            for t in range(TT):
                b = banks.take(conv_read, t + 1)
                for j in range(CW2 // P):
                    ins = nc.tensor.transpose(PS[:, b, j * P:(j + 1) * P], B["U"][:, j, t * P:(t + 1) * P], ident)
                ins.then_inc(groups_done, groups.mark("convT", t))
                groups.at["convT", t, "bank"] = b
            pe.wait_ge(merged_ready, 1)
            transposes(pe, banks, groups, "oT", lambda t, k: B["O"][:, t, k * P:(k + 1) * P], 4, catT_ready, 0)
            pe.wait_ge(merged_ready, 2)
            transposes(pe, banks, groups, "yT", lambda t, k: B["Y"][:, t, k * P:(k + 1) * P], 4, catT_ready, 2)
            pe.wait_ge(catT_ready, 4)
            for c in range(2):
                weights_in(pe, 4 + c)
                for t in range(TT):
                    b = banks.take(mix_read, c * TT + t + 1)
                    matmul_rows(pe, b, (0, 512), lambda k: CT[:, k, t * P:(t + 1) * P],
                                lambda k: wslot(c, DK, 512)[:, k, :], DK).then_inc(
                        groups_done, groups.mark("mix", c, t))
                    groups.at["mix", c, t, "bank"] = b
            pe.wait_ge(late_rows_loaded, 16 * 2)
            for g in range(2):
                b = banks.take(keysT_ready, g + 1)
                for h in range(4):
                    o = (g * 4 + h) * P
                    ins = nc.tensor.transpose(PS[:, b, h * P:(h + 1) * P], B["KEYS"][:, o:o + P], ident)
                ins.then_inc(groups_done, groups.mark("keys", g))
                groups.at["keys", g, "bank"] = b
            pe.wait_ge(h_ready, 1)
            transposes(pe, banks, groups, "hT", lambda t, k: H[:, t, k * P:(k + 1) * P], DK, xT_ready, 4)
            pe.wait_ge(xT_ready, 8)
            for j in range(EH):
                if j % 4 == 0:
                    weights_in(pe, 6 + j // 4)
                b = banks.take(picksT_ready, j + 1)
                matmul_rows(pe, b, (0, S), lambda k: wslot(2 + j // 4, DK, 512)[:, k, (j % 4) * P:(j % 4 + 1) * P],
                            lambda k: XT[:, k, :], DK).then_inc(groups_done, groups.mark("pq", j))
                groups.at["pq", j, "bank"] = b
            pe.wait_ge(keysT_ready, 2)
            for t in range(TT):
                for g in range(4):
                    b = banks.take(score_read, t * 4 + g + 1)
                    for i in range(4):
                        h, c = (g // 2) * 4 + i, g % 2
                        if i == 0:
                            pe.wait_ge(picksT_ready, h + 4)
                        ins = nc.tensor.matmul(PS[:, b, i * P:(i + 1) * P], B["QPT"][c * HD:(c + 1) * HD, h, t * P:(t + 1) * P],
                                               B["KPT"][c * HD:(c + 1) * HD, h, :], start=True, stop=True)
                    ins.then_inc(groups_done, groups.mark("ps", t, g))
                    groups.at["ps", t, g, "bank"] = b

        def CT_tok(B):
            return CT[:].rearrange("p k s -> p (k s)").rearrange("p (t d) -> p t d", t=TT)

        def stream_sp(sp, groups, B, l, who):
            m = mod_dram[l][who:who + 1]
            sp.dma_start(B["MODR"][:], m[:, 0:2 * D].rearrange("o (k p) -> (o k) p", p=P)).then_inc(rows_loaded, 16)
            sp.dma_start(B["COLR"][0:TAPS2, :], A["conv_w_2"][l]).then_inc(rows_loaded, 16)
            for i, name in enumerate(("conv_b_2", "beta_attn_2", "beta_conv_2")):
                sp.dma_start(B["COLR"][TAPS2 + i:TAPS2 + i + 1, :], A[name].rearrange("(o l) n -> l o n", o=1)[l]
                             ).then_inc(rows_loaded, 16)
            sp.dma_start(B["GAIN"][:, 0, :], A["q_gain_2"].rearrange("(o l) n -> l o n", o=1)[l].to_broadcast([P, HD])
                         ).then_inc(rows_loaded, 16)
            for c in range(4):
                name, o, n = CHUNKS2[c]
                sp.dma_start(wslot(c, DK, n), wview(name, l)[:, :, o:o + n]).then_inc(weights_loaded[c], 16)
            sp.dma_start(B["GAIN"][:, 1, :], A["k_gain_2"].rearrange("(o l) n -> l o n", o=1)[l].to_broadcast([P, HD])
                         ).then_inc(inputs_loaded, 16)
            for i, name in enumerate(("ln_g_2", "ln_b_2")):
                sp.dma_start(B["LNR"][:, i, :], A[name].rearrange("(o l) n -> l o n", o=1)[l].to_broadcast([P, CW2])
                             ).then_inc(inputs_loaded, 16)
            for i in range(3):
                sp.dma_start(B["ROW"][i], m[:, (2 + i) * D:(3 + i) * D].to_broadcast([P, D])).then_inc(inputs_loaded, 16)
            for c in range(4, 8):
                name, o, n = CHUNKS2[c]
                last = {4: ("proj", 0, 1), 5: ("proj", 1, 1), 6: ("u", 3), 7: ("u", 7)}[c]
                sp.wait_ge(groups_done, groups.of(*last))
                sp.dma_start(wslot(c % WS, DK, n), wview(name, l)[:, :, o:o + n]).then_inc(weights_loaded[c % WS], 16)
            sp.wait_ge(rot_ready, 1)
            for c in range(2):
                sp.dma_start(B["KEYS"].rearrange("p (h c d) -> p h c d", h=EH, c=2)[:, :, c, :],
                             A["peer_keys_2"][l][:, c].rearrange("h k d -> k h d")).then_inc(late_rows_loaded, 16)
            sp.wait_ge(groups_done, groups.of("pq", EH - 1))
            sp.dma_start(G2ROW, m[:, 5 * D:6 * D].to_broadcast([P, D])).then_inc(rows_loaded, 16)

        def root(act, n, i, scale, e):
            act.wait_ge(stat_ready, i + 1)
            nc.scalar.activation(rt[:, i % 2, 0:n], st[:, i % 2, 0:n], ACT.Sqrt, bias=eps[:, e:e + 1],
                                 scale=scale).then_inc(root_ready, 1)

        def stream_act(act, groups, B, l, latent):
            nk = 2 * S if latent else S

            def bank(*name):
                act.wait_ge(groups_done, groups.of(*name))
                return groups.at[name + ("bank",)]

            root(act, TT, 0, 1.0 / D, 1)
            act.wait_ge(cols_ready, 1)
            for j in range(DK // 2):
                b = bank("xT", j)
                for k in range(2):
                    ins = nc.scalar.activation(XT[:, 2 * j + k, :], PS[:, b, k * S:(k + 1) * S], ACT.Identity,
                                               bias=B["MODC"][:, 2 * j + k:2 * j + k + 1],
                                               scale=B["MODC"][:, 8 + 2 * j + k:9 + 2 * j + k])
                ins.then_inc(xT_ready, 1)
            for c, (o, n) in enumerate(((0, 512), (512, 256))):
                for t in range(TT):
                    b = bank("proj", c, t)
                    nc.scalar.copy(B["PROJ"][:, t, o:o + n], PS[:, b, 0:n]).then_inc(proj_ready, 1)
            for j in range(8):
                b = bank("u", j)
                nc.scalar.activation(B["U"][:, j, :], PS[:, b, 0:S], ACT.Identity if j < 4 else ACT.Sigmoid
                                     ).then_inc(conv_in_ready, 1)
            root(act, TT * 10 // 2, 1, 1.0 / HD, 1)
            root(act, TT * 10 // 2, 2, 1.0 / HD, 1)
            for j in range(3):
                b = bank("qk", j)
                if j < 2:
                    nc.scalar.copy(B["QT"][:, 2 * j:2 * j + 2, :].rearrange("p k s -> p (k s)"), PS[:, b, :]
                                   ).then_inc(qkT_ready, 1)
                else:
                    nc.scalar.copy(B["KT"][:, :, nk - S:nk], PS[:, b, :].rearrange("p (k s) -> p k s", k=KVH)
                                   ).then_inc(qkT_ready, 1)
            for i in range(TT * QH):
                act.wait_ge(max_ready, i + 1)
                if i >= 2:
                    act.wait_ge(groups_done, groups.of("pT", i - 2))
                nc.scalar.activation(B["PR"][:, i % 2, 0:nk], PS[:, groups.at["score", i, "bank"], 0:nk], ACT.Exp,
                                     bias=B["NMAX"][:, i:i + 1], accum_out=B["SUM"][:, 0, i:i + 1]
                                     ).then_inc(probs_ready, 1)
            root(act, TT, 3, 1.0 / QW, 1)
            root(act, TT, 4, 1.0, 0)
            act.wait_ge(act_in_ready, 1)
            nc.scalar.activation(B["Y"], B["Y"], ACT.Silu).then_inc(act_out_ready, 1)
            for j in range(2):
                b = bank("oT", j)
                for k in range(2):
                    ins = nc.scalar.activation(CT[:, 2 * j + k, :], PS[:, b, k * S:(k + 1) * S], ACT.Copy,
                                               scale=B["COLC"][:, 2 * j + k, TAPS2 + 1:TAPS2 + 2])
                ins.then_inc(catT_ready, 1)
            root(act, TT, 5, 1.0 / CW2, 1)
            for j in range(2):
                b = bank("yT", j)
                for k in range(2):
                    ins = nc.scalar.activation(CT[:, 4 + 2 * j + k, :], PS[:, b, k * S:(k + 1) * S], ACT.Copy,
                                               scale=B["COLC"][:, 2 * j + k, TAPS2 + 2:TAPS2 + 3])
                ins.then_inc(catT_ready, 1)
            for g in range(2):
                b = bank("keys", g)
                nc.scalar.copy(B["KPT"][:, 4 * g:4 * g + 4, :].rearrange("p h k -> p (h k)"), PS[:, b, :]
                               ).then_inc(keysT_ready, 1)
            root(act, TT, 6, 1.0 / D, 1)
            for j in range(DK // 2):
                b = bank("hT", j)
                nc.scalar.copy(XT[:, 2 * j:2 * j + 2, :].rearrange("p k s -> p (k s)"), PS[:, b, :]).then_inc(xT_ready, 1)
            for j in range(EH):
                b = bank("pq", j)
                nc.scalar.copy(B["QPT"][:, j, :], PS[:, b, 0:S]).then_inc(picksT_ready, 1)
            for t in range(TT):
                if t:
                    act.wait_ge(topk_free, t)
                for g in range(4):
                    b = bank("ps", t, g)
                    dst = B["SC"].rearrange("p (h c k) -> p h c k", c=2, k=EK)[:, (g // 2) * 4:(g // 2) * 4 + 4, g % 2, :]
                    nc.scalar.copy(dst, PS[:, b, :].rearrange("p (h k) -> p h k", h=4)).then_inc(score_read, 1)
                act.wait_ge(act_in_ready, 2 + t)
                nc.scalar.activation(B["EI"][:, 2, :], B["EI"][:, 2, :], ACT.Exp).then_inc(act_out_ready, 1)

        def stream_dve(dve, link, groups, B, SRC, l, latent):
            cur = {"stat": 0}

            def inverse_root(n, ins):
                i = cur["stat"]
                ins.then_inc(stat_ready, 1)
                cur["stat"] += 1
                dve.wait_ge(root_ready, i + 1)
                link(nc.vector.reciprocal(ri[:, i % 2, 0:n], rt[:, i % 2, 0:n]))
                return ri[:, i % 2]

            def sum_squares(src, width):
                i = cur["stat"] % 2
                for t in range(TT):
                    ins = nc.vector.tensor_tensor_reduce(PROD[:, 0:width], src(t), src(t), 1.0, 0.0, ALU.mult,
                                                         ALU.add, st[:, i, t:t + 1])
                    if t < TT - 1:
                        link(ins)
                return ins

            r = inverse_root(TT, sum_squares(lambda t: SRC[:, t, :], D))
            for t in range(TT):
                nc.vector.tensor_scalar(CT_tok(B)[:, t, :], SRC[:, t, :], r[:, t:t + 1], None, ALU.mult).then_inc(norm_ready, 1)
            dve.wait_ge(groups_done, groups.of("cols"))
            nc.vector.tensor_copy(B["MODC"][:, 0:8], PS[:, 0, 136:144])
            nc.vector.tensor_scalar(B["MODC"][:, 8:16], PS[:, 0, 144:152], 1.0, None, ALU.add)
            nc.vector.tensor_copy(B["COLC"][:].rearrange("p j n -> p (j n)"), PS[:, 0, 0:136]).then_inc(cols_ready, 1)
            dve.wait_ge(inputs_loaded, 16 * 6)
            link(nc.vector.tensor_scalar(B["ROW"][2], B["ROW"][2], 1.0, None, ALU.add))
            link(nc.vector.tensor_scalar(B["GAIN"][:, 0, :], B["GAIN"][:, 0, :], HD ** -0.5, None, ALU.mult))
            nc.vector.memset(B["PAD"][:, :, 0:HALO], 0.0)
            link(nc.vector.memset(B["PAD"][:, :, HALO + S:S + 2 * HALO], 0.0))
            dve.wait_ge(proj_ready, 4)
            for t in range(TT):
                link(nc.vector.tensor_tensor(PROD[:, 0:640], B["PROJ"][:, t, 0:640], B["PROJ"][:, t, 0:640], ALU.mult))
                r = inverse_root(10, nc.vector.tensor_reduce(st[:, cur["stat"] % 2, 0:10],
                                                             PROD[:, 0:640].rearrange("p (h d) -> p h d", h=10), AX, ALU.add))
                q = B["PROJ"][:, t, 0:640].rearrange("p (h d) -> p h d", h=10)
                link(nc.vector.tensor_tensor(q, q, r[:, 0:10].rearrange("p (h o) -> p h o", o=1).to_broadcast([P, 10, HD]), ALU.mult))
                for i, (a, b) in enumerate(((0, 8), (8, 10))):
                    ins = nc.vector.tensor_tensor(q[:, a:b, :], q[:, a:b, :], B["GAIN"][:, i:i + 1, :].to_broadcast([P, b - a, HD]), ALU.mult)
                link(ins)
            kdst = B["QR"][:, :, QW:].rearrange("p t (h c d) -> p t h c d", h=KVH, c=2)
            if latent:
                cos, sin = angles(C_COS2), angles(C_SIN2)
                for a, b in ((0, 8), (8, 10)):
                    src = B["PROJ"][:, :, a * HD:b * HD].rearrange("p t (h d) -> p t h d", h=b - a)
                    q1, q2 = src[:, :, :, 0:32], src[:, :, :, 32:64]
                    n = b - a
                    t1 = B["T1"][:, :, 0:n * 32].rearrange("p t (h d) -> p t h d", h=n)
                    t2 = B["T2"][:, :, 0:n * 32].rearrange("p t (h d) -> p t h d", h=n)
                    cb, sb_ = cos.to_broadcast([P, TT, n, 32]), sin.to_broadcast([P, TT, n, 32])
                    for half, (f1, f2, op) in enumerate(((cb, sb_, ALU.subtract), (sb_, cb, ALU.add))):
                        nc.vector.tensor_tensor(t1, q1, f1, ALU.mult)
                        link(nc.vector.tensor_tensor(t2, q2, f2, ALU.mult))
                        if a == 0:
                            dst = [B["QR"][:, :, 0:QW].rearrange("p t (h d) -> p t h d", h=n)[:, :, :, half * 32:half * 32 + 32]]
                        else:
                            dst = [kdst[:, :, :, c, half * 32:half * 32 + 32] for c in range(2)]
                        for d in dst:
                            ins = nc.vector.tensor_tensor(d, t1, t2, op)
                        link(ins)
            else:
                nc.vector.tensor_copy(B["QR"][:, :, 0:QW], B["PROJ"][:, :, 0:QW])
                for c in range(2):
                    ins = nc.vector.tensor_copy(kdst[:, :, :, c, :], B["PROJ"][:, :, QW:QW + KVW].rearrange("p t (h d) -> p t h d", h=KVH))
                link(ins)
            v0 = TT if latent else 0
            link(nc.vector.tensor_copy(B["V"][:, v0:v0 + TT, :], B["PROJ"][:, :, QW + KVW:QKV2]))
            if latent:
                for h in range(KVH):
                    nc.vector.tensor_copy(B["KT"][:, h, 0:S], KTC[:].rearrange("p l h s -> p (l h) s")[:, bass.ds(l * KVH + h, 1), :].rearrange("p o s -> p (o s)"))
                link(nc.vector.tensor_copy(B["V"][:, 0:TT, :], VC[:].rearrange("p l t n -> p l (t n)")[:, bass.ds(l, 1), :].rearrange("p o n -> p (o n)").rearrange("p (t n) -> p t n", t=TT)))
            dve.sem_inc(rot_ready, 1)
            nk = 2 * S if latent else S
            dve.wait_ge(conv_in_ready, 8)
            link(nc.vector.tensor_tensor(B["PAD"][:, :, HALO:HALO + S], B["U"][:, 0:4, :], B["U"][:, 4:8, :], ALU.mult))
            n = TT * QH
            for i in range(n + 1):
                if i < n:
                    dve.wait_ge(groups_done, groups.of("score", i))
                    nc.vector.tensor_reduce(B["NMAX"][:, i:i + 1], PS[:, groups.at["score", i, "bank"], 0:nk], AX, ALU.max,
                                            negate=True).then_inc(max_ready, 1)
                if i >= 1:
                    j = i - 1
                    dve.wait_ge(groups_done, groups.of("pT", j))
                    if j >= 2:
                        dve.wait_ge(groups_done, groups.of("pv", j - 2))
                    nc.vector.tensor_copy(B["PT"][:, j % 2, 0:nk], PS[:, groups.at["pT", j, "bank"], 0:nk]).then_inc(probsT_ready, 1)
            if not latent:
                dve.wait_ge(qkT_ready, 3)
                nc.vector.tensor_copy(KTC[:, 0], B["KT"][:, :, 0:S])
                nc.vector.tensor_copy(VC[:, 0], B["V"][:, 0:TT, :])
            link(nc.vector.reciprocal(B["SUM"][:, 1, :], B["SUM"][:, 0, :]))
            dve.wait_ge(groups_done, groups.of("pv", n - 1))
            for t in range(TT):
                ins = nc.vector.tensor_tensor(B["O"][:, t, :].rearrange("p (h d) -> p h d", h=QH),
                                              PS[:, 6 + t, :].rearrange("p (h d) -> p h d", h=QH),
                                              B["SUM"][:, 1, t * QH:(t + 1) * QH].rearrange("p (h o) -> p h o", o=1).to_broadcast([P, QH, HD]), ALU.mult)
            link(ins)
            r = inverse_root(TT, sum_squares(lambda t: B["O"][:, t, :], QW))
            for t in range(TT):
                ins = nc.vector.tensor_scalar(B["O"][:, t, :], B["O"][:, t, :], r[:, t:t + 1], None, ALU.mult)
            ins.then_inc(merged_ready, 1)
            for k in range(TAPS2):
                for j in range(4):
                    tap = B["COLC"][:, j, k:k + 1]
                    if k == 0:
                        ins = nc.vector.tensor_scalar(B["U"][:, j, :], B["PAD"][:, j, 0:S], tap, B["COLC"][:, j, TAPS2:TAPS2 + 1], ALU.mult, ALU.add)
                    else:
                        ins = nc.vector.scalar_tensor_tensor(B["U"][:, j, :], B["PAD"][:, j, k:k + S], tap, B["U"][:, j, :], ALU.mult, ALU.add)
                if k < TAPS2 - 1:
                    link(ins)
            ins.then_inc(conv_ready, 1)
            i = cur["stat"] % 2
            for t in range(TT):
                dve.wait_ge(groups_done, groups.of("convT", t))
                b = groups.at["convT", t, "bank"]
                link(nc.vector.bn_stats(B["BN"][:, t, 0:6], PS[:, b, :]))
                link(nc.vector.bn_aggr(B["BN"][:, t, 6:8], B["BN"][:, t, 0:6]))
            r = inverse_root(TT, nc.vector.tensor_copy(st[:, i, 0:TT], B["BN"][:, :, 7]))
            for t in range(TT):
                b = groups.at["convT", t, "bank"]
                nc.vector.tensor_scalar(B["Y"][:, t, :], PS[:, b, :], B["BN"][:, t, 6:7], r[:, t:t + 1], ALU.subtract, ALU.mult
                                        ).then_inc(conv_read, 1)
            dve.wait_ge(conv_read, TT)
            link(nc.vector.tensor_tensor(B["Y"], B["Y"], B["LNR"][:, 0:1, :].to_broadcast([P, TT, CW2]), ALU.mult))
            nc.vector.tensor_tensor(B["Y"], B["Y"], B["LNR"][:, 1:2, :].to_broadcast([P, TT, CW2]), ALU.add).then_inc(act_in_ready, 1)
            dve.wait_ge(act_out_ready, 1)
            r = inverse_root(TT, sum_squares(lambda t: B["Y"][:, t, :], CW2))
            for t in range(TT):
                ins = nc.vector.tensor_scalar(B["Y"][:, t, :], B["Y"][:, t, :], r[:, t:t + 1], None, ALU.mult)
            ins.then_inc(merged_ready, 1)
            for c in range(2):
                for t in range(TT):
                    dve.wait_ge(groups_done, groups.of("mix", c, t))
                    b = groups.at["mix", c, t, "bank"]
                    cols = slice(c * 512, (c + 1) * 512)
                    ins = nc.vector.tensor_tensor(H[:, t, cols], PS[:, b, :], B["ROW"][0][:, cols], ALU.mult)
                    ins.then_inc(mix_read, 1)
            dve.wait_ge(mix_read, 4)
            nc.vector.tensor_tensor(SRC[:], SRC[:], H[:], ALU.add).then_inc(merged_ready, 1)
            dve.wait_ge(merged_ready, 3)
            r = inverse_root(TT, sum_squares(lambda t: SRC[:, t, :], D))
            for t in range(TT):
                ins = nc.vector.scalar_tensor_tensor(H[:, t, :], SRC[:, t, :], r[:, t:t + 1], B["ROW"][2], ALU.mult, ALU.mult)
            link(ins)
            nc.vector.tensor_tensor(H[:], H[:], B["ROW"][1].rearrange("p (o d) -> p o d", o=1).to_broadcast([P, TT, D]), ALU.add).then_inc(h_ready, 1)

            def best(vals, idx, src, groups_):
                for rnd in range(2):
                    o = slice(8 * rnd, 8 * rnd + 8)
                    for g in range(groups_):
                        ins = nc.vector.max(vals[:, g, o], src[:, g, :])
                    link(ins)
                    for g in range(groups_):
                        ins = nc.vector.max_index(idx[:, g, o], vals[:, g, o], src[:, g, :])
                    link(ins)
                    if rnd == 0:
                        for g in range(groups_):
                            ins = nc.vector.match_replace(src[:, g, :], vals[:, g, o], src[:, g, :], LOW)
                        link(ins)

            for t in range(TT):
                dve.wait_ge(score_read, 4 * (t + 1))
                best(B["TV"], B["TI"], B["SC"].rearrange("p (g k) -> p g k", k=EK), 2 * EH)
                dve.sem_inc(topk_free, 1)
                link(nc.vector.tensor_copy(B["TF"][:], B["TI"][:]))
                tv = B["TV"][:].rearrange("p (h c) k -> p h c k", c=2)
                tf = B["TF"][:].rearrange("p (h c) k -> p h c k", c=2)
                cand = B["CAND"].rearrange("p (h a b) -> p h a b", h=EH, a=TOPK)
                link(nc.vector.tensor_tensor(cand, tv[:, :, 0, :].rearrange("p h (k o) -> p h k o", o=1).to_broadcast([P, EH, TOPK, TOPK]),
                                             tv[:, :, 1:2, :].to_broadcast([P, EH, TOPK, TOPK]), ALU.add))
                best(B["BV"], B["BJ"], B["CAND"].rearrange("p (h n) -> p h n", h=EH), EH)
                bj = B["BJ"][:].rearrange("p h k -> p (h k)")
                nc.vector.tensor_scalar(B["J"][:, 0, :], bj, 4, None, ALU.logical_shift_right)
                link(nc.vector.tensor_scalar(B["J"][:, 1, :], bj, TOPK - 1, None, ALU.bitwise_and))
                link(nc.vector.tensor_copy(B["JF"][:], B["J"][:]))
                hot = B["HOT"].rearrange("p (h a b) -> p h a b", h=EH, a=TOPK)
                hotf = B["HOT"].rearrange("p (n b) -> p n b", b=TOPK)
                for c in range(2):
                    link(nc.vector.tensor_tensor(hotf, B["JF"][:, c, :].rearrange("p (n o) -> p n o", o=1).to_broadcast([P, PICKS, TOPK]),
                                                 iota16.rearrange("p (o k) -> p o k", o=1).to_broadcast([P, PICKS, TOPK]), ALU.is_equal))
                    link(nc.vector.tensor_tensor(hot, hot, tf[:, :, c:c + 1, :].to_broadcast([P, EH, TOPK, TOPK]), ALU.mult))
                    link(nc.vector.tensor_reduce(B["EI"][:, c, :], hotf, AX, ALU.add))
                link(nc.vector.scalar_tensor_tensor(B["EI"][:, 0, :], B["EI"][:, 0, :], float(EK), B["EI"][:, 1, :], ALU.mult, ALU.add))
                nc.vector.tensor_scalar(IDX[:, t, :], B["EI"][:, 0, :], BASE[:, 0:1], None, ALU.add).then_inc(picks_ready, 1)
                ei = B["EI"][:, 2, :].rearrange("p (h k) -> p h k", h=EH)
                nc.vector.tensor_tensor(ei, B["BV"][:], B["BV"][:, :, 0:1].to_broadcast([P, EH, TOPK]), ALU.subtract).then_inc(act_in_ready, 1)
                dve.wait_ge(act_out_ready, 2 + t)
                link(nc.vector.tensor_reduce(B["SUM"][:, 0, 0:EH], ei, AX, ALU.add))
                link(nc.vector.reciprocal(B["SUM"][:, 1, 0:EH], B["SUM"][:, 0, 0:EH]))
                link(nc.vector.tensor_tensor(WGT[:, t, :].rearrange("p (h k) -> p h k", h=EH), ei,
                                             B["SUM"][:, 1, 0:EH].rearrange("p (h o) -> p h o", o=1).to_broadcast([P, EH, TOPK]), ALU.mult))

        with ExitStack() as ph:
            B = stream_buffers(ph, False)
            CX = sbuf("CX", [P, TT, D], at=ph)
            with nc.Block() as block:
                groups = Groups()

                @block.tensor
                def _(pe):
                    stream_pe(pe, groups, B, False)

                @block.sync
                def _(sp):
                    sp.dma_start(CX[:], ctx_dram).then_inc(consts_loaded, 16)
                    stream_sp(sp, groups, B, 0, 1)
                    sp.wait_ge(merged_ready, 3)
                    sp.dma_start(cx_dram, CX[:].rearrange("p t d -> p (t d)")).then_inc(stored, 16)
                    sp.wait_ge(stored, 16)
                    sp.wait_ge(rows_loaded, 16 * 7)

                @block.scalar
                def _(act):
                    stream_act(act, groups, B, 0, False)

                @block.vector
                def _(dve):
                    dve.wait_ge(consts_loaded, 16)
                    stream_dve(dve, dve_chain(dve), groups, B, CX, 0, False)
            phase_end()

        with ExitStack() as ph:
            PROJ = sbuf("PROJ1", [P, TT, QKV1], at=ph)
            DEC = sbuf("DEC", [P, RET_H, 3 * P], at=ph)
            BIAS = sbuf("BIAS", [P, MOBA_H, 3 * P], at=ph)
            PP = sbuf("PP", [P, 4 * 3 * P], at=ph)
            CF = sbuf("CF", [P, 6 * S], at=ph)
            GP = sbuf("GP", [P, 2, S + 2], at=ph)
            RAW = sbuf("RAW", [3 * FT + 6, P], at=ph)
            COLS = sbuf("COLS", [P, 3 * FT + 6], at=ph)
            ALPHAI = sbuf("ALPHAI", [P, P], at=ph)
            NM = sbuf("NM1", [P, 2 * MOBA_H], at=ph)
            SUM = sbuf("SUM1", [P, 2, 2 * MOBA_H], at=ph)
            BN = sbuf("BN1", [P, TT, 14], at=ph)
            RQ, RV, RG, MQ, MV = 0, 2 * RW, 3 * RW, 4 * RW, 4 * RW + 2 * MW
            QROT = CT[:].rearrange("p k s -> p (k s)")[:, 0:TT * 2 * RW].rearrange("p (t n) -> p t n", t=TT)
            SQ = CT[:].rearrange("p k s -> p (k s)")[:, 0:TT * RW].rearrange("p (t n) -> p t n", t=TT)
            RT = XT

            def MT(k):
                return PROJ[:, k // 3, (k % 3) * S:(k % 3 + 1) * S]

            T1 = PP[:, 0:768].rearrange("p (t h d) -> p t h d", t=TT, h=12)
            T2 = PP[:, 768:1536].rearrange("p (t h d) -> p t h d", t=TT, h=12)
            PR = PP[:, 0:768].rearrange("p (i n) -> p i n", i=2)
            PT = PP[:, 768:1536].rearrange("p (i n) -> p i n", i=2)
            YR = PROJ[:, :, MQ:MQ + RW]
            YM = PROJ[:, :, MQ + RW:MQ + RW + MW]
            CONV = CF[:].rearrange("p (j s) -> p j s", j=6)
            APAD = CF[:, 0:4 * (S + 2)].rearrange("p (i j s) -> p i j s", i=2, j=2)
            HC = PP[:, 0:1024].rearrange("p (i j s) -> p i j s", i=2, j=2)
            HG = [PP[:, 1024:1536].rearrange("p (j s) -> p j s", j=2), PROJ[:, 0, 2048:2560].rearrange("p (j s) -> p j s", j=2)]
            PAIRS = FT // 2
            PROJ_CH = [(o, min(512, QKV1 - o)) for o in range(0, QKV1, 512)]
            CONV_CH = [(QKV1, 512), (QKV1 + 512, 256)]
            IN_CH = PROJ_CH + CONV_CH
            NPC = len(PROJ_CH)
            V_ROUNDS = PICKS // RING

            with nc.Fori(0, L) as l:
                with nc.Block() as block:
                    groups = Groups()
                    taken = {}

                    @block.tensor
                    def _(pe):
                        banks = Banks(pe, [0, 1, 2, 3])
                        pe.wait_ge(inputs_loaded, 16 * 2)
                        b = banks.take(cols_ready, 1)
                        nc.tensor.transpose(PS[:, b, 0:3 * FT + 6], RAW[:], ident[0:3 * FT + 6, 0:3 * FT + 6]).then_inc(
                            groups_done, groups.mark("cols"))
                        transposes(pe, banks, groups, "xT", lambda t, k: X[:, t, k * P:(k + 1) * P], DK, xT_ready, 0)
                        pe.wait_ge(xT_ready, 4)
                        for c, (o, n) in enumerate(PROJ_CH):
                            weights_in(pe, c)
                            for t in range(TT):
                                b = banks.take(proj_ready, c * TT + t + 1)
                                matmul_rows(pe, b, (0, n), lambda k: XT[:, k, t * P:(t + 1) * P],
                                            lambda k: wslot(c % WS, DK, n)[:, k, :], DK).then_inc(
                                    groups_done, groups.mark("proj", c, t))
                                groups.at["proj", c, t, "bank"] = b
                        for j in range(6):
                            c = NPC + j // 4
                            if j % 4 == 0:
                                weights_in(pe, c)
                            n = IN_CH[c][1]
                            b = banks.take(conv_in_ready, j + 1)
                            matmul_rows(pe, b, (0, S), lambda k: wslot(c % WS, DK, n)[:, k, (j % 4) * P:(j % 4 + 1) * P],
                                        lambda k: XT[:, k, :], DK).then_inc(groups_done, groups.mark("u", j))
                            groups.at["u", j, "bank"] = b
                        pe.wait_ge(proj_ready, TT * NPC)
                        transposes(pe, banks, groups, "mqk", lambda t, k: PROJ[:, t, MQ + k * P:MQ + (k + 1) * P], 6, qkT_ready, 0)
                        pe.wait_ge(rot_ready, 1)
                        transposes(pe, banks, groups, "rqk", lambda t, k: QROT[:, t, k * P:(k + 1) * P], 6, qkT_ready, 3)
                        pe.wait_ge(qkT_ready, 6)
                        for h in range(RET_H + 1):
                            if h < RET_H:
                                q0, pair = HD * (h % 2), h // 2
                                b = banks.take(ret_ready, h + 1)
                                nc.tensor.matmul(PS[:, b, 0:S], RT[q0:q0 + HD, 3 + pair, 0:P], RT[q0:q0 + HD, pair, :], start=True, stop=True)
                                nc.tensor.matmul(PS[:, b, S:3 * P], RT[q0:q0 + HD, 3 + pair, P:S], RT[q0:q0 + HD, pair, P:S], start=True, stop=True
                                                 ).then_inc(groups_done, groups.mark("rs", h))
                                groups.at["rs", h, "bank"] = b
                            if h >= 1:
                                g = h - 1
                                pe.wait_ge(ret_ready, g + 1)
                                w = PT[:, g % 2, :]
                                cols = slice(g * HD, (g + 1) * HD)
                                v = [PROJ[:, t, RV + g * HD:RV + (g + 1) * HD] for t in range(TT)]
                                nc.tensor.matmul(PS[:, 4, cols], w[:, 0:P], v[0], start=True, stop=True)
                                nc.tensor.matmul(PS[:, 5, cols], w[:, P:S], v[0], start=True, stop=False)
                                nc.tensor.matmul(PS[:, 5, cols], w[:, S:3 * P], v[1], start=False, stop=True
                                                 ).then_inc(groups_done, groups.mark("rpv", g))
                        for i in range(MOBA_H + 2):
                            if i < MOBA_H:
                                q0, pair = HD * (i % 2), i // 2
                                b = banks.take(act_in_ready, i + 1)
                                nc.tensor.matmul(PS[:, b, 0:P], MT(pair)[q0:q0 + HD, 0:P], MT(3 + pair)[q0:q0 + HD, 0:P], start=True, stop=True)
                                nc.tensor.matmul(PS[:, b, P:3 * P], MT(pair)[q0:q0 + HD, P:S], MT(3 + pair)[q0:q0 + HD, :], start=True, stop=True
                                                 ).then_inc(groups_done, groups.mark("ms", i))
                                groups.at["ms", i, "bank"] = b
                            if 1 <= i <= MOBA_H:
                                j = i - 1
                                pe.wait_ge(probs_ready, j + 1)
                                b = banks.take(probsT_ready, j + 1)
                                for kb in range(3):
                                    ins = nc.tensor.transpose(PS[:, b, kb * P:(kb + 1) * P], PR[:, j % 2, kb * P:(kb + 1) * P], ident)
                                ins.then_inc(groups_done, groups.mark("pT", j))
                                groups.at["pT", j, "bank"] = b
                            if i >= 2:
                                j = i - 2
                                pe.wait_ge(probsT_ready, j + 1)
                                w = PT[:, j % 2, :]
                                cols = slice(j * HD, (j + 1) * HD)
                                v = [PROJ[:, t, MV + j * HD:MV + (j + 1) * HD] for t in range(TT)]
                                nc.tensor.matmul(PS[:, 6, cols], w[:, 0:P], v[0], start=True, stop=True)
                                nc.tensor.matmul(PS[:, 7, cols], w[:, P:S], v[0], start=True, stop=False)
                                nc.tensor.matmul(PS[:, 7, cols], w[:, S:3 * P], v[1], start=False, stop=True
                                                 ).then_inc(groups_done, groups.mark("pv", j))
                        pe.wait_ge(merged_ready, 1)
                        transposes(pe, banks, groups, "yT", lambda t, k: YR[:, t, k * P:(k + 1) * P], 3, catT_ready, 0)
                        pe.wait_ge(merged_ready, 2)
                        transposes(pe, banks, groups, "oT", lambda t, k: YM[:, t, k * P:(k + 1) * P], 3, catT_ready, 2)
                        pe.wait_ge(catT_ready, 4)
                        pe.wait_ge(conv_ready, 1)
                        for c in range(2):
                            weights_in(pe, 8 + c)
                            for t in range(TT):
                                b = banks.take(mix_read, c * TT + t + 1)
                                matmul_rows(pe, b, (0, 512), lambda k: CT[:, k, t * P:(t + 1) * P],
                                            lambda k: wslot(c, DK, 512)[:, k, :], DK).then_inc(
                                    groups_done, groups.mark("mix", c, t))
                                groups.at["mix", c, t, "bank"] = b
                        pe.wait_ge(h_ready, 1)
                        transposes(pe, banks, groups, "x1T", lambda t, k: X[:, t, k * P:(k + 1) * P], DK, xT_ready, 4)
                        for t in range(TT):
                            for n in range(2):
                                nc.tensor.matmul(PS[:, 4 + 2 * t + n, :], ALPHAI[:], X[:, t, n * 512:(n + 1) * 512], start=True,
                                                 stop=False, skip_group_check=True)
                        pe.wait_ge(xT_ready, 8)

                        def up(i, r, lap):
                            pe.wait_ge(up_loaded[r], 32 * (i // 2 + 1) + lap * 16)
                            if i >= 2:
                                pe.wait_ge(up_read, i - 1 + lap)
                                pe.wait_ge(hidden_ready, i - 1 + lap)
                            for half in range(2):
                                for j in range(2):
                                    for k in range(DK):
                                        c = half * 2 * P + j * P
                                        ins = nc.tensor.matmul(PS[:, 2 * r + half, j * S:(j + 1) * S], wslot(r, DK, 512)[:, k, c:c + P],
                                                               XT[:, k, :], start=(k == 0), stop=(k == DK - 1))
                                ins.then_inc(groups_done, groups.mark("up", i, half))

                        def down(i, r, lap, last=False):
                            pe.wait_ge(down_loaded[r], 16 * (i // 2 + 1) + lap * 8)
                            pe.wait_ge(hidden_ready, i + 1 + lap)
                            for j in range(2):
                                for t in range(TT):
                                    for n in range(2):
                                        ins = nc.tensor.matmul(PS[:, 4 + 2 * t + n, :], HG[r][:, j, t * P:(t + 1) * P],
                                                               wslot(2 + r, 2, D)[:, j, n * 512:(n + 1) * 512], start=False,
                                                               stop=last and j == 1, skip_group_check=True)
                            ins.then_inc(groups_done, groups.mark("down", i))

                        up(0, 0, 0)
                        up(1, 1, 0)
                        down(0, 0, 0)
                        at_loop = groups.n
                        with pe.Fori(0, (PAIRS - 3) // 2) as it:
                            for i in (2, 3):
                                up(i, i % 2, it * 2)
                                down(i - 1, (i - 1) % 2, it * 2)
                        taken["per"] = groups.n - at_loop
                        groups.n += taken["per"] * ((PAIRS - 3) // 2 - 1)
                        up(PAIRS - 1, 0, 0)
                        down(PAIRS - 2, 1, 0)
                        down(PAIRS - 1, 0, 0, last=True)

                    @block.sync
                    def _(sp):
                        sp.dma_start(RAW[0:3 * FT, :], A["ffn_conv_w"].rearrange("l k (f p) -> l (k f) p", p=P)[l]).then_inc(inputs_loaded, 16)
                        sp.dma_start(RAW[3 * FT:3 * FT + 6, :], A["conv_w"].rearrange("l k (f p) -> l (k f) p", p=P)[l]).then_inc(inputs_loaded, 16)

                        def load(c):
                            name, o, n = ("w_in", *IN_CH[c]) if c < 8 else ("w_out", (c - 8) * 512, 512)
                            sp.dma_start(wslot(c % WS, DK, n), wview(name, l)[:, :, o:o + n]).then_inc(weights_loaded[c % WS], 16)

                        last = [("proj", c, 1) for c in range(NPC)]
                        for c in range(4):
                            load(c)
                        sp.dma_start(DEC[:].rearrange("p h n -> p (h n)"), A["decay"]).then_inc(consts_loaded, 16)
                        sp.dma_start(BIAS[:].rearrange("p h n -> p (h n)"), bias_dram).then_inc(consts_loaded, 16)
                        for c in range(4, 10):
                            sp.wait_ge(groups_done, groups.of(*last[c - 4]))
                            load(c)

                        up_v = A["w_up"].rearrange("l (k p) (h f n) -> l f h p k n", p=P, h=2, n=2 * P)[l]
                        down_v = A["w_down"].rearrange("l (f j p) n -> l f p j n", p=P, j=2)[l]

                        def load_up(i, r):
                            for half in range(2):
                                sp.dma_start(wslot(r, DK, 512)[:, :, half * 2 * P:(half + 1) * 2 * P], up_v[i, half]
                                             ).then_inc(up_loaded[r], 16)

                        def load_down(i, r):
                            sp.dma_start(wslot(2 + r, 2, D), down_v[i]).then_inc(down_loaded[r], 16)

                        sp.wait_ge(groups_done, groups.of("u", 3))
                        load_down(0, 0)
                        sp.wait_ge(groups_done, groups.of("u", 5))
                        load_down(1, 1)
                        sp.wait_ge(groups_done, groups.of("ms", MOBA_H - 1))
                        for i, name in enumerate(("ln1_g", "ln1_b")):
                            sp.dma_start(PROJ[:, i, 0:D], A[name].rearrange("(o l) n -> l o n", o=1)[l].to_broadcast([P, D])
                                         ).then_inc(late_rows_loaded, 16)
                        sp.wait_ge(groups_done, groups.of("mix", 0, 1))
                        load_up(0, 0)
                        sp.wait_ge(groups_done, groups.of("mix", 1, 1))
                        load_up(1, 1)
                        for i, name in enumerate(("ln2_g", "ln2_b")):
                            sp.dma_start(PROJ[:, i, D:2 * D], A[name].rearrange("(o l) n -> l o n", o=1)[l].to_broadcast([P, D])
                                         ).then_inc(rows_loaded, 16)
                        per = taken["per"]
                        sp.wait_ge(groups_done, groups.of("up", 0, 1))
                        load_up(2, 0)
                        sp.wait_ge(groups_done, groups.of("down", 0))
                        load_down(2, 0)
                        with sp.Fori(0, (PAIRS - 3) // 2) as it:
                            sp.wait_ge(groups_done, it * per + groups.of("up", 1, 1))
                            load_up(it * 2 + 3, 1)
                            sp.wait_ge(groups_done, it * per + groups.of("down", 1))
                            load_down(it * 2 + 3, 1)
                            sp.wait_ge(groups_done, it * per + groups.of("up", 2, 1))
                            load_up(it * 2 + 4, 0)
                            sp.wait_ge(groups_done, it * per + groups.of("down", 2))
                            load_down(it * 2 + 4, 0)

                    @block.scalar
                    def _(act):
                        def bank(*name):
                            act.wait_ge(groups_done, groups.of(*name))
                            return groups.at[name + ("bank",)]

                        for j in range(DK // 2):
                            b = bank("xT", j)
                            nc.scalar.copy(XT[:, 2 * j:2 * j + 2, :].rearrange("p k s -> p (k s)"), PS[:, b, :]).then_inc(xT_ready, 1)
                        for c, (o, n) in enumerate(PROJ_CH):
                            for t in range(TT):
                                b = bank("proj", c, t)
                                nc.scalar.copy(PROJ[:, t, o:o + n], PS[:, b, 0:n]).then_inc(proj_ready, 1)
                        for j in range(6):
                            b = bank("u", j)
                            nc.scalar.copy(CONV[:, j, :], PS[:, b, 0:S]).then_inc(conv_in_ready, 1)
                        act.wait_ge(proj_ready, TT * NPC)
                        nc.scalar.activation(PROJ[:, :, RG:RG + RW], PROJ[:, :, RG:RG + RW], ACT.Silu).then_inc(silu_ready, 1)
                        act.wait_ge(rot_ready, 1)
                        for j in range(3):
                            b = bank("mqk", j)
                            nc.scalar.copy(MT(2 * j), PS[:, b, 0:S])
                            nc.scalar.copy(MT(2 * j + 1), PS[:, b, S:2 * S]).then_inc(qkT_ready, 1)
                        for j in range(3):
                            b = bank("rqk", j)
                            nc.scalar.copy(RT[:, 2 * j:2 * j + 2, :].rearrange("p k s -> p (k s)"), PS[:, b, :]).then_inc(qkT_ready, 1)
                        root(act, TT * RET_H, 0, 1.0 / HD, 0)
                        for i in range(MOBA_H):
                            act.wait_ge(max_ready, i + 1)
                            nc.scalar.activation(PR[:, i % 2, 0:P], PR[:, i % 2, 0:P], ACT.Exp, bias=NM[:, 2 * i:2 * i + 1],
                                                 accum_out=SUM[:, 0, i:i + 1])
                            nc.scalar.activation(PR[:, i % 2, P:3 * P], PR[:, i % 2, P:3 * P], ACT.Exp, bias=NM[:, 2 * i + 1:2 * i + 2],
                                                 accum_out=SUM[:, 0, MOBA_H + i:MOBA_H + i + 1]).then_inc(probs_ready, 1)
                        for name, k0 in (("yT", 0), ("oT", 3)):
                            for j in range(2):
                                b = bank(name, j)
                                n = 2 - j
                                nc.scalar.copy(CT[:, k0 + 2 * j:k0 + 2 * j + n, :].rearrange("p k s -> p (k s)"), PS[:, b, 0:n * S]).then_inc(catT_ready, 1)
                        act.wait_ge(dots_ready, 1)
                        nc.scalar.activation(DOT[:, 0, :], DOT[:, 0, :], ACT.Gelu).then_inc(gelu_ready, 1)
                        root(act, TT, 1, 1.0, 0)
                        for j in range(DK // 2):
                            b = bank("x1T", j)
                            nc.scalar.copy(XT[:, 2 * j:2 * j + 2, :].rearrange("p k s -> p (k s)"), PS[:, b, :]).then_inc(xT_ready, 1)
                        per = taken["per"]

                        def hidden(i, r, lap, glap):
                            act.wait_ge(groups_done, groups.of("up", i, 0) + glap)
                            if i >= 2:
                                act.wait_ge(conv_done, i + lap)
                            nc.scalar.copy(APAD[:, r, :, 2:2 + S], PS[:, 2 * r, :].rearrange("p (j s) -> p j s", j=2)).then_inc(up_read, 1)
                            act.wait_ge(conv_done, i + 2 + lap)
                            nc.scalar.activation(HC[:, r], HC[:, r], ACT.Gelu).then_inc(gelu_done, 1)

                        act.wait_ge(conv_done, 1)
                        hidden(0, 0, 0, 0)
                        hidden(1, 1, 0, 0)
                        with act.Fori(0, (PAIRS - 3) // 2) as it:
                            hidden(2, 0, it * 2, it * per)
                            hidden(3, 1, it * 2, it * per)
                        hidden(PAIRS - 1, 0, 0, 0)
                        root(act, TT, 2, 1.0, 0)

                    @block.vector
                    def _(dve):
                        link = dve_chain(dve)
                        dve.sem_inc(rows_used, RING)
                        link(nc.vector.tensor_copy(PROD[:], H[:].rearrange("p t d -> p (t d)")[:, bass.ts(l, D)]))
                        link(nc.vector.tensor_copy(COEF[:, 1, :], WGT[:].rearrange("p t d -> p (t d)")[:, bass.ts(l, PICKS)]))
                        nc.vector.tensor_scalar(ALPHAI[:], ident, ALPHA, None, ALU.mult)
                        link(nc.vector.memset(GP[:, :, 0:2], 0.0))
                        dve.wait_ge(groups_done, groups.of("cols"))
                        nc.vector.tensor_copy(COLS[:], PS[:, 0, 0:3 * FT + 6]).then_inc(cols_ready, 1)
                        before = l * 2 * V_ROUNDS
                        EARLY = 12
                        with dve.Fori(0, EARLY) as e:
                            link.count.enter(e, 1)
                            dot_steps(dve, PROD[:], DOT[:, 0, bass.ts(e, RING)], e, before, link)
                        link.count.leave(EARLY)

                        def dots(e):
                            dot_steps(dve, PROD[:], DOT[:, 0, e * RING:(e + 1) * RING], e, before, link)

                        dve.wait_ge(proj_ready, TT * NPC)
                        cos, sin = (angles(c).to_broadcast([P, TT, 12, 32]) for c in (C_COS1, C_SIN1))
                        qk = PROJ[:, :, 0:2 * RW].rearrange("p t (h d) -> p t h d", h=12)
                        qr = QROT.rearrange("p t (h d) -> p t h d", h=12)
                        for half, (f1, f2, op) in enumerate(((cos, sin, ALU.subtract), (sin, cos, ALU.add))):
                            nc.vector.tensor_tensor(T1, qk[:, :, :, 0:32], f1, ALU.mult)
                            link(nc.vector.tensor_tensor(T2, qk[:, :, :, 32:64], f2, ALU.mult))
                            ins = nc.vector.tensor_tensor(qr[:, :, :, half * 32:half * 32 + 32], T1, T2, op)
                            if half == 0:
                                link(ins)
                        ins.then_inc(rot_ready, 1)
                        dve.wait_ge(conv_in_ready, 6)
                        dve.wait_ge(rot_ready, 1)
                        link(nc.vector.tensor_tensor(GP[:, :, 2:2 + S], CONV[:, 2:4, :], CONV[:, 4:6, :], ALU.mult))
                        for k in range(3):
                            for j in range(2):
                                tap = COLS[:, 3 * FT + 2 * k + j:3 * FT + 2 * k + j + 1]
                                if k == 0:
                                    ins = nc.vector.tensor_scalar(CT[:, 6 + j, :], GP[:, j, 0:S], tap, None, ALU.mult)
                                else:
                                    ins = nc.vector.scalar_tensor_tensor(CT[:, 6 + j, :], GP[:, j, k:k + S], tap, CT[:, 6 + j, :], ALU.mult, ALU.add)
                            link(ins)
                        nc.vector.tensor_tensor(CT[:, 6:8, :], CT[:, 6:8, :], CONV[:, 0:2, :], ALU.mult).then_inc(conv_ready, 1)
                        dve.wait_ge(consts_loaded, 32)
                        for h in range(RET_H):
                            dve.wait_ge(groups_done, groups.of("rs", h))
                            if h >= 2:
                                dve.wait_ge(groups_done, groups.of("rpv", h - 2))
                            nc.vector.tensor_tensor(PT[:, h % 2, :], PS[:, groups.at["rs", h, "bank"], 0:3 * P], DEC[:, h, :], ALU.mult
                                                    ).then_inc(ret_ready, 1)
                        dve.wait_ge(groups_done, groups.of("rpv", RET_H - 1))

                        def heads(ap):
                            return ap.rearrange("p t (h d) -> p (t h) d", h=RET_H)

                        def spread(ap):
                            return ap.rearrange("p (t h o) -> p t h o", t=TT, o=1).to_broadcast([P, TT, RET_H, HD])

                        raw = PS[:, 4:6, 0:RW].rearrange("p t (h d) -> p t h d", h=RET_H)
                        yr = YR.rearrange("p t (h d) -> p t h d", h=RET_H)
                        link(nc.vector.tensor_reduce(NM[:, 0:12].rearrange("p (t h) -> p t h", t=TT), raw, AX, ALU.add))
                        link(nc.vector.tensor_scalar(NM[:, 0:12], NM[:, 0:12], 1.0 / HD, None, ALU.mult))
                        link(nc.vector.tensor_tensor(yr, raw, spread(NM[:, 0:12]), ALU.subtract))
                        link(nc.vector.tensor_tensor(SQ, YR, YR, ALU.mult))
                        nc.vector.tensor_reduce(st[:, 0, 0:12].rearrange("p (t h) -> p t h", t=TT),
                                                SQ.rearrange("p t (h d) -> p t h d", h=RET_H), AX, ALU.add).then_inc(stat_ready, 1)

                        def scores(i):
                            dve.wait_ge(groups_done, groups.of("ms", i))
                            if i >= 2:
                                dve.wait_ge(groups_done, groups.of("pT", i - 2))
                            ins = nc.vector.scalar_tensor_tensor(PR[:, i % 2, :], PS[:, groups.at["ms", i, "bank"], 0:3 * P], HD ** -0.5,
                                                                 BIAS[:, i, :], ALU.mult, ALU.add)
                            ins.then_inc(act_in_ready, 1)
                            dve.wait_ge(act_in_ready, i + 1)
                            nc.vector.tensor_reduce(NM[:, 2 * i:2 * i + 1], PR[:, i % 2, 0:P], AX, ALU.max, negate=True)
                            nc.vector.tensor_reduce(NM[:, 2 * i + 1:2 * i + 2], PR[:, i % 2, P:3 * P], AX, ALU.max, negate=True
                                                    ).then_inc(max_ready, 1)

                        scores(0)
                        dve.wait_ge(root_ready, 1)
                        link(nc.vector.reciprocal(ri[:, 0, 0:12], rt[:, 0, 0:12]))
                        link(nc.vector.tensor_tensor(yr, yr, spread(ri[:, 0, 0:12]), ALU.mult))
                        dve.wait_ge(silu_ready, 1)
                        nc.vector.tensor_tensor(YR, YR, PROJ[:, :, RG:RG + RW], ALU.mult).then_inc(merged_ready, 1)
                        for i in range(MOBA_H):
                            if i + 1 < MOBA_H:
                                scores(i + 1)
                            dve.wait_ge(groups_done, groups.of("pT", i))
                            if i >= 2:
                                dve.wait_ge(groups_done, groups.of("pv", i - 2))
                            nc.vector.tensor_copy(PT[:, i % 2, :], PS[:, groups.at["pT", i, "bank"], 0:3 * P]).then_inc(probsT_ready, 1)
                        link(nc.vector.reciprocal(SUM[:, 1, :], SUM[:, 0, :]))
                        dve.wait_ge(groups_done, groups.of("pv", MOBA_H - 1))
                        nc.vector.tensor_tensor(YM.rearrange("p t (h d) -> p t h d", h=MOBA_H),
                                                PS[:, 6:8, 0:MW].rearrange("p t (h d) -> p t h d", h=MOBA_H),
                                                spread(SUM[:, 1, :]), ALU.mult).then_inc(merged_ready, 1)
                        for e in range(EARLY, V_ROUNDS):
                            dots(e)
                        dve.sem_inc(dots_ready, 1)
                        for c in range(2):
                            for t in range(TT):
                                dve.wait_ge(groups_done, groups.of("mix", c, t))
                                cols = slice(c * 512, (c + 1) * 512)
                                nc.vector.scalar_tensor_tensor(X[:, t, cols], X[:, t, cols], ALPHA, PS[:, groups.at["mix", c, t, "bank"], :],
                                                               ALU.mult, ALU.add).then_inc(mix_read, 1)
                        dve.wait_ge(mix_read, 4)

                        def norm(halves, i, rows):
                            for t in range(TT):
                                nc.vector.bn_stats(BN[:, t, 0:6], halves(t, 0))
                                link(nc.vector.bn_stats(BN[:, t, 6:12], halves(t, 1)))
                                link(nc.vector.bn_aggr(BN[:, t, 12:14], BN[:, t, 0:12]))
                            nc.vector.tensor_copy(st[:, i % 2, 0:TT], BN[:, :, 13]).then_inc(stat_ready, 1)
                            dve.wait_ge(root_ready, i + 1)
                            link(nc.vector.reciprocal(ri[:, i % 2, 0:TT], rt[:, i % 2, 0:TT]))
                            for t in range(TT):
                                for n in range(2):
                                    ins = nc.vector.tensor_scalar(X[:, t, n * 512:(n + 1) * 512], halves(t, n), BN[:, t, 12:13],
                                                                  ri[:, i % 2, t:t + 1], ALU.subtract, ALU.mult)
                            link(ins)
                            link(nc.vector.tensor_tensor(X[:], X[:], PROJ[:, 0:1, rows:rows + D].to_broadcast([P, TT, D]), ALU.mult))
                            nc.vector.tensor_tensor(X[:], X[:], PROJ[:, 1:2, rows:rows + D].to_broadcast([P, TT, D]), ALU.add).then_inc(h_ready, 1)

                        dve.wait_ge(late_rows_loaded, 32)
                        norm(lambda t, n: X[:, t, n * 512:(n + 1) * 512], 1, 0)
                        dve.wait_ge(gelu_ready, 1)
                        link(nc.vector.tensor_tensor(COEF[:, 0, :], DOT[:, 0, :], COEF[:, 1, :], ALU.mult))
                        link(nc.vector.memset(PROD[:], 0.0))
                        dve.wait_ge(catT_ready, 4)
                        nc.vector.memset(APAD[:, :, :, 0:2], 0.0).then_inc(conv_done, 1)
                        per = taken["per"]

                        def hidden(i, r, pair, lap, glap, rounds, n8):
                            dve.wait_ge(up_read, i + 1 + lap)
                            for k in range(3):
                                for j in range(2):
                                    c = k * FT + j
                                    tap = COLS[:, 2 * i + c:2 * i + c + 1] if pair is None else COLS[:, bass.ds(pair * 2 + c, 1)]
                                    if k == 0:
                                        ins = nc.vector.tensor_scalar(HC[:, r, j, :], APAD[:, r, j, 0:S], tap, None, ALU.mult)
                                    else:
                                        ins = nc.vector.scalar_tensor_tensor(HC[:, r, j, :], APAD[:, r, j, k:k + S], tap, HC[:, r, j, :], ALU.mult, ALU.add)
                                if k < 2:
                                    link(ins)
                            ins.then_inc(conv_done, 1)
                            for v in range(rounds):
                                m = n8 + v
                                sum_steps(dve, PROD[:], lambda k: COEF[:, 0, m * RING + k:m * RING + k + 1] if isinstance(m, int)
                                          else COEF[:, 0, bass.ds(m * RING + k, 1)], m + V_ROUNDS, before)
                            dve.wait_ge(gelu_done, i + 1 + lap)
                            dve.wait_ge(groups_done, groups.of("up", i, 1) + glap)
                            if i >= 2:
                                down_before = groups.of("down", 0) if i == 2 else groups.of("down", 1)
                                if i == PAIRS - 1:
                                    down_before = groups.of("down", 2) + per * ((PAIRS - 3) // 2 - 1)
                                dve.wait_ge(groups_done, down_before + glap)
                            nc.vector.tensor_tensor(HG[r], HC[:, r], PS[:, 2 * r + 1, :].rearrange("p (j s) -> p j s", j=2), ALU.mult
                                                    ).then_inc(hidden_ready, 1)

                        hidden(0, 0, None, 0, 0, 1, 0)
                        hidden(1, 1, None, 0, 0, 1, 1)
                        with dve.Fori(0, (PAIRS - 3) // 2) as it:
                            link.count.enter(it, 4)
                            hidden(2, 0, it * 2 + 2, it * 2, it * per, 2, it * 3 + 2)
                            hidden(3, 1, it * 2 + 3, it * 2, it * per, 1, it * 3 + 4)
                        link.count.leave((PAIRS - 3) // 2)
                        hidden(PAIRS - 1, 0, None, 0, 0, 2, 14)
                        dve.wait_ge(rows_used, RING + 2 * PICKS)
                        nc.vector.tensor_copy(ACC[:].rearrange("p t d -> p (t d)")[:, bass.ts(l, D)], PROD[:])
                        dve.wait_ge(groups_done, groups.of("down", PAIRS - 1))
                        dve.wait_ge(rows_loaded, 32)
                        norm(lambda t, n: PS[:, 4 + 2 * t + n, :], 2, D)

                    @block.gpsimd
                    def _(pool):
                        idx = IDX[:].rearrange("p t n -> p (t n)")
                        for i, table in enumerate(("peer_u_2", "peer_v_2")):
                            gather_rows(pool, table, lambda e8: idx[:, bass.ds(l * PICKS + e8 * RING, RING)], None, i * PICKS)
                phase_end()

        with ExitStack() as ph:
            CX = sbuf("CXK", [P, TT, D], at=ph)
            GATE = sbuf("GATEK", [P, D], at=ph)
            MODR = sbuf("MODRK", [16, P], at=ph)
            MODC = sbuf("MODCK", [P, 16], at=ph)
            GAIN = sbuf("GAINK", [P, 1, HD], at=ph)
            KV = sbuf("KV", [P, TT, 2 * KVW], at=ph)
            KD = sbuf("KD", [P, TT, KVH, 2, HD], at=ph)
            XN = CT[:].rearrange("p k s -> p (k s)").rearrange("p (t d) -> p t d", t=TT)
            with nc.Block() as block:
                groups = Groups()

                @block.tensor
                def _(pe):
                    banks = Banks(pe, list(range(8)))
                    pe.wait_ge(inputs_loaded, 16)
                    b = banks.take(cols_ready, 1)
                    nc.tensor.transpose(PS[:, b, 0:16], MODR[:], ident[0:16, 0:16]).then_inc(groups_done, groups.mark("cols"))
                    pe.wait_ge(norm_ready, TT)
                    transposes(pe, banks, groups, "xT", lambda t, k: XN[:, t, k * P:(k + 1) * P], DK, xT_ready, 0)
                    pe.wait_ge(xT_ready, 4)
                    weights_in(pe, 0)
                    for t in range(TT):
                        b = banks.take(proj_ready, t + 1)
                        matmul_rows(pe, b, (0, 2 * KVW), lambda k: XT[:, k, t * P:(t + 1) * P],
                                    lambda k: wslot(0, DK, 2 * KVW)[:, k, :], DK).then_inc(groups_done, groups.mark("proj", t))
                        groups.at["proj", t, "bank"] = b
                    pe.wait_ge(rot_ready, 1)
                    transposes(pe, banks, groups, "kT", lambda t, k: KD[:, t, k].rearrange("p c d -> p (c d)"), KVH, qkT_ready, 0)

                @block.sync
                def _(sp):
                    sp.dma_start(CX[:].rearrange("p t d -> p (t d)"), cx_dram).then_inc(rows_loaded, 16)
                    sp.dma_start(GATE[:], mod_dram[0, 1:2, 5 * D:6 * D].to_broadcast([P, D])).then_inc(rows_loaded, 16)
                    sp.dma_start(GAIN[:, 0, :], A["k_gain_2"][1:2, :].to_broadcast([P, HD])).then_inc(rows_loaded, 16)
                    sp.dma_start(MODR[:], mod_dram[1, 1:2, 0:2 * D].rearrange("o (k p) -> (o k) p", p=P)).then_inc(inputs_loaded, 16)
                    sp.dma_start(wslot(0, DK, 2 * KVW), wview("w_in_2", 1)[:, :, QW:QKV2]).then_inc(weights_loaded[0], 16)

                @block.scalar
                def _(act):
                    root(act, TT, 0, 1.0 / D, 1)
                    act.wait_ge(cols_ready, 1)
                    for j in range(DK // 2):
                        act.wait_ge(groups_done, groups.of("xT", j))
                        for k in range(2):
                            ins = nc.scalar.activation(XT[:, 2 * j + k, :], PS[:, groups.at["xT", j, "bank"], k * S:(k + 1) * S], ACT.Identity,
                                                       bias=MODC[:, 2 * j + k:2 * j + k + 1], scale=MODC[:, 8 + 2 * j + k:9 + 2 * j + k])
                        ins.then_inc(xT_ready, 1)
                    for t in range(TT):
                        act.wait_ge(groups_done, groups.of("proj", t))
                        nc.scalar.copy(KV[:, t, :], PS[:, groups.at["proj", t, "bank"], 0:2 * KVW]).then_inc(proj_ready, 1)
                    root(act, TT * KVH, 1, 1.0 / HD, 1)
                    act.wait_ge(groups_done, groups.of("kT", 0))
                    nc.scalar.copy(KTC[:, 1], PS[:, groups.at["kT", 0, "bank"], :].rearrange("p (k s) -> p k s", k=KVH)).then_inc(qkT_ready, 1)

                @block.vector
                def _(dve):
                    link = dve_chain(dve)
                    dve.wait_ge(rows_loaded, 16 * 3)
                    link(nc.vector.tensor_tensor(ACC[:], ACC[:], GATE[:].rearrange("p (o d) -> p o d", o=1).to_broadcast([P, TT, D]), ALU.mult))
                    link(nc.vector.tensor_tensor(CX[:], CX[:], ACC[:], ALU.add))
                    for t in range(TT):
                        ins = nc.vector.tensor_tensor_reduce(PROD[:], CX[:, t, :], CX[:, t, :], 1.0, 0.0, ALU.mult, ALU.add, st[:, 0, t:t + 1])
                        if t == 0:
                            link(ins)
                    ins.then_inc(stat_ready, 1)
                    dve.wait_ge(groups_done, groups.of("cols"))
                    nc.vector.tensor_copy(MODC[:, 0:8], PS[:, 0, 0:8])
                    nc.vector.tensor_scalar(MODC[:, 8:16], PS[:, 0, 8:16], 1.0, None, ALU.add).then_inc(cols_ready, 1)
                    dve.wait_ge(root_ready, 1)
                    link(nc.vector.reciprocal(ri[:, 0, 0:TT], rt[:, 0, 0:TT]))
                    for t in range(TT):
                        nc.vector.tensor_scalar(XN[:, t, :], CX[:, t, :], ri[:, 0, t:t + 1], None, ALU.mult).then_inc(norm_ready, 1)
                    dve.wait_ge(proj_ready, TT)
                    nc.vector.tensor_copy(VC[:, 1], KV[:, :, KVW:2 * KVW])
                    k4 = KV[:, :, 0:KVW].rearrange("p t (h d) -> p t h d", h=KVH)
                    sq = PROD[:, 0:TT * KVW].rearrange("p (t h d) -> p t h d", t=TT, h=KVH)
                    link(nc.vector.tensor_tensor(sq, k4, k4, ALU.mult))
                    nc.vector.tensor_reduce(st[:, 1, 0:4].rearrange("p (t h) -> p t h", t=TT), sq, AX, ALU.add).then_inc(stat_ready, 1)
                    dve.wait_ge(root_ready, 2)
                    link(nc.vector.reciprocal(ri[:, 1, 0:4], rt[:, 1, 0:4]))
                    link(nc.vector.tensor_tensor(k4, k4, ri[:, 1, 0:4].rearrange("p (t h o) -> p t h o", t=TT, o=1).to_broadcast([P, TT, KVH, HD]), ALU.mult))
                    for c in range(2):
                        ins = nc.vector.tensor_tensor(KD[:, :, :, c, :], k4, GAIN[:].rearrange("p (t o) d -> p t o d", t=1).to_broadcast([P, TT, KVH, HD]), ALU.mult)
                    ins.then_inc(rot_ready, 1)
            phase_end()

        with ExitStack() as ph:
            B = stream_buffers(ph, True)
            with nc.Fori(0, L) as l:
                with nc.Block() as block:
                    groups = Groups()

                    @block.tensor
                    def _(pe):
                        stream_pe(pe, groups, B, True)

                    @block.sync
                    def _(sp):
                        stream_sp(sp, groups, B, l, 0)

                    @block.scalar
                    def _(act):
                        stream_act(act, groups, B, l, True)
                        for t in range(TT):
                            act.wait_ge(dots_ready, t + 1)
                            nc.scalar.activation(DOT[:, t, :], DOT[:, t, :], ACT.Gelu).then_inc(gelu_ready, 1)

                    @block.vector
                    def _(dve):
                        link = dve_chain(dve)
                        stream_dve(dve, link, groups, B, X, l, True)
                        dve.sem_inc(rows_used, RING)
                        rounds = PICKS // RING
                        before = l * 2 * TT * rounds + L * 2 * rounds
                        for t in range(TT):
                            with dve.Fori(0, rounds) as e:
                                link.count.enter(e, 1)
                                dot_steps(dve, H[:, t, :], DOT[:, t, bass.ts(e, RING)], e + t * rounds, before, link)
                            link.count.leave(rounds)
                            dve.sem_inc(dots_ready, 1)
                        link(nc.vector.memset(ACC[:], 0.0))
                        for t in range(TT):
                            dve.wait_ge(gelu_ready, t + 1)
                            link(nc.vector.tensor_tensor(COEF[:, t, :], DOT[:, t, :], WGT[:, t, :], ALU.mult))
                            with dve.Fori(0, rounds) as e:
                                sum_steps(dve, ACC[:, t, :], lambda k: COEF[:, t, bass.ds(e * RING + k, 1)], e + (TT + t) * rounds, before)
                        dve.wait_ge(rows_used, RING + 2 * TT * PICKS)
                        dve.wait_ge(rows_loaded, 16 * 7)
                        link(nc.vector.tensor_tensor(ACC[:], ACC[:], G2ROW.rearrange("p (o d) -> p o d", o=1).to_broadcast([P, TT, D]), ALU.mult))
                        nc.vector.tensor_tensor(X[:], X[:], ACC[:], ALU.add)
                        link(nc.vector.tensor_scalar(BASE[:], BASE[:], float(N_EXP), None, ALU.add))

                    @block.gpsimd
                    def _(pool):
                        pool.wait_ge(picks_ready, TT)
                        for i, table in enumerate(("peer_u_2", "peer_v_2")):
                            for t in range(TT):
                                gather_rows(pool, table, lambda e8: IDX[:, t, bass.ds(e8 * RING, RING)], None, (i * TT + t) * PICKS)
                phase_end()

        with ExitStack() as ph:
            FG = sbuf("FG", [P, D], at=ph)
            with nc.Block() as block:

                @block.sync
                def _(sp):
                    sp.dma_start(FG[:], A["final_g_2"].rearrange("(o n) -> o n", o=1).to_broadcast([P, D])).then_inc(rows_loaded, 16)
                    for t in range(TT):
                        sp.wait_ge(norm_ready, t + 1)
                        sp.dma_start(out_dram[:, t, :], X[:, t, :]).then_inc(stored, 16)
                    sp.wait_ge(stored, 16 * TT)

                @block.scalar
                def _(act):
                    root(act, TT, 0, 1.0 / D, 1)

                @block.vector
                def _(dve):
                    link = dve_chain(dve)
                    for t in range(TT):
                        ins = nc.vector.tensor_tensor_reduce(H[:, t, :], X[:, t, :], X[:, t, :], 1.0, 0.0, ALU.mult, ALU.add, st[:, 0, t:t + 1])
                    ins.then_inc(stat_ready, 1)
                    dve.wait_ge(root_ready, 1)
                    link(nc.vector.reciprocal(ri[:, 0, 0:TT], rt[:, 0, 0:TT]))
                    dve.wait_ge(rows_loaded, 16)
                    for t in range(TT):
                        nc.vector.scalar_tensor_tensor(X[:, t, :], X[:, t, :], ri[:, 0, t:t + 1], FG[:], ALU.mult, ALU.mult
                                                       ).then_inc(norm_ready, 1)


def constants():
    c = np.zeros((P, C_END), np.float32)
    c[:, C_ID:C_ID + P] = np.eye(P)
    c[:, C_FLIP:C_FLIP + P] = np.eye(P)[::-1]
    c[:, C_IOTA:C_IOTA + TOPK] = np.arange(TOPK)
    pos = np.arange(S, dtype=np.float32)
    inv1 = np.float32(10000.0) ** (-np.arange(0, HD, 2, dtype=np.float32) / np.float32(HD))
    ang1 = pos[:, None] * inv1[None, :].astype(np.float32)
    n = HD // 4
    inv2 = np.float32(10000.0) ** (-np.arange(n, dtype=np.float32) / np.float32(n))
    row, col = np.arange(S) // 64, np.arange(S) % 64
    ang2 = np.concatenate([row[:, None].astype(np.float32) * inv2, col[:, None].astype(np.float32) * inv2], -1)
    for c0, table in ((C_COS1, np.cos(ang1.astype(np.float64))), (C_SIN1, np.sin(ang1.astype(np.float64))),
                      (C_COS2, np.cos(ang2.astype(np.float64))), (C_SIN2, np.sin(ang2.astype(np.float64)))):
        c[:, c0:c0 + TT * 32] = table.reshape(TT, P, 32).transpose(1, 0, 2).reshape(P, TT * 32)
    dist = S - 1 - np.arange(2 * S - 1)
    exact = REL_BUCKETS // 2
    nf = np.maximum(dist, 1).astype(np.float32)
    large = exact + (np.log(nf / np.float32(exact)) / np.float32(np.log(REL_MAX / exact))
                     * np.float32(REL_BUCKETS - exact)).astype(np.int32)
    bucket = np.where(dist < exact, np.maximum(dist, 0), np.minimum(large, REL_BUCKETS - 1))
    buckets = np.zeros((REL_BUCKETS + 1, 2 * S - 1), np.float32)
    ok = dist >= 0
    buckets[bucket[ok], np.nonzero(ok)[0]] = 1.0
    buckets[REL_BUCKETS, ~ok] = MASKED
    e, q = np.arange(P)[:, None], np.arange(S)[None, :]
    decay = np.zeros((P, RET_H, 3 * P), np.float32)
    for h in range(RET_H):
        log_g = np.log(np.float32(1.0) - np.float32(2.0) ** np.float32(-5.0 - h)).astype(np.float64)
        d = q - e
        full = np.where(d >= 0, np.exp(np.maximum(d, 0) * log_g), 0.0) * HD ** -0.5
        decay[:, h, 0:S] = full
        decay[:, h, S:] = full[:, 0:P]
    return {"consts": c, "buckets": buckets, "decay": decay.reshape(P, RET_H * 3 * P)}


_INS = ["x", "w_in", "conv_w", "w_out", "ln1_g", "ln1_b", "w_up", "ffn_conv_w", "w_down", "ln2_g", "ln2_b",
        "rel_bias", "c_2", "ctx_2", "c_ctx_2", "w_mod_2", "b_mod_2", "w_in_2", "q_gain_2", "k_gain_2",
        "conv_w_2", "conv_b_2", "ln_g_2", "ln_b_2", "beta_attn_2", "beta_conv_2", "w_o_2", "peer_wq_2",
        "peer_keys_2", "peer_u_2", "peer_v_2", "final_g_2"]


def kernel(**inputs):
    import concourse.bacc as bacc
    from concourse.bass_utils import run_bass_kernel_spmd

    nc = bacc.Bacc("TRN2", target_bir_lowering=False, num_devices=1)
    arrays, aps = {}, {}
    given = {n: np.ascontiguousarray(inputs[n]) for n in _INS}
    given.update(constants())
    for name, a in given.items():
        arrays[f"in_{name}"] = a
        aps[name] = nc.dram_tensor(f"in_{name}", a.shape, mybir.dt.from_np(a.dtype), kind="ExternalInput").ap()
    out = nc.dram_tensor("out", (1, S, D), F32, kind="ExternalOutput").ap()
    program(nc, aps, out)
    r = run_bass_kernel_spmd(nc, [arrays], core_ids=[0])
    return r.results[0]["out"]
```

```python
from contextlib import ExitStack

import concourse.bass as bass
import numpy as np
from concourse import mybir

F32 = mybir.dt.float32
I32 = mybir.dt.int32
U32 = mybir.dt.uint32
ALU = mybir.AluOpType
ACT = mybir.ActivationFunctionType
AX = mybir.AxisListType.X

P = 128
D = 1024
S = 256
TT = S // P
DK = D // P
L = 2
HD = 64

RET_H, MOBA_H = 6, 6
RW, MW, CW1 = 384, 384, 256
QKV1 = 4 * RW + 3 * MW
FF = 2816
FT = FF // P
ALPHA = (2.0 * L) ** 0.25
LN_EPS = 1e-5
REL_BUCKETS, REL_MAX = 32, 128
MASKED = -1.0e30

QH, KVH = 8, 2
QW, KVW = QH * HD, KVH * HD
CW2, TAPS2 = 512, 31
HALO = TAPS2 // 2
QKV2 = QW + 2 * KVW
RMS_EPS = 1e-6
EH, EK, TOPK = 8, 128, 16
PICKS = EH * TOPK
N_EXP = EK * EK
LOW = -3.0e38

RING = 8
RING2 = 16
WS = 4
WCOL = 4096

C_ID, C_FLIP, C_IOTA = 0, P, 2 * P
C_COS1, C_SIN1 = C_IOTA + 16, C_IOTA + 16 + TT * 32
C_COS2, C_SIN2 = C_SIN1 + TT * 32, C_SIN1 + 2 * TT * 32
C_END = C_SIN2 + TT * 32


class Groups:

    def __init__(self):
        self.n, self.at = 0, {}

    def mark(self, *name):
        self.n += 1
        self.at[name] = self.n
        return 1

    def of(self, *name):
        return self.at[name]


class Banks:

    def __init__(self, pe, banks):
        self.pe, self.banks, self.i, self.read_out = pe, banks, 0, {}

    def take(self, sem, value):
        b = self.banks[self.i % len(self.banks)]
        self.i += 1
        self.hold(b, sem, value)
        return b

    def hold(self, b, sem, value):
        if b in self.read_out:
            self.pe.wait_ge(*self.read_out[b])
        self.read_out[b] = (sem, value)


class Count:

    def __init__(self):
        self.n, self.reg, self.per = 0, 0, 0

    def next(self, step=1):
        self.n += step
        return self.value()

    def value(self):
        return self.n if self.per == 0 else self.n + self.reg * self.per

    def enter(self, reg, per):
        self.reg, self.per, self.start = reg, per, self.n

    def leave(self, rounds):
        assert self.n - self.start == self.per, (self.n - self.start, self.per)
        self.n = self.start + self.per * rounds
        self.per = 0


def program(nc, A, out):
    with ExitStack() as ctx:
        sems, named = [], {}

        def sem(name):
            sems.append(ctx.enter_context(nc.semaphore(name)))
            return sems[-1]

        def sbuf(name, shape, dt=F32, at=None):
            named[name] = named.get(name, 0) + 1
            name += f"_{named[name]}" if named[name] > 1 else ""
            return (at or ctx).enter_context(nc.sbuf_tensor(name, shape, dt))

        mod_stored = [sem(f"mod_stored{i}") for i in range(2)]
        row_landed = [sem(f"row_landed{i}") for i in range(RING)]
        row_landed2 = [sem(f"row_landed2_{i}") for i in range(RING2)]
        sems.clear()
        consts_loaded = sem("consts_loaded")
        inputs_loaded = sem("inputs_loaded")
        rows_loaded = sem("rows_loaded")
        late_rows_loaded = sem("late_rows_loaded")
        weights_loaded = [sem(f"weights_loaded{i}") for i in range(WS)]
        stored = sem("stored")
        groups_done = sem("groups_done")
        dve_step = sem("dve_step")
        act_step = sem("act_step")
        silu_ready = sem("silu_ready")
        mod_read = sem("mod_read")
        mod_bias_loaded = [sem(f"mod_bias_loaded{i}") for i in range(2)]
        stat_ready = sem("stat_ready")
        root_ready = sem("root_ready")
        norm_ready = sem("norm_ready")
        xT_ready = sem("xT_ready")
        cols_ready = sem("cols_ready")
        proj_ready = sem("proj_ready")
        conv_in_ready = sem("conv_in_ready")
        rot_ready = sem("rot_ready")
        qkT_ready = sem("qkT_ready")
        max_ready = sem("max_ready")
        probs_ready = sem("probs_ready")
        probsT_ready = sem("probsT_ready")
        ret_ready = sem("ret_ready")
        attn_ready = sem("attn_ready")
        conv_ready = sem("conv_ready")
        conv_read = sem("conv_read")
        act_in_ready = sem("act_in_ready")
        act_out_ready = sem("act_out_ready")
        merged_ready = sem("merged_ready")
        catT_ready = sem("catT_ready")
        mix_read = sem("mix_read")
        h_ready = sem("h_ready")
        picksT_ready = sem("picksT_ready")
        keysT_ready = sem("keysT_ready")
        score_read = sem("score_read")
        up_loaded = [sem(f"up_loaded{i}") for i in range(2)]
        down_loaded = [sem(f"down_loaded{i}") for i in range(2)]
        up_read = sem("up_read")
        conv_done = sem("conv_done")
        gelu_done = sem("gelu_done")
        hidden_ready = sem("hidden_ready")
        picks_ready = sem("picks_ready")
        idx_copied = sem("idx_copied")
        gather_issued = sem("gather_issued")
        rows_used = sem("rows_used")
        dots_ready = sem("dots_ready")
        gelu_ready = sem("gelu_ready")
        coef_ready = sem("coef_ready")

        def phase_end():
            nc.all_engine_barrier(sems_to_clear=range(sems[0].num, sems[-1].num + 1))

        mod_dram = nc.dram_tensor("mod_dram", (L, 2, 6 * D), F32, kind="Internal").ap()
        rel_dram = nc.dram_tensor("rel_dram", (MOBA_H, 2 * S - 1), F32, kind="Internal")
        bias_dram = nc.dram_tensor("bias_dram", (P, MOBA_H * 3 * P), F32, kind="Internal").ap()

        cx_dram = nc.dram_tensor("cx_dram", (P, TT * D), F32, kind="Internal").ap()

        C = sbuf("C", [P, C_END])
        ident = C[:, C_ID:C_ID + P]
        flip = C[:, C_FLIP:C_FLIP + P]
        iota16 = C[:, C_IOTA:C_IOTA + TOPK]

        def angles(c0):
            return C[:, c0:c0 + TT * 32].rearrange("p (t o d) -> p t o d", t=TT, o=1)

        eps = sbuf("eps", [P, 2])
        X = sbuf("X", [P, TT, D])
        W = sbuf("W", [P, WS, WCOL])
        XT = sbuf("XT", [P, DK, S])
        CT = sbuf("CT", [P, DK, S])
        ROWS = sbuf("ROWS", [P, RING, D])
        H = sbuf("H", [P, TT, D])
        ACC = sbuf("ACC", [P, TT, D])
        PROD = sbuf("PROD", [P, D])
        G2ROW = XT[:].rearrange("p k s -> p (k s)")[:, 0:D]
        IDX = sbuf("IDX", [P, TT, PICKS], I32)
        IDXS = sbuf("IDXS", [P, 2, RING2], I32)
        WGT = sbuf("WGT", [P, TT, PICKS])
        DOT = sbuf("DOT", [P, TT, PICKS])
        DOTS = sbuf("DOTS", [P, RING2])
        SC = sbuf("SC", [P, 16])
        ONE = sbuf("ONE", [1, 2])
        MODB = XT[:].rearrange("p k s -> p (k s)")[0:1, 0:1024].rearrange("p (i n) -> p i n", i=2)
        MODS = XT[:].rearrange("p k s -> p (k s)")[0:2, 1024:2048].rearrange("p (i n) -> p i n", i=2)
        COEF = sbuf("COEF", [P, TT, PICKS])
        BASE = sbuf("BASE", [P, 1])
        KTC = sbuf("KTC", [P, L, KVH, S])
        VC = sbuf("VC", [P, L, TT, KVW])
        st = sbuf("st", [P, 2, 16])
        rt = sbuf("rt", [P, 2, 16])
        ri = sbuf("ri", [P, 2, 16])
        PS = ctx.enter_context(nc.psum_tensor("PS", [P, 8, 512], F32))

        x_dram = A["x"].rearrange("o (t p) d -> p (o t) d", p=P)
        ctx_dram = A["ctx_2"].rearrange("o (t p) d -> p (o t) d", p=P)
        out_dram = out.rearrange("o (t p) d -> p (o t) d", p=P)
        tables = {n: A[n].rearrange("l n d -> (l n) d") for n in ("peer_u_2", "peer_v_2")}

        def wview(name, l):
            return A[name].rearrange("l (k p) n -> l p k n", p=P)[l]

        def wslot(s, k, n):
            return W[:, s, 0:k * n].rearrange("p (k n) -> p k n", k=k)

        def dve_chain(dve):
            count = Count()

            def link(ins):
                ins.then_inc(dve_step, 1)
                dve.wait_ge(dve_step, count.next())

            link.count = count
            return link


        def transposes(pe, banks, groups, name, src, n_k, sem_, base, width=P):
            for j in range(0, n_k, 2):
                b = banks.take(sem_, base + j // 2 + 1)
                for k in range(j, min(j + 2, n_k)):
                    for t in range(TT):
                        o = ((k - j) * TT + t) * P
                        ins = nc.tensor.transpose(PS[:, b, o:o + P], src(t, k), ident)
                ins.then_inc(groups_done, groups.mark(name, j // 2))
                groups.at[name, j // 2, "bank"] = b

        def matmul_rows(pe, b, cols, lhs, rhs, n_k, start=True, stop=True):
            for k in range(n_k):
                ins = nc.tensor.matmul(PS[:, b, cols[0]:cols[1]], lhs(k), rhs(k),
                                       start=start and k == 0, stop=stop and k == n_k - 1)
            return ins

        def weights_in(pe, chunk):
            pe.wait_ge(weights_loaded[chunk % WS], 16 * (chunk // WS + 1))

        BESIDE = (lambda k: ROWS[:, k, :], row_landed, RING)
        ALONE = (lambda k: W[:, k // 4, (k % 4) * D:(k % 4 + 1) * D], row_landed2, RING2)

        def gather_rows(pool, ring, table, src, n0):
            slot, landed, size = ring
            with pool.Fori(0, PICKS // (2 * size)) as e:
                for half in range(2):
                    pool.wait_ge(rows_used, e * 2 * size + n0 + half * size + 1)
                    nc.gpsimd.tensor_copy(IDXS[:, half, 0:size], src(e * 2 + half)).then_inc(idx_copied, 1)
                    for k in range(size):
                        pool.wait_ge(rows_used, e * 2 * size + n0 + half * size + k + 1)
                        pool.sem_inc(gather_issued, 1)
                        if k == 0:
                            pool.wait_ge(idx_copied, e * 2 + n0 // size + half + 1)
                            pool.sem_inc(gather_issued, 1)
                        nc.gpsimd.indirect_dma_start(
                            slot(k), None, tables[table], bass.IndirectOffsetOnAxis(IDXS[:, half, k:k + 1], 0),
                        ).then_inc(landed[k], 16)

        def dot_step(dve, ring, h, k, n, before):
            slot, landed, size = ring
            dve.wait_ge(landed[k], (n + before) * 16 + 16)
            nc.vector.tensor_tensor_reduce(slot(k), slot(k), h, 1.0, 0.0, ALU.mult, ALU.add,
                                           DOTS[:, k:k + 1]).then_inc(rows_used, 1)

        def dots_out(dve, ring, dots, n, link):
            size = ring[2]
            dve.wait_ge(rows_used, n * size + 2 * size)
            link(nc.vector.tensor_copy(dots, DOTS[:, 0:size]))

        def dot_round(dve, ring, h, dots, n, before, link):
            for k in range(ring[2]):
                dot_step(dve, ring, h, k, n, before)
            dots_out(dve, ring, dots, n, link)

        def sum_round(dve, ring, acc, coef, n, before):
            slot, landed, size = ring
            for k in range(size):
                dve.wait_ge(landed[k], (n + before) * 16 + 16)
                dve.wait_ge(rows_used, n * size + size + k)
                nc.vector.scalar_tensor_tensor(acc, slot(k), coef(k), acc, ALU.mult, ALU.add).then_inc(rows_used, 1)

        NPIECE = 6 * D // 512

        def mod_sp(sp, l, w0, slot_used, xt_used=None):
            for i in range(NPIECE):
                c = w0 + i
                if c >= WS:
                    sp.wait_ge(groups_done, slot_used(c))
                cols = slice(i * 512, (i + 1) * 512)
                sp.dma_start(wslot(c % WS, DK, 512), wview("w_mod_2", l)[:, :, cols]).then_inc(weights_loaded[c % WS], 16)
                if i == 0 and xt_used:
                    sp.wait_ge(groups_done, xt_used())
                if i >= 2:
                    sp.wait_ge(mod_read, i - 1)
                sp.dma_start(MODB[:, i % 2, :], A["b_mod_2"][l:l + 1, cols]).then_inc(mod_bias_loaded[i % 2], 16)

        def mod_pe(pe, banks, groups, w0):
            for i in range(NPIECE):
                c = w0 + i
                weights_in(pe, c)
                pe.wait_ge(mod_bias_loaded[i % 2], 16 * (i // 2 + 1))
                b = banks.take(mod_read, i + 1)
                for k in range(DK):
                    nc.tensor.matmul(PS[0:2, b, :], SC[:, k:k + 9:8], wslot(c % WS, DK, 512)[:, k, :],
                                     start=(k == 0), stop=False)
                nc.tensor.matmul(PS[0:2, b, :], ONE[:], MODB[:, i % 2, :], start=False, stop=True
                                 ).then_inc(groups_done, groups.mark("mod", i))
                groups.at["mod", i, "bank"] = b

        def mod_act(act, groups, stored_before):
            for i in range(NPIECE):
                act.wait_ge(groups_done, groups.of("mod", i))
                if i >= 2:
                    act.wait_ge(mod_stored[i % 2], 16 * (i // 2) + stored_before)
                nc.scalar.copy(MODS[:, i % 2, :], PS[0:2, groups.at["mod", i, "bank"], :]).then_inc(mod_read, 1)

        def mod_pool(pool, l, stored_before):
            for i in range(NPIECE):
                pool.wait_ge(mod_read, i + 1)
                pool.dma_start(mod_dram[l, :, i * 512:(i + 1) * 512], MODS[:, i % 2, :]).then_inc(mod_stored[i % 2], 16)
            for i in range(2):
                pool.wait_ge(mod_stored[i], 16 * (NPIECE // 2) + stored_before)

        with ExitStack() as ph:
            SCR = sbuf("SCR", [16, P], at=ph)
            SCS = sbuf("SCS", [16, P], at=ph)
            REL = sbuf("REL", [REL_BUCKETS + 1, MOBA_H], at=ph)
            BUCK = sbuf("BUCK", [REL_BUCKETS + 1, 2 * S - 1], at=ph)
            RELT = sbuf("RELT", [MOBA_H, 2 * S - 1], at=ph)
            HANK = sbuf("HANK", [P, MOBA_H, 3 * P], at=ph)
            BIAS = sbuf("BIASS", [P, MOBA_H, 3 * P], at=ph)
            with nc.Block() as block:
                groups = Groups()

                @block.tensor
                def _(pe):
                    banks = Banks(pe, list(range(8)))
                    pe.wait_ge(consts_loaded, 16)
                    pe.wait_ge(silu_ready, 1)
                    b = banks.take(cols_ready, 1)
                    nc.tensor.transpose(PS[:, b, 0:16], SCS[:], ident[0:16, 0:16]).then_inc(
                        groups_done, groups.mark("sc"))
                    pe.wait_ge(inputs_loaded, 4 * 16)
                    pe.wait_ge(dve_step, 3)
                    b = banks.take(act_step, 1)
                    nc.tensor.matmul(PS[0:MOBA_H, b, 0:2 * S - 1], REL[:], BUCK[:], start=True,
                                     stop=True).then_inc(groups_done, groups.mark("rel"))
                    pe.wait_ge(cols_ready, 1)
                    mod_pe(pe, banks, groups, 0)
                    pe.wait_ge(late_rows_loaded, 12 * 16)
                    for h in range(MOBA_H):
                        b = banks.take(score_read, h + 1)
                        nc.tensor.matmul(PS[:, b, 0:3 * P], flip, HANK[:, h, :], start=True,
                                         stop=True).then_inc(groups_done, groups.mark("bias", h))
                        groups.at["bias", h, "bank"] = b

                @block.sync
                def _(sp):
                    sp.dma_start(SCR[0:8, :], A["c_2"].rearrange("o (k p) -> (o k) p", p=P)).then_inc(inputs_loaded, 16)
                    sp.dma_start(SCR[8:16, :], A["c_ctx_2"].rearrange("(k p) -> k p", p=P)).then_inc(inputs_loaded, 16)
                    sp.dma_start(C[:], A["consts"]).then_inc(consts_loaded, 16)
                    sp.dma_start(REL[0:REL_BUCKETS, :], A["rel_bias"]).then_inc(inputs_loaded, 16)
                    sp.dma_start(BUCK[:], A["buckets"]).then_inc(inputs_loaded, 16)
                    sp.dma_start(X[:], x_dram).then_inc(rows_loaded, 16)
                    mod_sp(sp, 0, 0, lambda c: groups.of("mod", c - WS))
                    sp.wait_ge(rows_loaded, 16)

                @block.scalar
                def _(act):
                    act.wait_ge(inputs_loaded, 4 * 16)
                    nc.scalar.activation(SCS[:], SCR[:], ACT.Silu).then_inc(silu_ready, 1)
                    act.wait_ge(groups_done, groups.of("rel"))
                    nc.scalar.copy(RELT[:], PS[0:MOBA_H, 1, 0:2 * S - 1]).then_inc(act_step, 1)
                    act.wait_ge(act_step, 1)
                    act.dma_start(rel_dram.ap(), RELT[:]).then_inc(stored, 16)
                    act.wait_ge(stored, 16)
                    for h in range(MOBA_H):
                        for first, n, o in ((P, P, 0), (0, 2 * P, P)):
                            src = bass.AP(rel_dram, h * (2 * S - 1) + first, [[1, P], [1, n]])
                            act.dma_start(HANK[:, h, o:o + n], src).then_inc(late_rows_loaded, 16)
                    mod_act(act, groups, 0)
                    for h in range(MOBA_H):
                        act.wait_ge(groups_done, groups.of("bias", h))
                        nc.scalar.copy(BIAS[:, h, :], PS[:, groups.at["bias", h, "bank"], 0:3 * P]).then_inc(score_read, 1)
                    act.wait_ge(score_read, MOBA_H)
                    act.dma_start(bias_dram, BIAS[:].rearrange("p h n -> p (h n)")).then_inc(stored, 16)
                    act.wait_ge(stored, 32)

                @block.vector
                def _(dve):
                    link = dve_chain(dve)
                    link(nc.vector.memset(ONE[:], 1.0))
                    link(nc.vector.memset(REL[REL_BUCKETS:REL_BUCKETS + 1, :], 1.0))
                    link(nc.vector.memset(eps[:, 0:1], LN_EPS))
                    nc.vector.memset(eps[:, 1:2], RMS_EPS)
                    nc.vector.memset(BASE[:], 0.0)
                    dve.wait_ge(groups_done, groups.of("sc"))
                    nc.vector.tensor_copy(SC[:], PS[:, 0, 0:16]).then_inc(cols_ready, 1)

                @block.gpsimd
                def _(pool):
                    mod_pool(pool, 0, 0)
            phase_end()


        def stream_buffers(ph, latent):
            B = {}
            B["PROJ"] = sbuf("PROJ2", [P, TT, QKV2], at=ph)
            B["QR"] = sbuf("QR", [P, TT, QW + 2 * KVW], at=ph)
            B["T1"] = PROD[:, 0:TT * 320].rearrange("p (t n) -> p t n", t=TT)
            B["T2"] = sbuf("T2", [P, TT, 10 * 32], at=ph)
            B["QT"] = sbuf("QT", [P, QH // 2, S], at=ph)
            B["KT"] = sbuf("KT", [P, KVH, 2 * S], at=ph)
            B["V"] = sbuf("V", [P, 2 * TT, KVW], at=ph)
            B["GAIN"] = sbuf("GAIN", [P, 2, HD], at=ph)
            B["COLR"] = sbuf("COLR", [TAPS2 + 3, CW2], at=ph)
            B["COLC"] = sbuf("COLC", [P, CW2 // P, TAPS2 + 3], at=ph)
            B["MODR"] = sbuf("MODR", [16, P], at=ph)
            B["MODC"] = sbuf("MODC", [P, 16], at=ph)
            B["LNR"] = sbuf("LNR", [P, 2, CW2], at=ph)
            B["ROW"] = [ACC[:, 0, :], ACC[:, 1, :], sbuf("ROW", [P, D], at=ph)[:]]
            AR = ROWS[:].rearrange("p k d -> p (k d)")
            B["U"] = AR[:, 0:2048].rearrange("p (j s) -> p j s", j=8)
            B["PAD"] = AR[:, 2048:2048 + 4 * (S + 2 * HALO)].rearrange("p (j s) -> p j s", j=4)
            B["PR"] = AR[:, 4096:5120].rearrange("p (i n) -> p i n", i=2)
            B["PT"] = AR[:, 5120:6144].rearrange("p (i n) -> p i n", i=2)
            B["O"] = AR[:, 6144:7168].rearrange("p (t n) -> p t n", t=TT)
            B["Y"] = AR[:, 7168:8192].rearrange("p (t n) -> p t n", t=TT)
            B["SC"] = [AR[:, 0:2048], AR[:, 2048:4096]]
            B["CAND"] = B["HOT"] = AR[:, 4096:6144]
            B["QPT"] = AR[:, 6144:8192].rearrange("p (t h s) -> p t h s", t=TT, h=EH)
            B["KPT"] = B["QR"][:].rearrange("p t n -> p (t n)")[:, 0:1024].rearrange("p (h k) -> p h k", h=EH)
            B["KEYS"] = B["PROJ"][:].rearrange("p t n -> p (t n)")[:, 0:1024]
            B["TV"] = sbuf("TV", [P, 2 * EH, TOPK], at=ph)
            B["TI"] = sbuf("TI", [P, 2 * EH, TOPK], U32, at=ph)
            B["TF"] = sbuf("TF", [P, 2 * EH, TOPK], at=ph)
            B["BV"] = sbuf("BV", [P, EH, TOPK], at=ph)
            B["BJ"] = sbuf("BJ", [P, EH, TOPK], U32, at=ph)
            B["J"] = sbuf("J", [P, 2, PICKS], U32, at=ph)
            B["JF"] = sbuf("JF", [P, 2, PICKS], at=ph)
            B["EI"] = sbuf("EI", [P, 3, PICKS], at=ph)
            B["SUM"] = sbuf("SUM", [P, 2, TT * QH], at=ph)
            B["NMAX"] = sbuf("NMAX", [P, TT * QH], at=ph)
            B["BN"] = sbuf("BN", [P, TT, 8], at=ph)
            return B

        CHUNKS2 = [("w_in_2", 0, 512), ("w_in_2", 512, 256), ("w_in_2", 768, 512), ("w_in_2", 1280, 512),
                   ("w_o_2", 0, 512), ("w_o_2", 512, 512), ("peer_wq_2", 0, 512), ("peer_wq_2", 512, 512)]

        def stream_pe(pe, groups, B, latent):
            banks = Banks(pe, [0, 1, 2, 3, 4, 5])
            nk = 2 * S if latent else S
            pe.wait_ge(rows_loaded, 16 * 6)
            b = banks.take(cols_ready, 1)
            for j in range(CW2 // P):
                nc.tensor.transpose(PS[:, b, j * 34:j * 34 + 34], B["COLR"][:, j * P:(j + 1) * P], ident[0:34, 0:34])
            nc.tensor.transpose(PS[:, b, 136:152], B["MODR"][:], ident[0:16, 0:16]).then_inc(
                groups_done, groups.mark("cols"))
            pe.wait_ge(norm_ready, TT)
            transposes(pe, banks, groups, "xT", lambda t, k: CT_tok(B)[:, t, k * P:(k + 1) * P], DK, xT_ready, 0)
            pe.wait_ge(xT_ready, 4)
            for c, (o, n) in enumerate(((0, 512), (512, 256))):
                weights_in(pe, c)
                for t in range(TT):
                    b = banks.take(proj_ready, c * TT + t + 1)
                    matmul_rows(pe, b, (0, n), lambda k: XT[:, k, t * P:(t + 1) * P],
                                lambda k: wslot(c, DK, n)[:, k, :], DK).then_inc(
                        groups_done, groups.mark("proj", c, t))
                    groups.at["proj", c, t, "bank"] = b
            for j in range(8):
                c = 2 + j // 4
                if j % 4 == 0:
                    weights_in(pe, c)
                b = banks.take(conv_in_ready, j + 1)
                matmul_rows(pe, b, (0, S), lambda k: wslot(c, DK, 512)[:, k, (j % 4) * P:(j % 4 + 1) * P],
                            lambda k: XT[:, k, :], DK).then_inc(groups_done, groups.mark("u", j))
                groups.at["u", j, "bank"] = b
            pe.wait_ge(rot_ready, 1)
            transposes(pe, banks, groups, "qk", lambda t, k: B["QR"][:, t, k * P:(k + 1) * P], 6, qkT_ready, 0)
            pe.wait_ge(qkT_ready, 3)
            n = TT * QH
            nb = nk // P
            for i in range(n + 2):
                if i < n:
                    t, h = divmod(i, QH)
                    q0 = HD * (h % 2)
                    b = banks.take(probs_ready, i + 1)
                    nc.tensor.matmul(PS[:, b, 0:nk], B["QT"][q0:q0 + HD, h // 2, t * P:(t + 1) * P],
                                     B["KT"][q0:q0 + HD, h // (QH // KVH), 0:nk], start=True, stop=True
                                     ).then_inc(groups_done, groups.mark("score", i))
                    groups.at["score", i, "bank"] = b
                if 1 <= i <= n:
                    j = i - 1
                    pe.wait_ge(probs_ready, j + 1)
                    b = banks.take(probsT_ready, j + 1)
                    for kb in range(nb):
                        ins = nc.tensor.transpose(PS[:, b, kb * P:(kb + 1) * P], B["PR"][:, j % 2, kb * P:(kb + 1) * P], ident)
                    ins.then_inc(groups_done, groups.mark("pT", j))
                    groups.at["pT", j, "bank"] = b
                if i >= 2:
                    j = i - 2
                    t, h = divmod(j, QH)
                    pe.wait_ge(probsT_ready, j + 1)
                    kv = h // (QH // KVH)
                    for kb in range(nb):
                        ins = nc.tensor.matmul(PS[:, 6 + t, h * HD:(h + 1) * HD], B["PT"][:, j % 2, kb * P:(kb + 1) * P],
                                               B["V"][:, kb, kv * HD:(kv + 1) * HD], start=(kb == 0), stop=(kb == nb - 1))
                    ins.then_inc(groups_done, groups.mark("pv", j))
            pe.wait_ge(conv_ready, 1)
            for t in range(TT):
                b = banks.take(conv_read, t + 1)
                for j in range(CW2 // P):
                    ins = nc.tensor.transpose(PS[:, b, j * P:(j + 1) * P], B["U"][:, j, t * P:(t + 1) * P], ident)
                ins.then_inc(groups_done, groups.mark("convT", t))
                groups.at["convT", t, "bank"] = b
            pe.wait_ge(merged_ready, 1)
            transposes(pe, banks, groups, "oT", lambda t, k: B["O"][:, t, k * P:(k + 1) * P], 4, catT_ready, 0)
            pe.wait_ge(merged_ready, 2)
            transposes(pe, banks, groups, "yT", lambda t, k: B["Y"][:, t, k * P:(k + 1) * P], 4, catT_ready, 2)
            pe.wait_ge(catT_ready, 4)
            pe.wait_ge(late_rows_loaded, 16 * 2)
            for g in range(2):
                b = banks.take(keysT_ready, g + 1)
                for h in range(4):
                    o = (g * 4 + h) * P
                    ins = nc.tensor.transpose(PS[:, b, h * P:(h + 1) * P], B["KEYS"][:, o:o + P], ident)
                ins.then_inc(groups_done, groups.mark("keys", g))
                groups.at["keys", g, "bank"] = b
            for t in range(TT):
                for c in range(2):
                    if t == 0:
                        weights_in(pe, 4 + c)
                    b = banks.take(mix_read, t * 2 + c + 1)
                    matmul_rows(pe, b, (0, 512), lambda k: CT[:, k, t * P:(t + 1) * P],
                                lambda k: wslot(c, DK, 512)[:, k, :], DK).then_inc(
                        groups_done, groups.mark("mix", c, t))
                    groups.at["mix", c, t, "bank"] = b
            for t in range(TT):
                pe.wait_ge(h_ready, t + 1)
                for j in range(2):
                    b = banks.take(xT_ready, 4 + t * 2 + j + 1)
                    for k in range(4):
                        o = (4 * j + k) * P
                        ins = nc.tensor.transpose(PS[:, b, k * P:(k + 1) * P], H[:, t, o:o + P], ident)
                    ins.then_inc(groups_done, groups.mark("hT", t, j))
                    groups.at["hT", t, j, "bank"] = b
                pe.wait_ge(xT_ready, 4 + t * 2 + 2)
                for j in range(2):
                    if t == 0:
                        weights_in(pe, 6 + j)
                    b = banks.take(picksT_ready, t * 2 + j + 1)
                    for h in range(4):
                        ins = matmul_rows(pe, b, (h * P, (h + 1) * P), lambda k: wslot(2 + j, DK, 512)[:, k, h * P:(h + 1) * P],
                                          lambda k: XT[:, k, t * P:(t + 1) * P], DK)
                    ins.then_inc(groups_done, groups.mark("pq", t, j))
                    groups.at["pq", t, j, "bank"] = b
                if t == 0:
                    pe.wait_ge(keysT_ready, 2)
                for g in range(4):
                    b = banks.take(score_read, t * 4 + g + 1)
                    for i in range(4):
                        h, c = (g // 2) * 4 + i, g % 2
                        if i == 0:
                            pe.wait_ge(picksT_ready, t * 2 + g // 2 + 1)
                        ins = nc.tensor.matmul(PS[:, b, i * P:(i + 1) * P], B["QPT"][c * HD:(c + 1) * HD, t, h, :],
                                               B["KPT"][c * HD:(c + 1) * HD, h, :], start=True, stop=True)
                    ins.then_inc(groups_done, groups.mark("ps", t, g))
                    groups.at["ps", t, g, "bank"] = b
            return banks

        def CT_tok(B):
            return CT[:].rearrange("p k s -> p (k s)").rearrange("p (t d) -> p t d", t=TT)

        def stream_sp(sp, groups, B, l, who):
            m = mod_dram[l][who:who + 1]
            sp.dma_start(B["MODR"][:], m[:, 0:2 * D].rearrange("o (k p) -> (o k) p", p=P)).then_inc(rows_loaded, 16)
            sp.dma_start(B["COLR"][0:TAPS2, :], A["conv_w_2"][l]).then_inc(rows_loaded, 16)
            for i, name in enumerate(("conv_b_2", "beta_attn_2", "beta_conv_2")):
                sp.dma_start(B["COLR"][TAPS2 + i:TAPS2 + i + 1, :], A[name].rearrange("(o l) n -> l o n", o=1)[l]
                             ).then_inc(rows_loaded, 16)
            sp.dma_start(B["GAIN"][:, 0, :], A["q_gain_2"].rearrange("(o l) n -> l o n", o=1)[l].to_broadcast([P, HD])
                         ).then_inc(rows_loaded, 16)
            for c in range(4):
                name, o, n = CHUNKS2[c]
                sp.dma_start(wslot(c, DK, n), wview(name, l)[:, :, o:o + n]).then_inc(weights_loaded[c], 16)
            sp.dma_start(B["GAIN"][:, 1, :], A["k_gain_2"].rearrange("(o l) n -> l o n", o=1)[l].to_broadcast([P, HD])
                         ).then_inc(inputs_loaded, 16)
            for i, name in enumerate(("ln_g_2", "ln_b_2")):
                sp.dma_start(B["LNR"][:, i, :], A[name].rearrange("(o l) n -> l o n", o=1)[l].to_broadcast([P, CW2])
                             ).then_inc(inputs_loaded, 16)
            for i in range(3):
                sp.dma_start(B["ROW"][i], m[:, (2 + i) * D:(3 + i) * D].to_broadcast([P, D])).then_inc(inputs_loaded, 16)
            for c in range(4, 8):
                name, o, n = CHUNKS2[c]
                last = {4: ("proj", 0, 1), 5: ("proj", 1, 1), 6: ("u", 3), 7: ("u", 7)}[c]
                sp.wait_ge(groups_done, groups.of(*last))
                sp.dma_start(wslot(c % WS, DK, n), wview(name, l)[:, :, o:o + n]).then_inc(weights_loaded[c % WS], 16)
            sp.wait_ge(rot_ready, 1)
            for c in range(2):
                sp.dma_start(B["KEYS"].rearrange("p (h c d) -> p h c d", h=EH, c=2)[:, :, c, :],
                             A["peer_keys_2"][l][:, c].rearrange("h k d -> k h d")).then_inc(late_rows_loaded, 16)

        def root(act, n, i, scale, e):
            act.wait_ge(stat_ready, i + 1)
            nc.scalar.activation(rt[:, i % 2, 0:n], st[:, i % 2, 0:n], ACT.Sqrt, bias=eps[:, e:e + 1],
                                 scale=scale).then_inc(root_ready, 1)

        def stream_act(act, groups, B, l, latent):
            nk = 2 * S if latent else S

            def bank(*name):
                act.wait_ge(groups_done, groups.of(*name))
                return groups.at[name + ("bank",)]

            root(act, TT, 0, 1.0 / D, 1)
            act.wait_ge(cols_ready, 1)
            for j in range(DK // 2):
                b = bank("xT", j)
                for k in range(2):
                    ins = nc.scalar.activation(XT[:, 2 * j + k, :], PS[:, b, k * S:(k + 1) * S], ACT.Identity,
                                               bias=B["MODC"][:, 2 * j + k:2 * j + k + 1],
                                               scale=B["MODC"][:, 8 + 2 * j + k:9 + 2 * j + k])
                ins.then_inc(xT_ready, 1)
            for c, (o, n) in enumerate(((0, 512), (512, 256))):
                for t in range(TT):
                    b = bank("proj", c, t)
                    nc.scalar.copy(B["PROJ"][:, t, o:o + n], PS[:, b, 0:n]).then_inc(proj_ready, 1)
            for j in range(8):
                b = bank("u", j)
                nc.scalar.activation(B["U"][:, j, :], PS[:, b, 0:S], ACT.Identity if j < 4 else ACT.Sigmoid
                                     ).then_inc(conv_in_ready, 1)
            root(act, TT * 10 // 2, 1, 1.0 / HD, 1)
            root(act, TT * 10 // 2, 2, 1.0 / HD, 1)
            for j in range(3):
                b = bank("qk", j)
                if j < 2:
                    nc.scalar.copy(B["QT"][:, 2 * j:2 * j + 2, :].rearrange("p k s -> p (k s)"), PS[:, b, :]
                                   ).then_inc(qkT_ready, 1)
                else:
                    nc.scalar.copy(B["KT"][:, :, nk - S:nk], PS[:, b, :].rearrange("p (k s) -> p k s", k=KVH)
                                   ).then_inc(qkT_ready, 1)
            for i in range(TT * QH):
                act.wait_ge(max_ready, i + 1)
                if i >= 2:
                    act.wait_ge(groups_done, groups.of("pT", i - 2))
                nc.scalar.activation(B["PR"][:, i % 2, 0:nk], PS[:, groups.at["score", i, "bank"], 0:nk], ACT.Exp,
                                     bias=B["NMAX"][:, i:i + 1], accum_out=B["SUM"][:, 0, i:i + 1]
                                     ).then_inc(probs_ready, 1)
            root(act, TT, 3, 1.0 / QW, 1)
            root(act, TT, 4, 1.0, 0)
            act.wait_ge(act_in_ready, 1)
            nc.scalar.activation(B["Y"], B["Y"], ACT.Silu).then_inc(act_out_ready, 1)
            for j in range(2):
                b = bank("oT", j)
                for k in range(2):
                    ins = nc.scalar.activation(CT[:, 2 * j + k, :], PS[:, b, k * S:(k + 1) * S], ACT.Copy,
                                               scale=B["COLC"][:, 2 * j + k, TAPS2 + 1:TAPS2 + 2])
                ins.then_inc(catT_ready, 1)
            root(act, TT, 5, 1.0 / CW2, 1)
            for j in range(2):
                b = bank("yT", j)
                for k in range(2):
                    ins = nc.scalar.activation(CT[:, 4 + 2 * j + k, :], PS[:, b, k * S:(k + 1) * S], ACT.Copy,
                                               scale=B["COLC"][:, 2 * j + k, TAPS2 + 2:TAPS2 + 3])
                ins.then_inc(catT_ready, 1)
            for g in range(2):
                b = bank("keys", g)
                nc.scalar.copy(B["KPT"][:, 4 * g:4 * g + 4, :].rearrange("p h k -> p (h k)"), PS[:, b, :]
                               ).then_inc(keysT_ready, 1)
            root(act, 1, 6, 1.0 / D, 1)
            for t in range(TT):
                for j in range(2):
                    b = bank("hT", t, j)
                    nc.scalar.copy(XT[:, 4 * j:4 * j + 4, t * P:(t + 1) * P], PS[:, b, :].rearrange("p (k s) -> p k s", k=4)
                                   ).then_inc(xT_ready, 1)
                if t == 0:
                    root(act, 1, 7, 1.0 / D, 1)
                for j in range(2):
                    b = bank("pq", t, j)
                    nc.scalar.copy(B["QPT"][:, t, 4 * j:4 * j + 4, :].rearrange("p h s -> p (h s)"), PS[:, b, :]
                                   ).then_inc(picksT_ready, 1)
                for g in range(4):
                    b = bank("ps", t, g)
                    dst = B["SC"][t].rearrange("p (h c k) -> p h c k", c=2, k=EK)[:, (g // 2) * 4:(g // 2) * 4 + 4, g % 2, :]
                    nc.scalar.copy(dst, PS[:, b, :].rearrange("p (h k) -> p h k", h=4)).then_inc(score_read, 1)

        def softmax_act(act, B, t):
            act.wait_ge(act_in_ready, 2 + t)
            nc.scalar.activation(B["EI"][:, 2, :], B["EI"][:, 2, :], ACT.Exp).then_inc(act_out_ready, 1)

        def stream_dve(dve, link, groups, B, SRC, l, latent):
            cur = {"stat": 0}

            def inverse_root(n, ins):
                i = cur["stat"]
                ins.then_inc(stat_ready, 1)
                cur["stat"] += 1
                dve.wait_ge(root_ready, i + 1)
                link(nc.vector.reciprocal(ri[:, i % 2, 0:n], rt[:, i % 2, 0:n]))
                return ri[:, i % 2]

            def sum_squares(src, width, n=TT):
                i = cur["stat"] % 2
                for t in range(n):
                    ins = nc.vector.tensor_tensor_reduce(PROD[:, 0:width], src(t), src(t), 1.0, 0.0, ALU.mult,
                                                         ALU.add, st[:, i, t:t + 1])
                    if t < n - 1:
                        link(ins)
                return ins

            r = inverse_root(TT, sum_squares(lambda t: SRC[:, t, :], D))
            for t in range(TT):
                nc.vector.tensor_scalar(CT_tok(B)[:, t, :], SRC[:, t, :], r[:, t:t + 1], None, ALU.mult).then_inc(norm_ready, 1)
            dve.wait_ge(groups_done, groups.of("cols"))
            nc.vector.tensor_copy(B["MODC"][:, 0:8], PS[:, 0, 136:144])
            nc.vector.tensor_scalar(B["MODC"][:, 8:16], PS[:, 0, 144:152], 1.0, None, ALU.add)
            nc.vector.tensor_copy(B["COLC"][:].rearrange("p j n -> p (j n)"), PS[:, 0, 0:136]).then_inc(cols_ready, 1)
            dve.wait_ge(inputs_loaded, 16 * 6)
            link(nc.vector.tensor_scalar(B["ROW"][2], B["ROW"][2], 1.0, None, ALU.add))
            link(nc.vector.tensor_scalar(B["GAIN"][:, 0, :], B["GAIN"][:, 0, :], HD ** -0.5, None, ALU.mult))
            nc.vector.memset(B["PAD"][:, :, 0:HALO], 0.0)
            link(nc.vector.memset(B["PAD"][:, :, HALO + S:S + 2 * HALO], 0.0))
            dve.wait_ge(proj_ready, 4)
            for t in range(TT):
                link(nc.vector.tensor_tensor(PROD[:, 0:640], B["PROJ"][:, t, 0:640], B["PROJ"][:, t, 0:640], ALU.mult))
                r = inverse_root(10, nc.vector.tensor_reduce(st[:, cur["stat"] % 2, 0:10],
                                                             PROD[:, 0:640].rearrange("p (h d) -> p h d", h=10), AX, ALU.add))
                q = B["PROJ"][:, t, 0:640].rearrange("p (h d) -> p h d", h=10)
                link(nc.vector.tensor_tensor(q, q, r[:, 0:10].rearrange("p (h o) -> p h o", o=1).to_broadcast([P, 10, HD]), ALU.mult))
                for i, (a, b) in enumerate(((0, 8), (8, 10))):
                    ins = nc.vector.tensor_tensor(q[:, a:b, :], q[:, a:b, :], B["GAIN"][:, i:i + 1, :].to_broadcast([P, b - a, HD]), ALU.mult)
                link(ins)
            kdst = B["QR"][:, :, QW:].rearrange("p t (h c d) -> p t h c d", h=KVH, c=2)
            if latent:
                cos, sin = angles(C_COS2), angles(C_SIN2)
                for a, b in ((0, 8), (8, 10)):
                    src = B["PROJ"][:, :, a * HD:b * HD].rearrange("p t (h d) -> p t h d", h=b - a)
                    q1, q2 = src[:, :, :, 0:32], src[:, :, :, 32:64]
                    n = b - a
                    t1 = B["T1"][:, :, 0:n * 32].rearrange("p t (h d) -> p t h d", h=n)
                    t2 = B["T2"][:, :, 0:n * 32].rearrange("p t (h d) -> p t h d", h=n)
                    cb, sb_ = cos.to_broadcast([P, TT, n, 32]), sin.to_broadcast([P, TT, n, 32])
                    for half, (f1, f2, op) in enumerate(((cb, sb_, ALU.subtract), (sb_, cb, ALU.add))):
                        nc.vector.tensor_tensor(t1, q1, f1, ALU.mult)
                        link(nc.vector.tensor_tensor(t2, q2, f2, ALU.mult))
                        if a == 0:
                            dst = [B["QR"][:, :, 0:QW].rearrange("p t (h d) -> p t h d", h=n)[:, :, :, half * 32:half * 32 + 32]]
                        else:
                            dst = [kdst[:, :, :, c, half * 32:half * 32 + 32] for c in range(2)]
                        for d in dst:
                            ins = nc.vector.tensor_tensor(d, t1, t2, op)
                        link(ins)
            else:
                nc.vector.tensor_copy(B["QR"][:, :, 0:QW], B["PROJ"][:, :, 0:QW])
                for c in range(2):
                    ins = nc.vector.tensor_copy(kdst[:, :, :, c, :], B["PROJ"][:, :, QW:QW + KVW].rearrange("p t (h d) -> p t h d", h=KVH))
                link(ins)
            v0 = TT if latent else 0
            link(nc.vector.tensor_copy(B["V"][:, v0:v0 + TT, :], B["PROJ"][:, :, QW + KVW:QKV2]))
            if latent:
                for h in range(KVH):
                    nc.vector.tensor_copy(B["KT"][:, h, 0:S], KTC[:].rearrange("p l h s -> p (l h) s")[:, bass.ds(l * KVH + h, 1), :].rearrange("p o s -> p (o s)"))
                link(nc.vector.tensor_copy(B["V"][:, 0:TT, :], VC[:].rearrange("p l t n -> p l (t n)")[:, bass.ds(l, 1), :].rearrange("p o n -> p (o n)").rearrange("p (t n) -> p t n", t=TT)))
            dve.sem_inc(rot_ready, 1)
            nk = 2 * S if latent else S
            dve.wait_ge(conv_in_ready, 8)
            link(nc.vector.tensor_tensor(B["PAD"][:, :, HALO:HALO + S], B["U"][:, 0:4, :], B["U"][:, 4:8, :], ALU.mult))
            n = TT * QH

            def tap_step(k):
                for j in range(4):
                    tap = B["COLC"][:, j, k:k + 1]
                    if k == 0:
                        ins = nc.vector.tensor_scalar(B["U"][:, j, :], B["PAD"][:, j, 0:S], tap, B["COLC"][:, j, TAPS2:TAPS2 + 1], ALU.mult, ALU.add)
                    else:
                        ins = nc.vector.scalar_tensor_tensor(B["U"][:, j, :], B["PAD"][:, j, k:k + S], tap, B["U"][:, j, :], ALU.mult, ALU.add)
                if k < TAPS2 - 1:
                    link(ins)
                else:
                    ins.then_inc(conv_ready, 1)

            for i in range(n + 1):
                if i < n:
                    dve.wait_ge(groups_done, groups.of("score", i))
                    nc.vector.tensor_reduce(B["NMAX"][:, i:i + 1], PS[:, groups.at["score", i, "bank"], 0:nk], AX, ALU.max,
                                            negate=True).then_inc(max_ready, 1)
                if i >= 1:
                    j = i - 1
                    dve.wait_ge(groups_done, groups.of("pT", j))
                    if j >= 2:
                        dve.wait_ge(groups_done, groups.of("pv", j - 2))
                    nc.vector.tensor_copy(B["PT"][:, j % 2, 0:nk], PS[:, groups.at["pT", j, "bank"], 0:nk]).then_inc(probsT_ready, 1)
                for k in range(2 * i, min(2 * i + 2, TAPS2)):
                    tap_step(k)
            if not latent:
                dve.wait_ge(qkT_ready, 3)
                nc.vector.tensor_copy(KTC[:, 0], B["KT"][:, :, 0:S])
                nc.vector.tensor_copy(VC[:, 0], B["V"][:, 0:TT, :])
            link(nc.vector.reciprocal(B["SUM"][:, 1, :], B["SUM"][:, 0, :]))
            dve.wait_ge(groups_done, groups.of("pv", n - 1))
            for t in range(TT):
                ins = nc.vector.tensor_tensor(B["O"][:, t, :].rearrange("p (h d) -> p h d", h=QH),
                                              PS[:, 6 + t, :].rearrange("p (h d) -> p h d", h=QH),
                                              B["SUM"][:, 1, t * QH:(t + 1) * QH].rearrange("p (h o) -> p h o", o=1).to_broadcast([P, QH, HD]), ALU.mult)
            link(ins)
            r = inverse_root(TT, sum_squares(lambda t: B["O"][:, t, :], QW))
            for t in range(TT):
                ins = nc.vector.tensor_scalar(B["O"][:, t, :], B["O"][:, t, :], r[:, t:t + 1], None, ALU.mult)
            ins.then_inc(merged_ready, 1)
            i = cur["stat"] % 2
            for t in range(TT):
                dve.wait_ge(groups_done, groups.of("convT", t))
                b = groups.at["convT", t, "bank"]
                link(nc.vector.bn_stats(B["BN"][:, t, 0:6], PS[:, b, :]))
                link(nc.vector.bn_aggr(B["BN"][:, t, 6:8], B["BN"][:, t, 0:6]))
            r = inverse_root(TT, nc.vector.tensor_copy(st[:, i, 0:TT], B["BN"][:, :, 7]))
            for t in range(TT):
                b = groups.at["convT", t, "bank"]
                nc.vector.tensor_scalar(B["Y"][:, t, :], PS[:, b, :], B["BN"][:, t, 6:7], r[:, t:t + 1], ALU.subtract, ALU.mult
                                        ).then_inc(conv_read, 1)
            dve.wait_ge(conv_read, TT)
            link(nc.vector.tensor_tensor(B["Y"], B["Y"], B["LNR"][:, 0:1, :].to_broadcast([P, TT, CW2]), ALU.mult))
            nc.vector.tensor_tensor(B["Y"], B["Y"], B["LNR"][:, 1:2, :].to_broadcast([P, TT, CW2]), ALU.add).then_inc(act_in_ready, 1)
            dve.wait_ge(act_out_ready, 1)
            r = inverse_root(TT, sum_squares(lambda t: B["Y"][:, t, :], CW2))
            for t in range(TT):
                ins = nc.vector.tensor_scalar(B["Y"][:, t, :], B["Y"][:, t, :], r[:, t:t + 1], None, ALU.mult)
            ins.then_inc(merged_ready, 1)
            for t in range(TT):
                for c in range(2):
                    dve.wait_ge(groups_done, groups.of("mix", c, t))
                    cols = slice(c * 512, (c + 1) * 512)
                    nc.vector.tensor_tensor(H[:, t, cols], PS[:, groups.at["mix", c, t, "bank"], :], B["ROW"][0][:, cols], ALU.mult
                                            ).then_inc(mix_read, 1)
                dve.wait_ge(mix_read, 2 * t + 2)
                nc.vector.tensor_tensor(SRC[:, t, :], SRC[:, t, :], H[:, t, :], ALU.add).then_inc(merged_ready, 1)
                dve.wait_ge(merged_ready, 3 + t)
                r = inverse_root(1, sum_squares(lambda _: SRC[:, t, :], D, 1))
                link(nc.vector.scalar_tensor_tensor(H[:, t, :], SRC[:, t, :], r[:, 0:1], B["ROW"][2], ALU.mult, ALU.mult))
                nc.vector.tensor_tensor(H[:, t, :], H[:, t, :], B["ROW"][1], ALU.add).then_inc(h_ready, 1)


            def best(vals, idx, src, groups_):
                for rnd in range(2):
                    o = slice(8 * rnd, 8 * rnd + 8)
                    for g in range(groups_):
                        ins = nc.vector.max(vals[:, g, o], src[:, g, :])
                    link(ins)
                    for g in range(groups_):
                        ins = nc.vector.max_index(idx[:, g, o], vals[:, g, o], src[:, g, :])
                    link(ins)
                    if rnd == 0:
                        for g in range(groups_):
                            ins = nc.vector.match_replace(src[:, g, :], vals[:, g, o], src[:, g, :], LOW)
                        link(ins)

            def search_keys(t):
                dve.wait_ge(score_read, 4 * (t + 1))
                best(B["TV"], B["TI"], B["SC"][t].rearrange("p (g k) -> p g k", k=EK), 2 * EH)
                link(nc.vector.tensor_copy(B["TF"][:], B["TI"][:]))

            def search_pairs(t):
                tv = B["TV"][:].rearrange("p (h c) k -> p h c k", c=2)
                tf = B["TF"][:].rearrange("p (h c) k -> p h c k", c=2)
                cand = B["CAND"].rearrange("p (h a b) -> p h a b", h=EH, a=TOPK)
                link(nc.vector.tensor_tensor(cand, tv[:, :, 0, :].rearrange("p h (k o) -> p h k o", o=1).to_broadcast([P, EH, TOPK, TOPK]),
                                             tv[:, :, 1:2, :].to_broadcast([P, EH, TOPK, TOPK]), ALU.add))
                best(B["BV"], B["BJ"], B["CAND"].rearrange("p (h n) -> p h n", h=EH), EH)
                bj = B["BJ"][:].rearrange("p h k -> p (h k)")
                nc.vector.tensor_scalar(B["J"][:, 0, :], bj, 4, None, ALU.logical_shift_right)
                link(nc.vector.tensor_scalar(B["J"][:, 1, :], bj, TOPK - 1, None, ALU.bitwise_and))
                link(nc.vector.tensor_copy(B["JF"][:], B["J"][:]))
                hot = B["HOT"].rearrange("p (h a b) -> p h a b", h=EH, a=TOPK)
                hotf = B["HOT"].rearrange("p (n b) -> p n b", b=TOPK)
                for c in range(2):
                    link(nc.vector.tensor_tensor(hotf, B["JF"][:, c, :].rearrange("p (n o) -> p n o", o=1).to_broadcast([P, PICKS, TOPK]),
                                                 iota16.rearrange("p (o k) -> p o k", o=1).to_broadcast([P, PICKS, TOPK]), ALU.is_equal))
                    link(nc.vector.tensor_tensor(hot, hot, tf[:, :, c:c + 1, :].to_broadcast([P, EH, TOPK, TOPK]), ALU.mult))
                    link(nc.vector.tensor_reduce(B["EI"][:, c, :], hotf, AX, ALU.add))
                link(nc.vector.scalar_tensor_tensor(B["EI"][:, 0, :], B["EI"][:, 0, :], float(EK), B["EI"][:, 1, :], ALU.mult, ALU.add))
                nc.vector.tensor_scalar(IDX[:, t, :], B["EI"][:, 0, :], BASE[:, 0:1], None, ALU.add).then_inc(picks_ready, 1)
                ei = B["EI"][:, 2, :].rearrange("p (h k) -> p h k", h=EH)
                nc.vector.tensor_tensor(ei, B["BV"][:], B["BV"][:, :, 0:1].to_broadcast([P, EH, TOPK]), ALU.subtract).then_inc(act_in_ready, 1)
                dve.wait_ge(act_out_ready, 2 + t)
                link(nc.vector.tensor_reduce(B["SUM"][:, 0, 0:EH], ei, AX, ALU.add))
                link(nc.vector.reciprocal(B["SUM"][:, 1, 0:EH], B["SUM"][:, 0, 0:EH]))
                link(nc.vector.tensor_tensor(WGT[:, t, :].rearrange("p (h k) -> p h k", h=EH), ei,
                                             B["SUM"][:, 1, 0:EH].rearrange("p (h o) -> p h o", o=1).to_broadcast([P, EH, TOPK]), ALU.mult))

            return search_keys, search_pairs

        with ExitStack() as ph:
            B = stream_buffers(ph, False)
            CX = sbuf("CX", [P, TT, D], at=ph)
            with nc.Block() as block:
                groups = Groups()

                @block.tensor
                def _(pe):
                    banks = stream_pe(pe, groups, B, False)
                    mod_pe(pe, banks, groups, len(CHUNKS2))

                @block.sync
                def _(sp):
                    sp.dma_start(CX[:], ctx_dram).then_inc(consts_loaded, 16)
                    stream_sp(sp, groups, B, 0, 1)
                    sp.wait_ge(merged_ready, 4)
                    sp.dma_start(cx_dram, CX[:].rearrange("p t d -> p (t d)")).then_inc(stored, 16)
                    used = {8: ("mix", 0, 1), 9: ("mix", 1, 1), 10: ("pq", 1, 0), 11: ("pq", 1, 1)}
                    mod_sp(sp, 1, len(CHUNKS2), lambda c: groups.of(*used[c]) if c in used else groups.of("mod", c - len(CHUNKS2) - WS),
                           lambda: groups.of("pq", TT - 1, 1))
                    sp.wait_ge(stored, 16)

                @block.scalar
                def _(act):
                    stream_act(act, groups, B, 0, False)
                    softmax_act(act, B, 0)
                    softmax_act(act, B, 1)
                    mod_act(act, groups, 16 * (NPIECE // 2))

                @block.vector
                def _(dve):
                    dve.wait_ge(consts_loaded, 16)
                    search_keys, search_pairs = stream_dve(dve, dve_chain(dve), groups, B, CX, 0, False)
                    for t in range(TT):
                        search_keys(t)
                        search_pairs(t)

                @block.gpsimd
                def _(pool):
                    mod_pool(pool, 1, 16 * (NPIECE // 2))
            phase_end()

        with ExitStack() as ph:
            PROJ = sbuf("PROJ1", [P, TT, QKV1], at=ph)
            DEC = sbuf("DEC", [P, RET_H, 3 * P], at=ph)
            BIAS = sbuf("BIAS", [P, MOBA_H, 3 * P], at=ph)
            PP = sbuf("PP", [P, 4 * 3 * P], at=ph)
            CF = sbuf("CF", [P, 6 * S], at=ph)
            GP = sbuf("GP", [P, 2, S + 2], at=ph)
            RAW = sbuf("RAW", [3 * FT + 6, P], at=ph)
            COLS = sbuf("COLS", [P, 3 * FT + 6], at=ph)
            ALPHAI = sbuf("ALPHAI", [P, P], at=ph)
            NM = sbuf("NM1", [P, 2 * MOBA_H], at=ph)
            SUM = sbuf("SUM1", [P, 2, 2 * MOBA_H], at=ph)
            BN = sbuf("BN1", [P, TT, 14], at=ph)
            RQ, RV, RG, MQ, MV = 0, 2 * RW, 3 * RW, 4 * RW, 4 * RW + 2 * MW
            QROT = CT[:].rearrange("p k s -> p (k s)")[:, 0:TT * 2 * RW].rearrange("p (t n) -> p t n", t=TT)
            SQ = CT[:].rearrange("p k s -> p (k s)")[:, 0:TT * RW].rearrange("p (t n) -> p t n", t=TT)
            RT = XT

            def MT(k):
                return PROJ[:, k // 3, (k % 3) * S:(k % 3 + 1) * S]

            T1 = PP[:, 0:768].rearrange("p (t h d) -> p t h d", t=TT, h=12)
            T2 = PP[:, 768:1536].rearrange("p (t h d) -> p t h d", t=TT, h=12)
            PR = PP[:, 0:768].rearrange("p (i n) -> p i n", i=2)
            PT = PP[:, 768:1536].rearrange("p (i n) -> p i n", i=2)
            YR = PROJ[:, :, MQ:MQ + RW]
            YM = PROJ[:, :, MQ + RW:MQ + RW + MW]
            CONV = CF[:].rearrange("p (j s) -> p j s", j=6)
            APAD = CF[:, 0:4 * (S + 2)].rearrange("p (i j s) -> p i j s", i=2, j=2)
            HC = PP[:, 0:1024].rearrange("p (i j s) -> p i j s", i=2, j=2)
            HG = [PP[:, 1024:1536].rearrange("p (j s) -> p j s", j=2), PROJ[:, 0, 2048:2560].rearrange("p (j s) -> p j s", j=2)]
            PAIRS = FT // 2
            PROJ_CH = [(o, min(512, QKV1 - o)) for o in range(0, QKV1, 512)]
            CONV_CH = [(QKV1, 512), (QKV1 + 512, 256)]
            IN_CH = PROJ_CH + CONV_CH
            NPC = len(PROJ_CH)
            V_ROUNDS = PICKS // RING

            with nc.Fori(0, L) as l:
                with nc.Block() as block:
                    groups = Groups()
                    taken = {}

                    @block.tensor
                    def _(pe):
                        banks = Banks(pe, [0, 1, 2, 3])
                        pe.wait_ge(inputs_loaded, 16 * 2)
                        b = banks.take(cols_ready, 1)
                        nc.tensor.transpose(PS[:, b, 0:3 * FT + 6], RAW[:], ident[0:3 * FT + 6, 0:3 * FT + 6]).then_inc(
                            groups_done, groups.mark("cols"))
                        transposes(pe, banks, groups, "xT", lambda t, k: X[:, t, k * P:(k + 1) * P], DK, xT_ready, 0)
                        pe.wait_ge(xT_ready, 4)
                        for c, (o, n) in enumerate(PROJ_CH):
                            weights_in(pe, c)
                            for t in range(TT):
                                b = banks.take(proj_ready, c * TT + t + 1)
                                matmul_rows(pe, b, (0, n), lambda k: XT[:, k, t * P:(t + 1) * P],
                                            lambda k: wslot(c % WS, DK, n)[:, k, :], DK).then_inc(
                                    groups_done, groups.mark("proj", c, t))
                                groups.at["proj", c, t, "bank"] = b
                        for j in range(6):
                            c = NPC + j // 4
                            if j % 4 == 0:
                                weights_in(pe, c)
                            n = IN_CH[c][1]
                            b = banks.take(conv_in_ready, j + 1)
                            matmul_rows(pe, b, (0, S), lambda k: wslot(c % WS, DK, n)[:, k, (j % 4) * P:(j % 4 + 1) * P],
                                        lambda k: XT[:, k, :], DK).then_inc(groups_done, groups.mark("u", j))
                            groups.at["u", j, "bank"] = b
                        pe.wait_ge(proj_ready, TT * NPC)
                        transposes(pe, banks, groups, "mqk", lambda t, k: PROJ[:, t, MQ + k * P:MQ + (k + 1) * P], 6, qkT_ready, 0)
                        pe.wait_ge(rot_ready, 1)
                        transposes(pe, banks, groups, "rqk", lambda t, k: QROT[:, t, k * P:(k + 1) * P], 6, qkT_ready, 3)
                        pe.wait_ge(qkT_ready, 6)
                        for h in range(RET_H + 1):
                            if h < RET_H:
                                q0, pair = HD * (h % 2), h // 2
                                b = banks.take(ret_ready, h + 1)
                                nc.tensor.matmul(PS[:, b, 0:S], RT[q0:q0 + HD, 3 + pair, 0:P], RT[q0:q0 + HD, pair, :], start=True, stop=True)
                                nc.tensor.matmul(PS[:, b, S:3 * P], RT[q0:q0 + HD, 3 + pair, P:S], RT[q0:q0 + HD, pair, P:S], start=True, stop=True
                                                 ).then_inc(groups_done, groups.mark("rs", h))
                                groups.at["rs", h, "bank"] = b
                            if h >= 1:
                                g = h - 1
                                pe.wait_ge(ret_ready, g + 1)
                                w = PT[:, g % 2, :]
                                cols = slice(g * HD, (g + 1) * HD)
                                v = [PROJ[:, t, RV + g * HD:RV + (g + 1) * HD] for t in range(TT)]
                                nc.tensor.matmul(PS[:, 4, cols], w[:, 0:P], v[0], start=True, stop=True)
                                nc.tensor.matmul(PS[:, 5, cols], w[:, P:S], v[0], start=True, stop=False)
                                nc.tensor.matmul(PS[:, 5, cols], w[:, S:3 * P], v[1], start=False, stop=True
                                                 ).then_inc(groups_done, groups.mark("rpv", g))
                        for i in range(MOBA_H + 2):
                            if i < MOBA_H:
                                q0, pair = HD * (i % 2), i // 2
                                b = banks.take(act_in_ready, i + 1)
                                nc.tensor.matmul(PS[:, b, 0:P], MT(pair)[q0:q0 + HD, 0:P], MT(3 + pair)[q0:q0 + HD, 0:P], start=True, stop=True)
                                nc.tensor.matmul(PS[:, b, P:3 * P], MT(pair)[q0:q0 + HD, P:S], MT(3 + pair)[q0:q0 + HD, :], start=True, stop=True
                                                 ).then_inc(groups_done, groups.mark("ms", i))
                                groups.at["ms", i, "bank"] = b
                            if 1 <= i <= MOBA_H:
                                j = i - 1
                                pe.wait_ge(probs_ready, j + 1)
                                b = banks.take(probsT_ready, j + 1)
                                for kb in range(3):
                                    ins = nc.tensor.transpose(PS[:, b, kb * P:(kb + 1) * P], PR[:, j % 2, kb * P:(kb + 1) * P], ident)
                                ins.then_inc(groups_done, groups.mark("pT", j))
                                groups.at["pT", j, "bank"] = b
                            if i >= 2:
                                j = i - 2
                                pe.wait_ge(probsT_ready, j + 1)
                                w = PT[:, j % 2, :]
                                cols = slice(j * HD, (j + 1) * HD)
                                v = [PROJ[:, t, MV + j * HD:MV + (j + 1) * HD] for t in range(TT)]
                                nc.tensor.matmul(PS[:, 6, cols], w[:, 0:P], v[0], start=True, stop=True)
                                nc.tensor.matmul(PS[:, 7, cols], w[:, P:S], v[0], start=True, stop=False)
                                nc.tensor.matmul(PS[:, 7, cols], w[:, S:3 * P], v[1], start=False, stop=True
                                                 ).then_inc(groups_done, groups.mark("pv", j))
                        pe.wait_ge(merged_ready, 1)
                        transposes(pe, banks, groups, "yT", lambda t, k: YR[:, t, k * P:(k + 1) * P], 3, catT_ready, 0)
                        pe.wait_ge(merged_ready, 2)
                        transposes(pe, banks, groups, "oT", lambda t, k: YM[:, t, k * P:(k + 1) * P], 3, catT_ready, 2)
                        pe.wait_ge(catT_ready, 4)
                        pe.wait_ge(conv_ready, 1)
                        for c in range(2):
                            weights_in(pe, 8 + c)
                            for t in range(TT):
                                b = banks.take(mix_read, c * TT + t + 1)
                                matmul_rows(pe, b, (0, 512), lambda k: CT[:, k, t * P:(t + 1) * P],
                                            lambda k: wslot(c, DK, 512)[:, k, :], DK).then_inc(
                                    groups_done, groups.mark("mix", c, t))
                                groups.at["mix", c, t, "bank"] = b
                        pe.wait_ge(h_ready, 1)
                        transposes(pe, banks, groups, "x1T", lambda t, k: X[:, t, k * P:(k + 1) * P], DK, xT_ready, 4)
                        for t in range(TT):
                            for n in range(2):
                                nc.tensor.matmul(PS[:, 4 + 2 * t + n, :], ALPHAI[:], X[:, t, n * 512:(n + 1) * 512], start=True,
                                                 stop=False, skip_group_check=True)
                        pe.wait_ge(xT_ready, 8)

                        def up(i, r, lap):
                            pe.wait_ge(up_loaded[r], 32 * (i // 2 + 1) + lap * 16)
                            if i >= 2:
                                pe.wait_ge(up_read, i - 1 + lap)
                                pe.wait_ge(hidden_ready, i - 1 + lap)
                            for half in range(2):
                                for j in range(2):
                                    for k in range(DK):
                                        c = half * 2 * P + j * P
                                        ins = nc.tensor.matmul(PS[:, 2 * r + half, j * S:(j + 1) * S], wslot(r, DK, 512)[:, k, c:c + P],
                                                               XT[:, k, :], start=(k == 0), stop=(k == DK - 1))
                                ins.then_inc(groups_done, groups.mark("up", i, half))

                        def down(i, r, lap, last=False):
                            pe.wait_ge(down_loaded[r], 16 * (i // 2 + 1) + lap * 8)
                            pe.wait_ge(hidden_ready, i + 1 + lap)
                            for j in range(2):
                                for t in range(TT):
                                    for n in range(2):
                                        ins = nc.tensor.matmul(PS[:, 4 + 2 * t + n, :], HG[r][:, j, t * P:(t + 1) * P],
                                                               wslot(2 + r, 2, D)[:, j, n * 512:(n + 1) * 512], start=False,
                                                               stop=last and j == 1, skip_group_check=True)
                            ins.then_inc(groups_done, groups.mark("down", i))

                        up(0, 0, 0)
                        up(1, 1, 0)
                        down(0, 0, 0)
                        at_loop = groups.n
                        with pe.Fori(0, (PAIRS - 3) // 2) as it:
                            for i in (2, 3):
                                up(i, i % 2, it * 2)
                                down(i - 1, (i - 1) % 2, it * 2)
                        taken["per"] = groups.n - at_loop
                        groups.n += taken["per"] * ((PAIRS - 3) // 2 - 1)
                        up(PAIRS - 1, 0, 0)
                        down(PAIRS - 2, 1, 0)
                        down(PAIRS - 1, 0, 0, last=True)

                    @block.sync
                    def _(sp):
                        sp.dma_start(RAW[0:3 * FT, :], A["ffn_conv_w"].rearrange("l k (f p) -> l (k f) p", p=P)[l]).then_inc(inputs_loaded, 16)
                        sp.dma_start(RAW[3 * FT:3 * FT + 6, :], A["conv_w"].rearrange("l k (f p) -> l (k f) p", p=P)[l]).then_inc(inputs_loaded, 16)

                        def load(c):
                            name, o, n = ("w_in", *IN_CH[c]) if c < 8 else ("w_out", (c - 8) * 512, 512)
                            sp.dma_start(wslot(c % WS, DK, n), wview(name, l)[:, :, o:o + n]).then_inc(weights_loaded[c % WS], 16)

                        last = [("proj", c, 1) for c in range(NPC)]
                        for c in range(4):
                            load(c)
                        sp.dma_start(DEC[:].rearrange("p h n -> p (h n)"), A["decay"]).then_inc(consts_loaded, 16)
                        sp.dma_start(BIAS[:].rearrange("p h n -> p (h n)"), bias_dram).then_inc(consts_loaded, 16)
                        for c in range(4, 10):
                            sp.wait_ge(groups_done, groups.of(*last[c - 4]))
                            load(c)

                        up_v = A["w_up"].rearrange("l (k p) (h f n) -> l f h p k n", p=P, h=2, n=2 * P)[l]
                        down_v = A["w_down"].rearrange("l (f j p) n -> l f p j n", p=P, j=2)[l]

                        def load_up(i, r):
                            for half in range(2):
                                sp.dma_start(wslot(r, DK, 512)[:, :, half * 2 * P:(half + 1) * 2 * P], up_v[i, half]
                                             ).then_inc(up_loaded[r], 16)

                        def load_down(i, r):
                            sp.dma_start(wslot(2 + r, 2, D), down_v[i]).then_inc(down_loaded[r], 16)

                        sp.wait_ge(groups_done, groups.of("u", 3))
                        load_down(0, 0)
                        sp.wait_ge(groups_done, groups.of("u", 5))
                        load_down(1, 1)
                        sp.wait_ge(groups_done, groups.of("ms", MOBA_H - 1))
                        for i, name in enumerate(("ln1_g", "ln1_b")):
                            sp.dma_start(PROJ[:, i, 0:D], A[name].rearrange("(o l) n -> l o n", o=1)[l].to_broadcast([P, D])
                                         ).then_inc(late_rows_loaded, 16)
                        sp.wait_ge(groups_done, groups.of("mix", 0, 1))
                        load_up(0, 0)
                        sp.wait_ge(groups_done, groups.of("mix", 1, 1))
                        load_up(1, 1)
                        for i, name in enumerate(("ln2_g", "ln2_b")):
                            sp.dma_start(PROJ[:, i, D:2 * D], A[name].rearrange("(o l) n -> l o n", o=1)[l].to_broadcast([P, D])
                                         ).then_inc(rows_loaded, 16)
                        per = taken["per"]
                        sp.wait_ge(groups_done, groups.of("up", 0, 1))
                        load_up(2, 0)
                        sp.wait_ge(groups_done, groups.of("down", 0))
                        load_down(2, 0)
                        with sp.Fori(0, (PAIRS - 3) // 2) as it:
                            sp.wait_ge(groups_done, it * per + groups.of("up", 1, 1))
                            load_up(it * 2 + 3, 1)
                            sp.wait_ge(groups_done, it * per + groups.of("down", 1))
                            load_down(it * 2 + 3, 1)
                            sp.wait_ge(groups_done, it * per + groups.of("up", 2, 1))
                            load_up(it * 2 + 4, 0)
                            sp.wait_ge(groups_done, it * per + groups.of("down", 2))
                            load_down(it * 2 + 4, 0)

                    @block.scalar
                    def _(act):
                        def bank(*name):
                            act.wait_ge(groups_done, groups.of(*name))
                            return groups.at[name + ("bank",)]

                        for j in range(DK // 2):
                            b = bank("xT", j)
                            nc.scalar.copy(XT[:, 2 * j:2 * j + 2, :].rearrange("p k s -> p (k s)"), PS[:, b, :]).then_inc(xT_ready, 1)
                        for c, (o, n) in enumerate(PROJ_CH):
                            for t in range(TT):
                                b = bank("proj", c, t)
                                nc.scalar.copy(PROJ[:, t, o:o + n], PS[:, b, 0:n]).then_inc(proj_ready, 1)
                        for j in range(6):
                            b = bank("u", j)
                            nc.scalar.copy(CONV[:, j, :], PS[:, b, 0:S]).then_inc(conv_in_ready, 1)
                        act.wait_ge(proj_ready, TT * NPC)
                        nc.scalar.activation(PROJ[:, :, RG:RG + RW], PROJ[:, :, RG:RG + RW], ACT.Silu).then_inc(silu_ready, 1)
                        act.wait_ge(rot_ready, 1)
                        for j in range(3):
                            b = bank("mqk", j)
                            nc.scalar.copy(MT(2 * j), PS[:, b, 0:S])
                            nc.scalar.copy(MT(2 * j + 1), PS[:, b, S:2 * S]).then_inc(qkT_ready, 1)
                        for j in range(3):
                            b = bank("rqk", j)
                            nc.scalar.copy(RT[:, 2 * j:2 * j + 2, :].rearrange("p k s -> p (k s)"), PS[:, b, :]).then_inc(qkT_ready, 1)
                        root(act, TT * RET_H, 0, 1.0 / HD, 0)
                        for i in range(MOBA_H):
                            act.wait_ge(max_ready, i + 1)
                            nc.scalar.activation(PR[:, i % 2, 0:P], PR[:, i % 2, 0:P], ACT.Exp, bias=NM[:, 2 * i:2 * i + 1],
                                                 accum_out=SUM[:, 0, i:i + 1])
                            nc.scalar.activation(PR[:, i % 2, P:3 * P], PR[:, i % 2, P:3 * P], ACT.Exp, bias=NM[:, 2 * i + 1:2 * i + 2],
                                                 accum_out=SUM[:, 0, MOBA_H + i:MOBA_H + i + 1]).then_inc(probs_ready, 1)
                        for name, k0 in (("yT", 0), ("oT", 3)):
                            for j in range(2):
                                b = bank(name, j)
                                n = 2 - j
                                nc.scalar.copy(CT[:, k0 + 2 * j:k0 + 2 * j + n, :].rearrange("p k s -> p (k s)"), PS[:, b, 0:n * S]).then_inc(catT_ready, 1)
                        act.wait_ge(dots_ready, 1)
                        nc.scalar.activation(DOT[:, 0, :], DOT[:, 0, :], ACT.Gelu).then_inc(gelu_ready, 1)
                        root(act, TT, 1, 1.0, 0)
                        for j in range(DK // 2):
                            b = bank("x1T", j)
                            nc.scalar.copy(XT[:, 2 * j:2 * j + 2, :].rearrange("p k s -> p (k s)"), PS[:, b, :]).then_inc(xT_ready, 1)
                        per = taken["per"]

                        def hidden(i, r, lap, glap):
                            act.wait_ge(groups_done, groups.of("up", i, 0) + glap)
                            if i >= 2:
                                act.wait_ge(conv_done, i + lap)
                            nc.scalar.copy(APAD[:, r, :, 2:2 + S], PS[:, 2 * r, :].rearrange("p (j s) -> p j s", j=2)).then_inc(up_read, 1)
                            act.wait_ge(conv_done, i + 2 + lap)
                            nc.scalar.activation(HC[:, r], HC[:, r], ACT.Gelu).then_inc(gelu_done, 1)

                        act.wait_ge(conv_done, 1)
                        hidden(0, 0, 0, 0)
                        hidden(1, 1, 0, 0)
                        with act.Fori(0, (PAIRS - 3) // 2) as it:
                            hidden(2, 0, it * 2, it * per)
                            hidden(3, 1, it * 2, it * per)
                        hidden(PAIRS - 1, 0, 0, 0)
                        root(act, TT, 2, 1.0, 0)

                    @block.vector
                    def _(dve):
                        link = dve_chain(dve)
                        dve.sem_inc(rows_used, RING)
                        link(nc.vector.tensor_copy(PROD[:], H[:].rearrange("p t d -> p (t d)")[:, bass.ts(l, D)]))
                        link(nc.vector.tensor_copy(COEF[:, 1, :], WGT[:].rearrange("p t d -> p (t d)")[:, bass.ts(l, PICKS)]))
                        nc.vector.tensor_scalar(ALPHAI[:], ident, ALPHA, None, ALU.mult)
                        link(nc.vector.memset(GP[:, :, 0:2], 0.0))
                        dve.wait_ge(groups_done, groups.of("cols"))
                        nc.vector.tensor_copy(COLS[:], PS[:, 0, 0:3 * FT + 6]).then_inc(cols_ready, 1)
                        before = l * 2 * V_ROUNDS
                        EARLY, MID = 6, 6
                        with dve.Fori(0, EARLY) as e:
                            link.count.enter(e, 1)
                            dot_round(dve, BESIDE, PROD[:], DOT[:, 0, bass.ts(e, RING)], e, before, link)
                        link.count.leave(EARLY)
                        taken["dots"] = EARLY * RING

                        def dots(n):
                            for _ in range(n):
                                e, k = divmod(taken["dots"], RING)
                                dot_step(dve, BESIDE, PROD[:], k, e, before)
                                if k == RING - 1:
                                    dots_out(dve, BESIDE, DOT[:, 0, e * RING:(e + 1) * RING], e, link)
                                taken["dots"] += 1

                        dve.wait_ge(proj_ready, TT * NPC)
                        cos, sin = (angles(c).to_broadcast([P, TT, 12, 32]) for c in (C_COS1, C_SIN1))
                        qk = PROJ[:, :, 0:2 * RW].rearrange("p t (h d) -> p t h d", h=12)
                        qr = QROT.rearrange("p t (h d) -> p t h d", h=12)
                        for half, (f1, f2, op) in enumerate(((cos, sin, ALU.subtract), (sin, cos, ALU.add))):
                            nc.vector.tensor_tensor(T1, qk[:, :, :, 0:32], f1, ALU.mult)
                            link(nc.vector.tensor_tensor(T2, qk[:, :, :, 32:64], f2, ALU.mult))
                            ins = nc.vector.tensor_tensor(qr[:, :, :, half * 32:half * 32 + 32], T1, T2, op)
                            if half == 0:
                                link(ins)
                        ins.then_inc(rot_ready, 1)
                        dve.wait_ge(conv_in_ready, 6)
                        dve.wait_ge(rot_ready, 1)
                        link(nc.vector.tensor_tensor(GP[:, :, 2:2 + S], CONV[:, 2:4, :], CONV[:, 4:6, :], ALU.mult))
                        for k in range(3):
                            for j in range(2):
                                tap = COLS[:, 3 * FT + 2 * k + j:3 * FT + 2 * k + j + 1]
                                if k == 0:
                                    ins = nc.vector.tensor_scalar(CT[:, 6 + j, :], GP[:, j, 0:S], tap, None, ALU.mult)
                                else:
                                    ins = nc.vector.scalar_tensor_tensor(CT[:, 6 + j, :], GP[:, j, k:k + S], tap, CT[:, 6 + j, :], ALU.mult, ALU.add)
                            link(ins)
                        nc.vector.tensor_tensor(CT[:, 6:8, :], CT[:, 6:8, :], CONV[:, 0:2, :], ALU.mult).then_inc(conv_ready, 1)
                        dve.wait_ge(consts_loaded, 32)
                        for h in range(RET_H):
                            dve.wait_ge(groups_done, groups.of("rs", h))
                            if h >= 2:
                                dve.wait_ge(groups_done, groups.of("rpv", h - 2))
                            nc.vector.tensor_tensor(PT[:, h % 2, :], PS[:, groups.at["rs", h, "bank"], 0:3 * P], DEC[:, h, :], ALU.mult
                                                    ).then_inc(ret_ready, 1)
                            dots(MID * RING // 2 // RET_H)
                        dve.wait_ge(groups_done, groups.of("rpv", RET_H - 1))

                        def heads(ap):
                            return ap.rearrange("p t (h d) -> p (t h) d", h=RET_H)

                        def spread(ap):
                            return ap.rearrange("p (t h o) -> p t h o", t=TT, o=1).to_broadcast([P, TT, RET_H, HD])

                        raw = PS[:, 4:6, 0:RW].rearrange("p t (h d) -> p t h d", h=RET_H)
                        yr = YR.rearrange("p t (h d) -> p t h d", h=RET_H)
                        link(nc.vector.tensor_reduce(NM[:, 0:12].rearrange("p (t h) -> p t h", t=TT), raw, AX, ALU.add))
                        link(nc.vector.tensor_scalar(NM[:, 0:12], NM[:, 0:12], 1.0 / HD, None, ALU.mult))
                        link(nc.vector.tensor_tensor(yr, raw, spread(NM[:, 0:12]), ALU.subtract))
                        link(nc.vector.tensor_tensor(SQ, YR, YR, ALU.mult))
                        nc.vector.tensor_reduce(st[:, 0, 0:12].rearrange("p (t h) -> p t h", t=TT),
                                                SQ.rearrange("p t (h d) -> p t h d", h=RET_H), AX, ALU.add).then_inc(stat_ready, 1)

                        def scores(i):
                            dve.wait_ge(groups_done, groups.of("ms", i))
                            if i >= 2:
                                dve.wait_ge(groups_done, groups.of("pT", i - 2))
                            ins = nc.vector.scalar_tensor_tensor(PR[:, i % 2, :], PS[:, groups.at["ms", i, "bank"], 0:3 * P], HD ** -0.5,
                                                                 BIAS[:, i, :], ALU.mult, ALU.add)
                            ins.then_inc(act_in_ready, 1)
                            dve.wait_ge(act_in_ready, i + 1)
                            nc.vector.tensor_reduce(NM[:, 2 * i:2 * i + 1], PR[:, i % 2, 0:P], AX, ALU.max, negate=True)
                            nc.vector.tensor_reduce(NM[:, 2 * i + 1:2 * i + 2], PR[:, i % 2, P:3 * P], AX, ALU.max, negate=True
                                                    ).then_inc(max_ready, 1)

                        scores(0)
                        dve.wait_ge(root_ready, 1)
                        link(nc.vector.reciprocal(ri[:, 0, 0:12], rt[:, 0, 0:12]))
                        link(nc.vector.tensor_tensor(yr, yr, spread(ri[:, 0, 0:12]), ALU.mult))
                        dve.wait_ge(silu_ready, 1)
                        nc.vector.tensor_tensor(YR, YR, PROJ[:, :, RG:RG + RW], ALU.mult).then_inc(merged_ready, 1)
                        for i in range(MOBA_H):
                            if i + 1 < MOBA_H:
                                scores(i + 1)
                            dve.wait_ge(groups_done, groups.of("pT", i))
                            if i >= 2:
                                dve.wait_ge(groups_done, groups.of("pv", i - 2))
                            nc.vector.tensor_copy(PT[:, i % 2, :], PS[:, groups.at["pT", i, "bank"], 0:3 * P]).then_inc(probsT_ready, 1)
                            dots(MID * RING // 2 // MOBA_H)
                        link(nc.vector.reciprocal(SUM[:, 1, :], SUM[:, 0, :]))
                        dve.wait_ge(groups_done, groups.of("pv", MOBA_H - 1))
                        nc.vector.tensor_tensor(YM.rearrange("p t (h d) -> p t h d", h=MOBA_H),
                                                PS[:, 6:8, 0:MW].rearrange("p t (h d) -> p t h d", h=MOBA_H),
                                                spread(SUM[:, 1, :]), ALU.mult).then_inc(merged_ready, 1)
                        dots(PICKS - taken["dots"])
                        dve.sem_inc(dots_ready, 1)
                        for c in range(2):
                            for t in range(TT):
                                dve.wait_ge(groups_done, groups.of("mix", c, t))
                                cols = slice(c * 512, (c + 1) * 512)
                                nc.vector.scalar_tensor_tensor(X[:, t, cols], X[:, t, cols], ALPHA, PS[:, groups.at["mix", c, t, "bank"], :],
                                                               ALU.mult, ALU.add).then_inc(mix_read, 1)
                        dve.wait_ge(mix_read, 4)

                        def norm(halves, i, rows):
                            for t in range(TT):
                                nc.vector.bn_stats(BN[:, t, 0:6], halves(t, 0))
                                link(nc.vector.bn_stats(BN[:, t, 6:12], halves(t, 1)))
                                link(nc.vector.bn_aggr(BN[:, t, 12:14], BN[:, t, 0:12]))
                            nc.vector.tensor_copy(st[:, i % 2, 0:TT], BN[:, :, 13]).then_inc(stat_ready, 1)
                            dve.wait_ge(root_ready, i + 1)
                            link(nc.vector.reciprocal(ri[:, i % 2, 0:TT], rt[:, i % 2, 0:TT]))
                            for t in range(TT):
                                for n in range(2):
                                    ins = nc.vector.tensor_scalar(X[:, t, n * 512:(n + 1) * 512], halves(t, n), BN[:, t, 12:13],
                                                                  ri[:, i % 2, t:t + 1], ALU.subtract, ALU.mult)
                            link(ins)
                            link(nc.vector.tensor_tensor(X[:], X[:], PROJ[:, 0:1, rows:rows + D].to_broadcast([P, TT, D]), ALU.mult))
                            nc.vector.tensor_tensor(X[:], X[:], PROJ[:, 1:2, rows:rows + D].to_broadcast([P, TT, D]), ALU.add).then_inc(h_ready, 1)

                        dve.wait_ge(late_rows_loaded, 32)
                        norm(lambda t, n: X[:, t, n * 512:(n + 1) * 512], 1, 0)
                        dve.wait_ge(gelu_ready, 1)
                        link(nc.vector.tensor_tensor(COEF[:, 0, :], DOT[:, 0, :], COEF[:, 1, :], ALU.mult))
                        link(nc.vector.memset(PROD[:], 0.0))
                        dve.wait_ge(catT_ready, 4)
                        nc.vector.memset(APAD[:, :, :, 0:2], 0.0).then_inc(conv_done, 1)
                        per = taken["per"]

                        def hidden(i, r, pair, lap, glap, rounds, n8):
                            dve.wait_ge(up_read, i + 1 + lap)
                            for k in range(3):
                                for j in range(2):
                                    c = k * FT + j
                                    tap = COLS[:, 2 * i + c:2 * i + c + 1] if pair is None else COLS[:, bass.ds(pair * 2 + c, 1)]
                                    if k == 0:
                                        ins = nc.vector.tensor_scalar(HC[:, r, j, :], APAD[:, r, j, 0:S], tap, None, ALU.mult)
                                    else:
                                        ins = nc.vector.scalar_tensor_tensor(HC[:, r, j, :], APAD[:, r, j, k:k + S], tap, HC[:, r, j, :], ALU.mult, ALU.add)
                                if k < 2:
                                    link(ins)
                            ins.then_inc(conv_done, 1)
                            for v in range(rounds):
                                m = n8 + v
                                sum_round(dve, BESIDE, PROD[:], lambda k: COEF[:, 0, m * RING + k:m * RING + k + 1] if isinstance(m, int)
                                          else COEF[:, 0, bass.ds(m * RING + k, 1)], m + V_ROUNDS, before)
                            dve.wait_ge(gelu_done, i + 1 + lap)
                            dve.wait_ge(groups_done, groups.of("up", i, 1) + glap)
                            if i >= 2:
                                down_before = groups.of("down", 0) if i == 2 else groups.of("down", 1)
                                if i == PAIRS - 1:
                                    down_before = groups.of("down", 2) + per * ((PAIRS - 3) // 2 - 1)
                                dve.wait_ge(groups_done, down_before + glap)
                            nc.vector.tensor_tensor(HG[r], HC[:, r], PS[:, 2 * r + 1, :].rearrange("p (j s) -> p j s", j=2), ALU.mult
                                                    ).then_inc(hidden_ready, 1)

                        hidden(0, 0, None, 0, 0, 1, 0)
                        hidden(1, 1, None, 0, 0, 1, 1)
                        with dve.Fori(0, (PAIRS - 3) // 2) as it:
                            link.count.enter(it, 4)
                            hidden(2, 0, it * 2 + 2, it * 2, it * per, 2, it * 3 + 2)
                            hidden(3, 1, it * 2 + 3, it * 2, it * per, 1, it * 3 + 4)
                        link.count.leave((PAIRS - 3) // 2)
                        hidden(PAIRS - 1, 0, None, 0, 0, 2, 14)
                        dve.wait_ge(rows_used, RING + 2 * PICKS)
                        nc.vector.tensor_copy(ACC[:].rearrange("p t d -> p (t d)")[:, bass.ts(l, D)], PROD[:])
                        dve.wait_ge(groups_done, groups.of("down", PAIRS - 1))
                        dve.wait_ge(rows_loaded, 32)
                        norm(lambda t, n: PS[:, 4 + 2 * t + n, :], 2, D)

                    @block.gpsimd
                    def _(pool):
                        idx = IDX[:].rearrange("p t n -> p (t n)")
                        for i, table in enumerate(("peer_u_2", "peer_v_2")):
                            gather_rows(pool, BESIDE, table, lambda e: idx[:, bass.ds(l * PICKS + e * RING, RING)], i * PICKS)
                phase_end()

        with ExitStack() as ph:
            CX = sbuf("CXK", [P, TT, D], at=ph)
            GATE = sbuf("GATEK", [P, D], at=ph)
            MODR = sbuf("MODRK", [16, P], at=ph)
            MODC = sbuf("MODCK", [P, 16], at=ph)
            GAIN = sbuf("GAINK", [P, 1, HD], at=ph)
            KV = sbuf("KV", [P, TT, 2 * KVW], at=ph)
            KD = sbuf("KD", [P, TT, KVH, 2, HD], at=ph)
            XN = CT[:].rearrange("p k s -> p (k s)").rearrange("p (t d) -> p t d", t=TT)
            with nc.Block() as block:
                groups = Groups()

                @block.tensor
                def _(pe):
                    banks = Banks(pe, list(range(8)))
                    pe.wait_ge(inputs_loaded, 16)
                    b = banks.take(cols_ready, 1)
                    nc.tensor.transpose(PS[:, b, 0:16], MODR[:], ident[0:16, 0:16]).then_inc(groups_done, groups.mark("cols"))
                    pe.wait_ge(norm_ready, TT)
                    transposes(pe, banks, groups, "xT", lambda t, k: XN[:, t, k * P:(k + 1) * P], DK, xT_ready, 0)
                    pe.wait_ge(xT_ready, 4)
                    weights_in(pe, 0)
                    for t in range(TT):
                        b = banks.take(proj_ready, t + 1)
                        matmul_rows(pe, b, (0, 2 * KVW), lambda k: XT[:, k, t * P:(t + 1) * P],
                                    lambda k: wslot(0, DK, 2 * KVW)[:, k, :], DK).then_inc(groups_done, groups.mark("proj", t))
                        groups.at["proj", t, "bank"] = b
                    pe.wait_ge(rot_ready, 1)
                    transposes(pe, banks, groups, "kT", lambda t, k: KD[:, t, k].rearrange("p c d -> p (c d)"), KVH, qkT_ready, 0)

                @block.sync
                def _(sp):
                    sp.dma_start(CX[:].rearrange("p t d -> p (t d)"), cx_dram).then_inc(rows_loaded, 16)
                    sp.dma_start(GATE[:], mod_dram[0, 1:2, 5 * D:6 * D].to_broadcast([P, D])).then_inc(rows_loaded, 16)
                    sp.dma_start(GAIN[:, 0, :], A["k_gain_2"][1:2, :].to_broadcast([P, HD])).then_inc(rows_loaded, 16)
                    sp.dma_start(MODR[:], mod_dram[1, 1:2, 0:2 * D].rearrange("o (k p) -> (o k) p", p=P)).then_inc(inputs_loaded, 16)
                    sp.dma_start(wslot(0, DK, 2 * KVW), wview("w_in_2", 1)[:, :, QW:QKV2]).then_inc(weights_loaded[0], 16)

                @block.scalar
                def _(act):
                    root(act, TT, 0, 1.0 / D, 1)
                    act.wait_ge(cols_ready, 1)
                    for j in range(DK // 2):
                        act.wait_ge(groups_done, groups.of("xT", j))
                        for k in range(2):
                            ins = nc.scalar.activation(XT[:, 2 * j + k, :], PS[:, groups.at["xT", j, "bank"], k * S:(k + 1) * S], ACT.Identity,
                                                       bias=MODC[:, 2 * j + k:2 * j + k + 1], scale=MODC[:, 8 + 2 * j + k:9 + 2 * j + k])
                        ins.then_inc(xT_ready, 1)
                    for t in range(TT):
                        act.wait_ge(groups_done, groups.of("proj", t))
                        nc.scalar.copy(KV[:, t, :], PS[:, groups.at["proj", t, "bank"], 0:2 * KVW]).then_inc(proj_ready, 1)
                    root(act, TT * KVH, 1, 1.0 / HD, 1)
                    act.wait_ge(groups_done, groups.of("kT", 0))
                    nc.scalar.copy(KTC[:, 1], PS[:, groups.at["kT", 0, "bank"], :].rearrange("p (k s) -> p k s", k=KVH)).then_inc(qkT_ready, 1)

                @block.vector
                def _(dve):
                    link = dve_chain(dve)
                    dve.wait_ge(rows_loaded, 16 * 3)
                    link(nc.vector.tensor_tensor(ACC[:], ACC[:], GATE[:].rearrange("p (o d) -> p o d", o=1).to_broadcast([P, TT, D]), ALU.mult))
                    link(nc.vector.tensor_tensor(CX[:], CX[:], ACC[:], ALU.add))
                    for t in range(TT):
                        ins = nc.vector.tensor_tensor_reduce(PROD[:], CX[:, t, :], CX[:, t, :], 1.0, 0.0, ALU.mult, ALU.add, st[:, 0, t:t + 1])
                        if t == 0:
                            link(ins)
                    ins.then_inc(stat_ready, 1)
                    dve.wait_ge(groups_done, groups.of("cols"))
                    nc.vector.tensor_copy(MODC[:, 0:8], PS[:, 0, 0:8])
                    nc.vector.tensor_scalar(MODC[:, 8:16], PS[:, 0, 8:16], 1.0, None, ALU.add).then_inc(cols_ready, 1)
                    dve.wait_ge(root_ready, 1)
                    link(nc.vector.reciprocal(ri[:, 0, 0:TT], rt[:, 0, 0:TT]))
                    for t in range(TT):
                        nc.vector.tensor_scalar(XN[:, t, :], CX[:, t, :], ri[:, 0, t:t + 1], None, ALU.mult).then_inc(norm_ready, 1)
                    dve.wait_ge(proj_ready, TT)
                    nc.vector.tensor_copy(VC[:, 1], KV[:, :, KVW:2 * KVW])
                    k4 = KV[:, :, 0:KVW].rearrange("p t (h d) -> p t h d", h=KVH)
                    sq = PROD[:, 0:TT * KVW].rearrange("p (t h d) -> p t h d", t=TT, h=KVH)
                    link(nc.vector.tensor_tensor(sq, k4, k4, ALU.mult))
                    nc.vector.tensor_reduce(st[:, 1, 0:4].rearrange("p (t h) -> p t h", t=TT), sq, AX, ALU.add).then_inc(stat_ready, 1)
                    dve.wait_ge(root_ready, 2)
                    link(nc.vector.reciprocal(ri[:, 1, 0:4], rt[:, 1, 0:4]))
                    link(nc.vector.tensor_tensor(k4, k4, ri[:, 1, 0:4].rearrange("p (t h o) -> p t h o", t=TT, o=1).to_broadcast([P, TT, KVH, HD]), ALU.mult))
                    for c in range(2):
                        ins = nc.vector.tensor_tensor(KD[:, :, :, c, :], k4, GAIN[:].rearrange("p (t o) d -> p t o d", t=1).to_broadcast([P, TT, KVH, HD]), ALU.mult)
                    ins.then_inc(rot_ready, 1)
            phase_end()

        with ExitStack() as ph:
            B = stream_buffers(ph, True)
            with nc.Fori(0, L) as l:
                with nc.Block() as block:
                    groups = Groups()

                    @block.tensor
                    def _(pe):
                        stream_pe(pe, groups, B, True)

                    @block.sync
                    def _(sp):
                        stream_sp(sp, groups, B, l, 0)
                        sp.wait_ge(groups_done, groups.of("pq", TT - 1, 1))
                        sp.dma_start(G2ROW, mod_dram[l][0:1, 5 * D:6 * D].to_broadcast([P, D])).then_inc(rows_loaded, 16)

                    @block.scalar
                    def _(act):
                        stream_act(act, groups, B, l, True)
                        softmax_act(act, B, 0)
                        softmax_act(act, B, 1)
                        for t in range(TT):
                            act.wait_ge(dots_ready, t + 1)
                            nc.scalar.activation(DOT[:, t, :], DOT[:, t, :], ACT.Gelu).then_inc(gelu_ready, 1)

                    @block.vector
                    def _(dve):
                        link = dve_chain(dve)
                        search_keys, search_pairs = stream_dve(dve, link, groups, B, X, l, True)
                        dve.sem_inc(rows_used, RING2)
                        rounds = PICKS // RING2
                        before = l * 2 * TT * rounds
                        search_keys(0)
                        search_pairs(0)
                        search_keys(1)
                        dot_round(dve, ALONE, H[:, 0, :], DOT[:, 0, 0:RING2], 0, before, link)
                        search_pairs(1)
                        for t in range(TT):
                            with dve.Fori(1 - t, rounds) as e:
                                link.count.enter(e - (1 - t), 1)
                                dot_round(dve, ALONE, H[:, t, :], DOT[:, t, bass.ts(e, RING2)], e + t * rounds, before, link)
                            link.count.leave(rounds - 1 + t)
                            dve.sem_inc(dots_ready, 1)
                        link(nc.vector.memset(ACC[:], 0.0))
                        for t in range(TT):
                            dve.wait_ge(gelu_ready, t + 1)
                            link(nc.vector.tensor_tensor(COEF[:, t, :], DOT[:, t, :], WGT[:, t, :], ALU.mult))
                            with dve.Fori(0, rounds) as e:
                                sum_round(dve, ALONE, ACC[:, t, :], lambda k: COEF[:, t, bass.ds(e * RING2 + k, 1)], e + (TT + t) * rounds, before)
                        dve.wait_ge(rows_used, RING2 + 2 * TT * PICKS)
                        dve.wait_ge(rows_loaded, 16 * 7)
                        link(nc.vector.tensor_tensor(ACC[:], ACC[:], G2ROW.rearrange("p (o d) -> p o d", o=1).to_broadcast([P, TT, D]), ALU.mult))
                        nc.vector.tensor_tensor(X[:], X[:], ACC[:], ALU.add)
                        link(nc.vector.tensor_scalar(BASE[:], BASE[:], float(N_EXP), None, ALU.add))

                    @block.gpsimd
                    def _(pool):
                        pool.wait_ge(groups_done, groups.of("pq", TT - 1, 1))
                        for i, table in enumerate(("peer_u_2", "peer_v_2")):
                            for t in range(TT):
                                pool.wait_ge(picks_ready, t + 1)
                                gather_rows(pool, ALONE, table, lambda e: IDX[:, t, bass.ds(e * RING2, RING2)], (i * TT + t) * PICKS)
                phase_end()

        with ExitStack() as ph:
            FG = sbuf("FG", [P, D], at=ph)
            with nc.Block() as block:

                @block.sync
                def _(sp):
                    sp.dma_start(FG[:], A["final_g_2"].rearrange("(o n) -> o n", o=1).to_broadcast([P, D])).then_inc(rows_loaded, 16)
                    for t in range(TT):
                        sp.wait_ge(norm_ready, t + 1)
                        sp.dma_start(out_dram[:, t, :], X[:, t, :]).then_inc(stored, 16)
                    sp.wait_ge(stored, 16 * TT)

                @block.scalar
                def _(act):
                    root(act, TT, 0, 1.0 / D, 1)

                @block.vector
                def _(dve):
                    link = dve_chain(dve)
                    for t in range(TT):
                        ins = nc.vector.tensor_tensor_reduce(H[:, t, :], X[:, t, :], X[:, t, :], 1.0, 0.0, ALU.mult, ALU.add, st[:, 0, t:t + 1])
                    ins.then_inc(stat_ready, 1)
                    dve.wait_ge(root_ready, 1)
                    link(nc.vector.reciprocal(ri[:, 0, 0:TT], rt[:, 0, 0:TT]))
                    dve.wait_ge(rows_loaded, 16)
                    for t in range(TT):
                        nc.vector.scalar_tensor_tensor(X[:, t, :], X[:, t, :], ri[:, 0, t:t + 1], FG[:], ALU.mult, ALU.mult
                                                       ).then_inc(norm_ready, 1)


def constants():
    c = np.zeros((P, C_END), np.float32)
    c[:, C_ID:C_ID + P] = np.eye(P)
    c[:, C_FLIP:C_FLIP + P] = np.eye(P)[::-1]
    c[:, C_IOTA:C_IOTA + TOPK] = np.arange(TOPK)
    pos = np.arange(S, dtype=np.float32)
    inv1 = np.float32(10000.0) ** (-np.arange(0, HD, 2, dtype=np.float32) / np.float32(HD))
    ang1 = pos[:, None] * inv1[None, :].astype(np.float32)
    n = HD // 4
    inv2 = np.float32(10000.0) ** (-np.arange(n, dtype=np.float32) / np.float32(n))
    row, col = np.arange(S) // 64, np.arange(S) % 64
    ang2 = np.concatenate([row[:, None].astype(np.float32) * inv2, col[:, None].astype(np.float32) * inv2], -1)
    for c0, table in ((C_COS1, np.cos(ang1.astype(np.float64))), (C_SIN1, np.sin(ang1.astype(np.float64))),
                      (C_COS2, np.cos(ang2.astype(np.float64))), (C_SIN2, np.sin(ang2.astype(np.float64)))):
        c[:, c0:c0 + TT * 32] = table.reshape(TT, P, 32).transpose(1, 0, 2).reshape(P, TT * 32)
    dist = S - 1 - np.arange(2 * S - 1)
    exact = REL_BUCKETS // 2
    nf = np.maximum(dist, 1).astype(np.float32)
    large = exact + (np.log(nf / np.float32(exact)) / np.float32(np.log(REL_MAX / exact))
                     * np.float32(REL_BUCKETS - exact)).astype(np.int32)
    bucket = np.where(dist < exact, np.maximum(dist, 0), np.minimum(large, REL_BUCKETS - 1))
    buckets = np.zeros((REL_BUCKETS + 1, 2 * S - 1), np.float32)
    ok = dist >= 0
    buckets[bucket[ok], np.nonzero(ok)[0]] = 1.0
    buckets[REL_BUCKETS, ~ok] = MASKED
    e, q = np.arange(P)[:, None], np.arange(S)[None, :]
    decay = np.zeros((P, RET_H, 3 * P), np.float32)
    for h in range(RET_H):
        log_g = np.log(np.float32(1.0) - np.float32(2.0) ** np.float32(-5.0 - h)).astype(np.float64)
        d = q - e
        full = np.where(d >= 0, np.exp(np.maximum(d, 0) * log_g), 0.0) * HD ** -0.5
        decay[:, h, 0:S] = full
        decay[:, h, S:] = full[:, 0:P]
    return {"consts": c, "buckets": buckets, "decay": decay.reshape(P, RET_H * 3 * P)}


_INS = ["x", "w_in", "conv_w", "w_out", "ln1_g", "ln1_b", "w_up", "ffn_conv_w", "w_down", "ln2_g", "ln2_b",
        "rel_bias", "c_2", "ctx_2", "c_ctx_2", "w_mod_2", "b_mod_2", "w_in_2", "q_gain_2", "k_gain_2",
        "conv_w_2", "conv_b_2", "ln_g_2", "ln_b_2", "beta_attn_2", "beta_conv_2", "w_o_2", "peer_wq_2",
        "peer_keys_2", "peer_u_2", "peer_v_2", "final_g_2"]


def kernel(**inputs):
    import concourse.bacc as bacc
    from concourse.bass_utils import run_bass_kernel_spmd

    nc = bacc.Bacc("TRN2", target_bir_lowering=False, num_devices=1)
    arrays, aps = {}, {}
    given = {n: np.ascontiguousarray(inputs[n]) for n in _INS}
    given.update(constants())
    for name, a in given.items():
        arrays[f"in_{name}"] = a
        aps[name] = nc.dram_tensor(f"in_{name}", a.shape, mybir.dt.from_np(a.dtype), kind="ExternalInput").ap()
    out = nc.dram_tensor("out", (1, S, D), F32, kind="ExternalOutput").ap()
    program(nc, aps, out)
    r = run_bass_kernel_spmd(nc, [arrays], core_ids=[0])
    return r.results[0]["out"]
```

```python
from contextlib import ExitStack

import concourse.bass as bass
import numpy as np
from concourse import mybir

F32 = mybir.dt.float32
I32 = mybir.dt.int32
U32 = mybir.dt.uint32
ALU = mybir.AluOpType
ACT = mybir.ActivationFunctionType
AX = mybir.AxisListType.X

P = 128
D = 1024
S = 256
TT = S // P
DK = D // P
L = 2
HD = 64

RET_H, MOBA_H = 6, 6
RW, MW, CW1 = 384, 384, 256
QKV1 = 4 * RW + 3 * MW
FF = 2816
FT = FF // P
ALPHA = (2.0 * L) ** 0.25
LN_EPS = 1e-5
REL_BUCKETS, REL_MAX = 32, 128
MASKED = -1.0e30

QH, KVH = 8, 2
QW, KVW = QH * HD, KVH * HD
CW2, TAPS2 = 512, 31
HALO = TAPS2 // 2
QKV2 = QW + 2 * KVW
RMS_EPS = 1e-6
EH, EK, TOPK = 8, 128, 16
PICKS = EH * TOPK
N_EXP = EK * EK
LOW = -3.0e38

RING = 8
RING2 = 16
WS = 4
WCOL = 4096

C_ID, C_FLIP, C_IOTA = 0, P, 2 * P
C_COS1, C_SIN1 = C_IOTA + 16, C_IOTA + 16 + TT * 32
C_COS2, C_SIN2 = C_SIN1 + TT * 32, C_SIN1 + 2 * TT * 32
C_END = C_SIN2 + TT * 32


class Groups:

    def __init__(self):
        self.n, self.at = 0, {}

    def mark(self, *name):
        self.n += 1
        self.at[name] = self.n
        return 1

    def of(self, *name):
        return self.at[name]


class Banks:

    def __init__(self, pe, banks):
        self.pe, self.banks, self.i, self.read_out = pe, banks, 0, {}

    def take(self, sem, value):
        b = self.banks[self.i % len(self.banks)]
        self.i += 1
        self.hold(b, sem, value)
        return b

    def in_turn(self):
        n = len(self.banks)
        return [self.banks[(self.i + j) % n] for j in range(n)]

    def leave_out(self, b):
        self.banks, self.i = [x for x in self.in_turn() if x != b], 0

    def put_back(self, b):
        self.banks, self.i = [b] + self.in_turn(), 0

    def hold(self, b, sem, value):
        if b in self.read_out:
            self.pe.wait_ge(*self.read_out[b])
        self.read_out[b] = (sem, value)


class Count:

    def __init__(self):
        self.n, self.reg, self.per = 0, 0, 0

    def next(self, step=1):
        self.n += step
        return self.value()

    def value(self):
        return self.n if self.per == 0 else self.n + self.reg * self.per

    def enter(self, reg, per):
        self.reg, self.per, self.start = reg, per, self.n

    def leave(self, rounds):
        assert self.n - self.start == self.per, (self.n - self.start, self.per)
        self.n = self.start + self.per * rounds
        self.per = 0


def program(nc, A, out):
    with ExitStack() as ctx:
        sems, named = [], {}

        def sem(name):
            sems.append(ctx.enter_context(nc.semaphore(name)))
            return sems[-1]

        def sbuf(name, shape, dt=F32, at=None):
            named[name] = named.get(name, 0) + 1
            name += f"_{named[name]}" if named[name] > 1 else ""
            return (at or ctx).enter_context(nc.sbuf_tensor(name, shape, dt))

        mod_stored = [sem(f"mod_stored{i}") for i in range(2)]
        row_landed = [sem(f"row_landed{i}") for i in range(RING)]
        row_landed2 = [sem(f"row_landed2_{i}") for i in range(RING2)]
        sems.clear()
        consts_loaded = sem("consts_loaded")
        inputs_loaded = sem("inputs_loaded")
        rows_loaded = sem("rows_loaded")
        late_rows_loaded = sem("late_rows_loaded")
        weights_loaded = [sem(f"weights_loaded{i}") for i in range(WS)]
        stored = sem("stored")
        groups_done = sem("groups_done")
        dve_step = sem("dve_step")
        act_step = sem("act_step")
        silu_ready = sem("silu_ready")
        mod_read = sem("mod_read")
        mod_bias_loaded = [sem(f"mod_bias_loaded{i}") for i in range(2)]
        stat_ready = sem("stat_ready")
        root_ready = sem("root_ready")
        norm_ready = sem("norm_ready")
        xT_ready = sem("xT_ready")
        cols_ready = sem("cols_ready")
        proj_ready = sem("proj_ready")
        conv_in_ready = sem("conv_in_ready")
        rot_ready = sem("rot_ready")
        qkT_ready = sem("qkT_ready")
        max_ready = sem("max_ready")
        probs_ready = sem("probs_ready")
        probsT_ready = sem("probsT_ready")
        ret_ready = sem("ret_ready")
        attn_ready = sem("attn_ready")
        conv_ready = sem("conv_ready")
        conv_read = sem("conv_read")
        pad_ready = sem("pad_ready")
        diag_ready = sem("diag_ready")
        keys_loaded = sem("keys_loaded")
        act_in_ready = sem("act_in_ready")
        act_out_ready = sem("act_out_ready")
        merged_ready = sem("merged_ready")
        catT_ready = sem("catT_ready")
        mix_read = sem("mix_read")
        h_ready = sem("h_ready")
        picksT_ready = sem("picksT_ready")
        keysT_ready = sem("keysT_ready")
        score_read = sem("score_read")
        up_loaded = [sem(f"up_loaded{i}") for i in range(2)]
        down_loaded = [sem(f"down_loaded{i}") for i in range(2)]
        up_read = sem("up_read")
        conv_done = sem("conv_done")
        gelu_done = sem("gelu_done")
        hidden_ready = sem("hidden_ready")
        picks_ready = sem("picks_ready")
        idx_copied = sem("idx_copied")
        gather_issued = sem("gather_issued")
        rows_used = sem("rows_used")
        dots_ready = sem("dots_ready")
        gelu_ready = sem("gelu_ready")
        coef_ready = sem("coef_ready")

        def phase_end():
            nc.all_engine_barrier(sems_to_clear=range(sems[0].num, sems[-1].num + 1))

        mod_dram = nc.dram_tensor("mod_dram", (L, 2, 6 * D), F32, kind="Internal").ap()
        rel_dram = nc.dram_tensor("rel_dram", (MOBA_H, 2 * S - 1), F32, kind="Internal")
        bias_dram = nc.dram_tensor("bias_dram", (P, MOBA_H * 3 * P), F32, kind="Internal").ap()

        cs_dram = nc.dram_tensor("cs_dram", (L, P, D), F32, kind="Internal").ap()
        cx_dram = nc.dram_tensor("cx_dram", (P, TT * D), F32, kind="Internal").ap()

        C = sbuf("C", [P, C_END])
        ident = C[:, C_ID:C_ID + P]
        flip = C[:, C_FLIP:C_FLIP + P]
        iota16 = C[:, C_IOTA:C_IOTA + TOPK]

        def angles(c0):
            return C[:, c0:c0 + TT * 32].rearrange("p (t o d) -> p t o d", t=TT, o=1)

        eps = sbuf("eps", [P, 2])
        X = sbuf("X", [P, TT, D])
        W = sbuf("W", [P, WS, WCOL])
        XT = sbuf("XT", [P, DK, S])
        CT = sbuf("CT", [P, DK, S])
        ROWS = sbuf("ROWS", [P, RING, D])
        H = sbuf("H", [P, TT, D])
        ACC = sbuf("ACC", [P, TT, D])
        PROD = sbuf("PROD", [P, D])
        IDX = sbuf("IDX", [P, TT, PICKS], I32)
        IDXS = sbuf("IDXS", [P, 2, RING2], I32)
        WGT = sbuf("WGT", [P, TT, PICKS])
        DOT = sbuf("DOT", [P, TT, PICKS])
        DOTS = sbuf("DOTS", [P, RING2])
        SC = sbuf("SC", [P, 16])
        ONE = sbuf("ONE", [1, 2])
        MODB = XT[:].rearrange("p k s -> p (k s)")[0:1, 0:1024].rearrange("p (i n) -> p i n", i=2)
        MODS = XT[:].rearrange("p k s -> p (k s)")[0:2, 1024:2048].rearrange("p (i n) -> p i n", i=2)
        COEF = sbuf("COEF", [P, TT, PICKS])
        BASE = sbuf("BASE", [P, 1])
        KTC = sbuf("KTC", [P, L, KVH, S])
        VC = sbuf("VC", [P, L, TT, KVW])
        st = sbuf("st", [P, 2, 20])
        rt = sbuf("rt", [P, 2, 20])
        ri = sbuf("ri", [P, 2, 20])
        PS = ctx.enter_context(nc.psum_tensor("PS", [P, 8, 512], F32))

        x_dram = A["x"].rearrange("o (t p) d -> p (o t) d", p=P)
        ctx_dram = A["ctx_2"].rearrange("o (t p) d -> p (o t) d", p=P)
        out_dram = out.rearrange("o (t p) d -> p (o t) d", p=P)
        tables = {n: A[n].rearrange("l n d -> (l n) d") for n in ("peer_u_2", "peer_v_2")}

        def wview(name, l):
            return A[name].rearrange("l (k p) n -> l p k n", p=P)[l]

        def wslot(s, k, n):
            return W[:, s, 0:k * n].rearrange("p (k n) -> p k n", k=k)

        def dve_chain(dve):
            count = Count()

            def link(ins):
                ins.then_inc(dve_step, 1)
                dve.wait_ge(dve_step, count.next())

            link.count = count
            return link


        def transposes(pe, banks, groups, name, src, n_k, sem_, base, width=P):
            for j in range(0, n_k, 2):
                b = banks.take(sem_, base + j // 2 + 1)
                for k in range(j, min(j + 2, n_k)):
                    for t in range(TT):
                        o = ((k - j) * TT + t) * P
                        ins = nc.tensor.transpose(PS[:, b, o:o + P], src(t, k), ident)
                ins.then_inc(groups_done, groups.mark(name, j // 2))
                groups.at[name, j // 2, "bank"] = b

        def matmul_rows(pe, b, cols, lhs, rhs, n_k, start=True, stop=True):
            for k in range(n_k):
                ins = nc.tensor.matmul(PS[:, b, cols[0]:cols[1]], lhs(k), rhs(k),
                                       start=start and k == 0, stop=stop and k == n_k - 1)
            return ins

        def weights_in(pe, chunk):
            pe.wait_ge(weights_loaded[chunk % WS], 16 * (chunk // WS + 1))

        BESIDE = (lambda k: ROWS[:, k, :], row_landed, RING)
        ALONE = (lambda k: W[:, k // 4, (k % 4) * D:(k % 4 + 1) * D], row_landed2, RING2)

        def gather_rows(pool, ring, table, src, n0, n=PICKS):
            slot, landed, size = ring
            with pool.Fori(0, n // (2 * size)) as e:
                for half in range(2):
                    pool.wait_ge(rows_used, e * 2 * size + n0 + half * size + 1)
                    nc.gpsimd.tensor_copy(IDXS[:, half, 0:size], src(e * 2 + half)).then_inc(idx_copied, 1)
                    for k in range(size):
                        pool.wait_ge(rows_used, e * 2 * size + n0 + half * size + k + 1)
                        pool.sem_inc(gather_issued, 1)
                        if k == 0:
                            pool.wait_ge(idx_copied, e * 2 + n0 // size + half + 1)
                            pool.sem_inc(gather_issued, 1)
                        nc.gpsimd.indirect_dma_start(
                            slot(k), None, tables[table], bass.IndirectOffsetOnAxis(IDXS[:, half, k:k + 1], 0),
                        ).then_inc(landed[k], 16)

        def dot_step(dve, ring, h, k, n, before):
            slot, landed, size = ring
            dve.wait_ge(landed[k], (n + before) * 16 + 16)
            nc.vector.tensor_tensor_reduce(slot(k), slot(k), h, 1.0, 0.0, ALU.mult, ALU.add,
                                           DOTS[:, k:k + 1]).then_inc(rows_used, 1)

        def dots_out(dve, ring, dots, n, link):
            size = ring[2]
            dve.wait_ge(rows_used, n * size + 2 * size)
            link(nc.vector.tensor_copy(dots, DOTS[:, 0:size]))

        def dot_round(dve, ring, h, dots, n, before, link):
            for k in range(ring[2]):
                dot_step(dve, ring, h, k, n, before)
            dots_out(dve, ring, dots, n, link)

        def sum_round(dve, ring, acc, coef, n, before):
            slot, landed, size = ring
            for k in range(size):
                dve.wait_ge(landed[k], (n + before) * 16 + 16)
                dve.wait_ge(rows_used, n * size + size + k)
                nc.vector.scalar_tensor_tensor(acc, slot(k), coef(k), acc, ALU.mult, ALU.add).then_inc(rows_used, 1)

        NPIECE = 6 * D // 512

        def mod_sp(sp, l, w0, slot_used, xt_used=None):
            for i in range(NPIECE):
                c = w0 + i
                if c >= WS:
                    sp.wait_ge(groups_done, slot_used(c))
                cols = slice(i * 512, (i + 1) * 512)
                sp.dma_start(wslot(c % WS, DK, 512), wview("w_mod_2", l)[:, :, cols]).then_inc(weights_loaded[c % WS], 16)
                if i == 0 and xt_used:
                    sp.wait_ge(groups_done, xt_used())
                if i >= 2:
                    sp.wait_ge(mod_read, i - 1)
                sp.dma_start(MODB[:, i % 2, :], A["b_mod_2"][l:l + 1, cols]).then_inc(mod_bias_loaded[i % 2], 16)

        def mod_pe(pe, banks, groups, w0):
            for i in range(NPIECE):
                c = w0 + i
                weights_in(pe, c)
                pe.wait_ge(mod_bias_loaded[i % 2], 16 * (i // 2 + 1))
                b = banks.take(mod_read, i + 1)
                for k in range(DK):
                    nc.tensor.matmul(PS[0:2, b, :], SC[:, k:k + 9:8], wslot(c % WS, DK, 512)[:, k, :],
                                     start=(k == 0), stop=False)
                nc.tensor.matmul(PS[0:2, b, :], ONE[:], MODB[:, i % 2, :], start=False, stop=True
                                 ).then_inc(groups_done, groups.mark("mod", i))
                groups.at["mod", i, "bank"] = b

        def mod_act(act, groups, stored_before):
            for i in range(NPIECE):
                act.wait_ge(groups_done, groups.of("mod", i))
                if i >= 2:
                    act.wait_ge(mod_stored[i % 2], 16 * (i // 2) + stored_before)
                nc.scalar.copy(MODS[:, i % 2, :], PS[0:2, groups.at["mod", i, "bank"], :]).then_inc(mod_read, 1)

        def mod_pool(pool, l, stored_before):
            for i in range(NPIECE):
                pool.wait_ge(mod_read, i + 1)
                pool.dma_start(mod_dram[l, :, i * 512:(i + 1) * 512], MODS[:, i % 2, :]).then_inc(mod_stored[i % 2], 16)
            for i in range(2):
                pool.wait_ge(mod_stored[i], 16 * (NPIECE // 2) + stored_before)

        with ExitStack() as ph:
            SCR = sbuf("SCR", [16, P], at=ph)
            SCS = sbuf("SCS", [16, P], at=ph)
            REL = sbuf("REL", [REL_BUCKETS + 1, MOBA_H], at=ph)
            BUCK = sbuf("BUCK", [REL_BUCKETS + 1, 2 * S - 1], at=ph)
            RELT = sbuf("RELT", [MOBA_H, 2 * S - 1], at=ph)
            HANK = sbuf("HANK", [P, MOBA_H, 3 * P], at=ph)
            BIAS = sbuf("BIASS", [P, MOBA_H, 3 * P], at=ph)
            with nc.Block() as block:
                groups = Groups()

                @block.tensor
                def _(pe):
                    banks = Banks(pe, list(range(8)))
                    pe.wait_ge(consts_loaded, 16)
                    pe.wait_ge(silu_ready, 1)
                    b = banks.take(cols_ready, 1)
                    nc.tensor.transpose(PS[:, b, 0:16], SCS[:], ident[0:16, 0:16]).then_inc(
                        groups_done, groups.mark("sc"))
                    pe.wait_ge(inputs_loaded, 4 * 16)
                    pe.wait_ge(dve_step, 3)
                    b = banks.take(act_step, 1)
                    nc.tensor.matmul(PS[0:MOBA_H, b, 0:2 * S - 1], REL[:], BUCK[:], start=True,
                                     stop=True).then_inc(groups_done, groups.mark("rel"))
                    pe.wait_ge(cols_ready, 1)
                    mod_pe(pe, banks, groups, 0)
                    pe.wait_ge(late_rows_loaded, 12 * 16)
                    for h in range(MOBA_H):
                        b = banks.take(score_read, h + 1)
                        nc.tensor.matmul(PS[:, b, 0:3 * P], flip, HANK[:, h, :], start=True,
                                         stop=True).then_inc(groups_done, groups.mark("bias", h))
                        groups.at["bias", h, "bank"] = b

                @block.sync
                def _(sp):
                    sp.dma_start(SCR[0:8, :], A["c_2"].rearrange("o (k p) -> (o k) p", p=P)).then_inc(inputs_loaded, 16)
                    sp.dma_start(SCR[8:16, :], A["c_ctx_2"].rearrange("(k p) -> k p", p=P)).then_inc(inputs_loaded, 16)
                    sp.dma_start(C[:], A["consts"]).then_inc(consts_loaded, 16)
                    sp.dma_start(REL[0:REL_BUCKETS, :], A["rel_bias"]).then_inc(inputs_loaded, 16)
                    sp.dma_start(BUCK[:], A["buckets"]).then_inc(inputs_loaded, 16)
                    sp.dma_start(X[:], x_dram).then_inc(rows_loaded, 16)
                    mod_sp(sp, 0, 0, lambda c: groups.of("mod", c - WS))
                    sp.wait_ge(rows_loaded, 16)

                @block.scalar
                def _(act):
                    act.wait_ge(inputs_loaded, 4 * 16)
                    nc.scalar.activation(SCS[:], SCR[:], ACT.Silu).then_inc(silu_ready, 1)
                    act.wait_ge(groups_done, groups.of("rel"))
                    nc.scalar.copy(RELT[:], PS[0:MOBA_H, 1, 0:2 * S - 1]).then_inc(act_step, 1)
                    act.wait_ge(act_step, 1)
                    act.dma_start(rel_dram.ap(), RELT[:]).then_inc(stored, 16)
                    act.wait_ge(stored, 16)
                    for h in range(MOBA_H):
                        for first, n, o in ((P, P, 0), (0, 2 * P, P)):
                            src = bass.AP(rel_dram, h * (2 * S - 1) + first, [[1, P], [1, n]])
                            act.dma_start(HANK[:, h, o:o + n], src).then_inc(late_rows_loaded, 16)
                    mod_act(act, groups, 0)
                    for h in range(MOBA_H):
                        act.wait_ge(groups_done, groups.of("bias", h))
                        nc.scalar.copy(BIAS[:, h, :], PS[:, groups.at["bias", h, "bank"], 0:3 * P]).then_inc(score_read, 1)
                    act.wait_ge(score_read, MOBA_H)
                    act.dma_start(bias_dram, BIAS[:].rearrange("p h n -> p (h n)")).then_inc(stored, 16)
                    act.wait_ge(stored, 32)

                @block.vector
                def _(dve):
                    link = dve_chain(dve)
                    link(nc.vector.memset(ONE[:], 1.0))
                    link(nc.vector.memset(REL[REL_BUCKETS:REL_BUCKETS + 1, :], 1.0))
                    link(nc.vector.memset(eps[:, 0:1], LN_EPS))
                    nc.vector.memset(eps[:, 1:2], RMS_EPS)
                    nc.vector.memset(BASE[:], 0.0)
                    dve.wait_ge(groups_done, groups.of("sc"))
                    nc.vector.tensor_copy(SC[:], PS[:, 0, 0:16]).then_inc(cols_ready, 1)

                @block.gpsimd
                def _(pool):
                    mod_pool(pool, 0, 0)
            phase_end()


        def stream_buffers(ph, latent):
            B = {}
            B["PROJ"] = sbuf("PROJ2", [P, TT, QKV2], at=ph)
            B["QR"] = sbuf("QR", [P, TT, QW + 2 * KVW], at=ph)
            B["T1"] = PROD[:, 0:TT * 320].rearrange("p (t n) -> p t n", t=TT)
            B["T2"] = sbuf("T2", [P, TT, 10 * 32], at=ph)
            B["QT"] = sbuf("QT", [P, QH // 2, S], at=ph)
            B["KT"] = sbuf("KT", [P, KVH, 2 * S], at=ph)
            B["V"] = sbuf("V", [P, 2 * TT, KVW], at=ph)
            B["GAIN"] = sbuf("GAIN", [P, 2, HD], at=ph)
            B["COLR"] = sbuf("COLR", [TAPS2 + 3, CW2], at=ph)
            B["COLC"] = sbuf("COLC", [P, CW2 // P, TAPS2 + 3], at=ph)
            B["MODR"] = sbuf("MODR", [16, P], at=ph)
            B["MODC"] = sbuf("MODC", [P, 16], at=ph)
            B["LNR"] = sbuf("LNR", [P, 2, CW2], at=ph)
            B["ROW"] = [ACC[:, 0, :], ACC[:, 1, :], sbuf("ROW", [P, D], at=ph)[:]]
            AR = ROWS[:].rearrange("p k d -> p (k d)")
            B["U"] = AR[:, 0:2048].rearrange("p (j s) -> p j s", j=8)
            B["PAD"] = AR[:, 2048:2048 + 4 * (S + 2 * HALO)].rearrange("p (j s) -> p j s", j=4)
            B["PR"] = AR[:, 4096:5120].rearrange("p (i n) -> p i n", i=2)
            B["PT"] = AR[:, 5120:6144].rearrange("p (i n) -> p i n", i=2)
            B["O"] = AR[:, 6144:7168].rearrange("p (t n) -> p t n", t=TT)
            B["Y"] = AR[:, 7168:8192].rearrange("p (t n) -> p t n", t=TT)
            B["SC"] = [AR[:, 0:2048], AR[:, 2048:4096]]
            B["CAND"] = B["HOT"] = AR[:, 4096:6144]
            B["QPT"] = AR[:, 6144:8192].rearrange("p (t h s) -> p t h s", t=TT, h=EH)
            B["KPT"] = B["QR"][:].rearrange("p t n -> p (t n)")[:, 0:1024].rearrange("p (h k) -> p h k", h=EH)
            B["KEYS"] = B["PROJ"][:].rearrange("p t n -> p (t n)")[:, 0:1024]
            B["TV"] = sbuf("TV", [P, 2 * EH, TOPK], at=ph)
            B["TI"] = sbuf("TI", [P, 2 * EH, TOPK], U32, at=ph)
            B["TF"] = sbuf("TF", [P, 2 * EH, TOPK], at=ph)
            B["BV"] = sbuf("BV", [P, EH, TOPK], at=ph)
            B["BJ"] = sbuf("BJ", [P, EH, TOPK], U32, at=ph)
            B["J"] = sbuf("J", [P, 2, PICKS], U32, at=ph)
            B["JF"] = sbuf("JF", [P, 2, PICKS], at=ph)
            B["EI"] = sbuf("EI", [P, 2 + TT, PICKS], at=ph)
            B["SUM"] = sbuf("SUM", [P, 2, TT * QH], at=ph)
            B["NMAX"] = sbuf("NMAX", [P, TT * QH], at=ph)
            B["BN"] = sbuf("BN", [P, TT, 8], at=ph)
            return B

        CHUNKS2 = [("w_in_2", 0, 512), ("w_in_2", 512, 256), ("w_in_2", 768, 512), ("w_in_2", 1280, 512),
                   ("w_o_2", 0, 512), ("w_o_2", 512, 512), ("peer_wq_2", 0, 512), ("peer_wq_2", 512, 512)]

        CONV_STEP = 12

        def stream_pe(pe, groups, B, latent):
            banks = Banks(pe, [0, 1, 2, 3, 4, 5])
            nk = 2 * S if latent else S
            pe.wait_ge(rows_loaded, 16 * 5)
            b = banks.take(cols_ready, 1)
            for j in range(CW2 // P):
                nc.tensor.transpose(PS[:, b, j * 34:j * 34 + 34], B["COLR"][:, j * P:(j + 1) * P], ident[0:34, 0:34])
            nc.tensor.transpose(PS[:, b, 136:152], B["MODR"][:], ident[0:16, 0:16]).then_inc(
                groups_done, groups.mark("cols"))
            pe.wait_ge(norm_ready, TT)
            transposes(pe, banks, groups, "xT", lambda t, k: CT_tok(B)[:, t, k * P:(k + 1) * P], DK, xT_ready, 0)
            pe.wait_ge(xT_ready, 4)
            for c, (o, n) in enumerate(((0, 512), (512, 256))):
                weights_in(pe, c)
                for t in range(TT):
                    b = banks.take(proj_ready, c * TT + t + 1)
                    matmul_rows(pe, b, (0, n), lambda k: XT[:, k, t * P:(t + 1) * P],
                                lambda k: wslot(c, DK, n)[:, k, :], DK).then_inc(
                        groups_done, groups.mark("proj", c, t))
                    groups.at["proj", c, t, "bank"] = b
            for j in range(8):
                c = 2 + j // 4
                if j % 4 == 0:
                    weights_in(pe, c)
                b = banks.take(conv_in_ready, j + 1)
                matmul_rows(pe, b, (0, S), lambda k: wslot(c, DK, 512)[:, k, (j % 4) * P:(j % 4 + 1) * P],
                            lambda k: XT[:, k, :], DK).then_inc(groups_done, groups.mark("u", j))
                groups.at["u", j, "bank"] = b
            pe.wait_ge(rot_ready, 1)
            transposes(pe, banks, groups, "qk", lambda t, k: B["QR"][:, t, k * P:(k + 1) * P], 6, qkT_ready, 0)
            pe.wait_ge(qkT_ready, 3)
            n = TT * QH
            nb = nk // P
            banks.leave_out(5)
            banks.hold(5, conv_ready, 2)
            for i in range(n + 3):
                if i < n:
                    t, h = divmod(i, QH)
                    q0 = HD * (h % 2)
                    b = banks.take(probs_ready, i + 1)
                    nc.tensor.matmul(PS[:, b, 0:nk], B["QT"][q0:q0 + HD, h // 2, t * P:(t + 1) * P],
                                     B["KT"][q0:q0 + HD, h // (QH // KVH), 0:nk], start=True, stop=True
                                     ).then_inc(groups_done, groups.mark("score", i))
                    groups.at["score", i, "bank"] = b
                for k in range(3 * i, min(3 * i + 3, TAPS2)):
                    pe.wait_ge(diag_ready, k + 1)
                    if k == 0:
                        pe.wait_ge(pad_ready, 1)
                    ins = nc.tensor.matmul(PS[:, 5, 0:S], diag(k), B["PAD"][:, 3, k:k + S], start=k == 0, stop=k == TAPS2 - 1)
                    if k == TAPS2 - 1:
                        ins.then_inc(groups_done, groups.mark("conv"))
                if i == CONV_STEP:
                    pe.wait_ge(conv_ready, 2)
                    banks.put_back(5)
                    for t in range(TT):
                        b = banks.take(conv_read, t + 1)
                        for j in range(CW2 // P):
                            ins = nc.tensor.transpose(PS[:, b, j * P:(j + 1) * P], B["U"][:, j, t * P:(t + 1) * P], ident)
                        ins.then_inc(groups_done, groups.mark("convT", t))
                        groups.at["convT", t, "bank"] = b
                if 2 <= i < n + 2:
                    j = i - 2
                    pe.wait_ge(probs_ready, j + 1)
                    b = banks.take(probsT_ready, j + 1)
                    for kb in range(nb):
                        ins = nc.tensor.transpose(PS[:, b, kb * P:(kb + 1) * P], B["PR"][:, j % 2, kb * P:(kb + 1) * P], ident)
                    ins.then_inc(groups_done, groups.mark("pT", j))
                    groups.at["pT", j, "bank"] = b
                if i >= 3:
                    j = i - 3
                    t, h = divmod(j, QH)
                    pe.wait_ge(probsT_ready, j + 1)
                    kv = h // (QH // KVH)
                    for kb in range(nb):
                        ins = nc.tensor.matmul(PS[:, 6 + t, h * HD:(h + 1) * HD], B["PT"][:, j % 2, kb * P:(kb + 1) * P],
                                               B["V"][:, kb, kv * HD:(kv + 1) * HD], start=(kb == 0), stop=(kb == nb - 1))
                    ins.then_inc(groups_done, groups.mark("pv", j))
            pe.wait_ge(late_rows_loaded, 16 * 2)
            for g in range(2):
                b = banks.take(keysT_ready, g + 1)
                for h in range(4):
                    o = (g * 4 + h) * P
                    ins = nc.tensor.transpose(PS[:, b, h * P:(h + 1) * P], B["KEYS"][:, o:o + P], ident)
                ins.then_inc(groups_done, groups.mark("keys", g))
                groups.at["keys", g, "bank"] = b
            pe.wait_ge(merged_ready, 1)
            transposes(pe, banks, groups, "yT", lambda t, k: B["Y"][:, t, k * P:(k + 1) * P], 4, catT_ready, 0)
            pe.wait_ge(catT_ready, 2)
            for half in range(2):
                for t in range(TT):
                    for c in range(2):
                        if half == 0:
                            if t == 0:
                                weights_in(pe, 4 + c)
                            groups.at["mix", c, t, "bank"] = banks.take(mix_read, t * 2 + c + 1)
                        k0 = 4 * (1 - half)
                        ins = matmul_rows(pe, groups.at["mix", c, t, "bank"], (0, 512), lambda k: CT[:, k0 + k, t * P:(t + 1) * P],
                                          lambda k: wslot(c, DK, 512)[:, k0 + k, :], 4, start=half == 0, stop=half == 1)
                        if half == 1:
                            ins.then_inc(groups_done, groups.mark("mix", c, t))
                if half == 0:
                    pe.wait_ge(merged_ready, 2)
                    transposes(pe, banks, groups, "oT", lambda t, k: B["O"][:, t, k * P:(k + 1) * P], 4, catT_ready, 2)
                    pe.wait_ge(catT_ready, 4)
            for t in range(TT):
                pe.wait_ge(h_ready, t + 1)
                for j in range(2):
                    b = banks.take(xT_ready, 4 + t * 2 + j + 1)
                    for k in range(4):
                        o = (4 * j + k) * P
                        ins = nc.tensor.transpose(PS[:, b, k * P:(k + 1) * P], H[:, t, o:o + P], ident)
                    ins.then_inc(groups_done, groups.mark("hT", t, j))
                    groups.at["hT", t, j, "bank"] = b
                pe.wait_ge(xT_ready, 4 + t * 2 + 2)
                for j in range(2):
                    if t == 0:
                        weights_in(pe, 6 + j)
                    b = banks.take(picksT_ready, t * 2 + j + 1)
                    for h in range(4):
                        ins = matmul_rows(pe, b, (h * P, (h + 1) * P), lambda k: wslot(2 + j, DK, 512)[:, k, h * P:(h + 1) * P],
                                          lambda k: XT[:, k, t * P:(t + 1) * P], DK)
                    ins.then_inc(groups_done, groups.mark("pq", t, j))
                    groups.at["pq", t, j, "bank"] = b
                if t == 0:
                    pe.wait_ge(keysT_ready, 2)
                for g in range(4):
                    b = banks.take(score_read, t * 4 + g + 1)
                    for i in range(4):
                        h, c = (g // 2) * 4 + i, g % 2
                        if i == 0:
                            pe.wait_ge(picksT_ready, t * 2 + g // 2 + 1)
                        ins = nc.tensor.matmul(PS[:, b, i * P:(i + 1) * P], B["QPT"][c * HD:(c + 1) * HD, t, h, :],
                                               B["KPT"][c * HD:(c + 1) * HD, h, :], start=True, stop=True)
                    ins.then_inc(groups_done, groups.mark("ps", t, g))
                    groups.at["ps", t, g, "bank"] = b
            return banks

        def CT_tok(B):
            return CT[:].rearrange("p k s -> p (k s)").rearrange("p (t d) -> p t d", t=TT)

        def stream_sp(sp, groups, B, l, who):
            m = mod_dram[l][who:who + 1]
            sp.dma_start(B["MODR"][:], m[:, 0:2 * D].rearrange("o (k p) -> (o k) p", p=P)).then_inc(rows_loaded, 16)
            sp.dma_start(B["COLR"][0:TAPS2, :], A["conv_w_2"][l]).then_inc(rows_loaded, 16)
            for i, name in enumerate(("conv_b_2", "beta_attn_2", "beta_conv_2")):
                sp.dma_start(B["COLR"][TAPS2 + i:TAPS2 + i + 1, :], A[name].rearrange("(o l) n -> l o n", o=1)[l]
                             ).then_inc(rows_loaded, 16)
            for c in range(4):
                name, o, n = CHUNKS2[c]
                sp.dma_start(wslot(c, DK, n), wview(name, l)[:, :, o:o + n]).then_inc(weights_loaded[c], 16)
            for i, name in enumerate(("q_gain_2", "k_gain_2")):
                sp.dma_start(B["GAIN"][:, i, :], A[name].rearrange("(o l) n -> l o n", o=1)[l].to_broadcast([P, HD])
                             ).then_inc(inputs_loaded, 16)
            for i, name in enumerate(("ln_g_2", "ln_b_2")):
                sp.dma_start(B["LNR"][:, i, :], A[name].rearrange("(o l) n -> l o n", o=1)[l].to_broadcast([P, CW2])
                             ).then_inc(inputs_loaded, 16)
            for i in range(3):
                sp.dma_start(B["ROW"][i], m[:, (2 + i) * D:(3 + i) * D].to_broadcast([P, D])).then_inc(inputs_loaded, 16)
            for c in range(4, 8):
                name, o, n = CHUNKS2[c]
                last = {4: ("proj", 0, 1), 5: ("proj", 1, 1), 6: ("u", 3), 7: ("u", 7)}[c]
                sp.wait_ge(groups_done, groups.of(*last))
                sp.dma_start(wslot(c % WS, DK, n), wview(name, l)[:, :, o:o + n]).then_inc(weights_loaded[c % WS], 16)
            sp.wait_ge(rot_ready, 1)
            for c in range(2):
                sp.dma_start(B["KEYS"].rearrange("p (h c d) -> p h c d", h=EH, c=2)[:, :, c, :],
                             A["peer_keys_2"][l][:, c].rearrange("h k d -> k h d")).then_inc(late_rows_loaded, 16)

        def root(act, n, i, scale, e):
            act.wait_ge(stat_ready, i + 1)
            nc.scalar.activation(rt[:, i % 2, 0:n], st[:, i % 2, 0:n], ACT.Sqrt, bias=eps[:, e:e + 1],
                                 scale=scale).then_inc(root_ready, 1)

        def stream_act(act, groups, B, l, latent):
            nk = 2 * S if latent else S

            def bank(*name):
                act.wait_ge(groups_done, groups.of(*name))
                return groups.at[name + ("bank",)]

            root(act, TT, 0, 1.0 / D, 1)
            act.wait_ge(cols_ready, 1)
            for j in range(DK // 2):
                b = bank("xT", j)
                for k in range(2):
                    ins = nc.scalar.activation(XT[:, 2 * j + k, :], PS[:, b, k * S:(k + 1) * S], ACT.Identity,
                                               bias=B["MODC"][:, 2 * j + k:2 * j + k + 1],
                                               scale=B["MODC"][:, 8 + 2 * j + k:9 + 2 * j + k])
                ins.then_inc(xT_ready, 1)
            for c, (o, n) in enumerate(((0, 512), (512, 256))):
                for t in range(TT):
                    b = bank("proj", c, t)
                    nc.scalar.copy(B["PROJ"][:, t, o:o + n], PS[:, b, 0:n]).then_inc(proj_ready, 1)
            for j in range(8):
                if j == 2:
                    root(act, TT * 10, 1, 1.0 / HD, 1)
                b = bank("u", j)
                nc.scalar.activation(B["U"][:, j, :], PS[:, b, 0:S], ACT.Identity if j < 4 else ACT.Sigmoid
                                     ).then_inc(conv_in_ready, 1)
            for j in range(3):
                b = bank("qk", j)
                if j < 2:
                    nc.scalar.copy(B["QT"][:, 2 * j:2 * j + 2, :].rearrange("p k s -> p (k s)"), PS[:, b, :]
                                   ).then_inc(qkT_ready, 1)
                else:
                    nc.scalar.copy(B["KT"][:, :, nk - S:nk], PS[:, b, :].rearrange("p (k s) -> p k s", k=KVH)
                                   ).then_inc(qkT_ready, 1)
            n = TT * QH
            for i in range(n + 2):
                if i == CONV_STEP - 1:
                    act.wait_ge(groups_done, groups.of("conv"))
                    nc.scalar.activation(B["U"][:, 3, :], PS[:, 5, 0:S], ACT.Identity, bias=B["COLC"][:, 3, TAPS2:TAPS2 + 1]).then_inc(conv_ready, 1)
                if i == CONV_STEP + 1:
                    root(act, TT, 2, 1.0, 0)
                if i == n:
                    act.wait_ge(act_in_ready, 1)
                    nc.scalar.activation(B["Y"], B["Y"], ACT.Silu).then_inc(act_out_ready, 1)
                if i < n:
                    act.wait_ge(max_ready, i + 1)
                    if i >= 2:
                        act.wait_ge(groups_done, groups.of("pT", i - 2))
                    nc.scalar.activation(B["PR"][:, i % 2, 0:nk], PS[:, groups.at["score", i, "bank"], 0:nk], ACT.Exp,
                                         bias=B["NMAX"][:, i:i + 1], accum_out=B["SUM"][:, 0, i:i + 1]
                                         ).then_inc(probs_ready, 1)
                if i >= 2:
                    j = i - 2
                    b = bank("pT", j)
                    if j >= 2:
                        act.wait_ge(groups_done, groups.of("pv", j - 2))
                    nc.scalar.copy(B["PT"][:, j % 2, 0:nk], PS[:, b, 0:nk]).then_inc(probsT_ready, 1)
            for g in range(2):
                b = bank("keys", g)
                nc.scalar.copy(B["KPT"][:, 4 * g:4 * g + 4, :].rearrange("p h k -> p (h k)"), PS[:, b, :]
                               ).then_inc(keysT_ready, 1)
            root(act, TT, 3, 1.0 / CW2, 1)
            root(act, TT, 4, 1.0 / QW, 1)
            for name, k0, beta in (("yT", 4, TAPS2 + 2), ("oT", 0, TAPS2 + 1)):
                for j in range(2):
                    b = bank(name, j)
                    for k in range(2 * j, 2 * j + 2):
                        ins = nc.scalar.activation(CT[:, k0 + k, :], PS[:, b, (k % 2) * S:(k % 2 + 1) * S], ACT.Copy,
                                                   scale=B["COLC"][:, k, beta:beta + 1])
                    ins.then_inc(catT_ready, 1)
            root(act, 1, 5, 1.0 / D, 1)
            for t in range(TT):
                for j in range(2):
                    b = bank("hT", t, j)
                    nc.scalar.copy(XT[:, 4 * j:4 * j + 4, t * P:(t + 1) * P], PS[:, b, :].rearrange("p (k s) -> p k s", k=4)
                                   ).then_inc(xT_ready, 1)
                if t == 0:
                    root(act, 1, 6, 1.0 / D, 1)
                for j in range(2):
                    b = bank("pq", t, j)
                    nc.scalar.copy(B["QPT"][:, t, 4 * j:4 * j + 4, :].rearrange("p h s -> p (h s)"), PS[:, b, :]
                                   ).then_inc(picksT_ready, 1)
                for g in range(4):
                    b = bank("ps", t, g)
                    dst = B["SC"][t].rearrange("p (h c k) -> p h c k", c=2, k=EK)[:, (g // 2) * 4:(g // 2) * 4 + 4, g % 2, :]
                    nc.scalar.copy(dst, PS[:, b, :].rearrange("p (h k) -> p h k", h=4)).then_inc(score_read, 1)

        def softmax_act(act, B, t):
            act.wait_ge(act_in_ready, 2 + t)
            nc.scalar.activation(B["EI"][:, 2 + t, :], B["EI"][:, 2 + t, :], ACT.Exp).then_inc(act_out_ready, 1)

        def diag(k):
            side = (CT if k < 16 else XT)[:].rearrange("p k s -> p (k s)")
            return side[:, (k % 16) * P:(k % 16 + 1) * P]

        def stream_pool(pool, groups, B):
            pool.wait_ge(cols_ready, 1)
            for k in range(TAPS2):
                if k in (0, 16):
                    pool.wait_ge(groups_done, groups.of(*{0: ("xT", DK // 2 - 1), 16: ("u", 7)}[k]))
                nc.gpsimd.tensor_scalar(diag(k), ident, B["COLC"][:, 3, k:k + 1], None, ALU.mult).then_inc(diag_ready, 1)

        def stream_dve(dve, link, groups, B, SRC, l, latent):
            cur = {"stat": 0}

            def statistic(ins):
                ins.then_inc(stat_ready, 1)
                cur["stat"] += 1

            def inverse(i, n):
                dve.wait_ge(root_ready, i + 1)
                link(nc.vector.reciprocal(ri[:, i % 2, 0:n], rt[:, i % 2, 0:n]))
                return ri[:, i % 2]

            def inverse_root(n, ins):
                statistic(ins)
                return inverse(cur["stat"] - 1, n)

            def sum_squares(src, width, n=TT):
                i = cur["stat"] % 2
                for t in range(n):
                    ins = nc.vector.tensor_tensor_reduce(PROD[:, 0:width], src(t), src(t), 1.0, 0.0, ALU.mult,
                                                         ALU.add, st[:, i, t:t + 1])
                    if t < n - 1:
                        link(ins)
                return ins

            r = inverse_root(TT, sum_squares(lambda t: SRC[:, t, :], D))
            for t in range(TT):
                nc.vector.tensor_scalar(CT_tok(B)[:, t, :], SRC[:, t, :], r[:, t:t + 1], None, ALU.mult).then_inc(norm_ready, 1)
            dve.wait_ge(groups_done, groups.of("cols"))
            nc.vector.tensor_copy(B["MODC"][:, 0:8], PS[:, 0, 136:144])
            nc.vector.tensor_scalar(B["MODC"][:, 8:16], PS[:, 0, 144:152], 1.0, None, ALU.add)
            nc.vector.tensor_copy(B["COLC"][:].rearrange("p j n -> p (j n)"), PS[:, 0, 0:136]).then_inc(cols_ready, 1)
            dve.wait_ge(inputs_loaded, 16 * 7)
            link(nc.vector.tensor_scalar(B["ROW"][2], B["ROW"][2], 1.0, None, ALU.add))
            link(nc.vector.tensor_scalar(B["GAIN"][:, 0, :], B["GAIN"][:, 0, :], HD ** -0.5, None, ALU.mult))
            nc.vector.memset(B["PAD"][:, :, 0:HALO], 0.0)
            link(nc.vector.memset(B["PAD"][:, :, HALO + S:S + 2 * HALO], 0.0))
            dve.wait_ge(proj_ready, 4)
            q = B["PROJ"][:, :, 0:640].rearrange("p t (h d) -> p t h d", h=10)
            sq = B["QR"][:, :, 0:640].rearrange("p t (h d) -> p t h d", h=10)
            link(nc.vector.tensor_tensor(sq, q, q, ALU.mult))
            r = inverse_root(TT * 10, nc.vector.tensor_reduce(st[:, 1, :].rearrange("p (t h) -> p t h", t=TT), sq, AX, ALU.add))
            link(nc.vector.tensor_tensor(q, q, r[:, 0:TT * 10].rearrange("p (t h o) -> p t h o", t=TT, o=1).to_broadcast([P, TT, 10, HD]), ALU.mult))
            for i, (a, b) in enumerate(((0, 8), (8, 10))):
                gain = B["GAIN"][:, i:i + 1, :].rearrange("p (t h) d -> p t h d", t=1)
                ins = nc.vector.tensor_tensor(q[:, :, a:b, :], q[:, :, a:b, :], gain.to_broadcast([P, TT, b - a, HD]), ALU.mult)
            link(ins)
            kdst = B["QR"][:, :, QW:].rearrange("p t (h c d) -> p t h c d", h=KVH, c=2)
            if latent:
                cos, sin = angles(C_COS2), angles(C_SIN2)
                for a, b in ((0, 8), (8, 10)):
                    src = B["PROJ"][:, :, a * HD:b * HD].rearrange("p t (h d) -> p t h d", h=b - a)
                    q1, q2 = src[:, :, :, 0:32], src[:, :, :, 32:64]
                    n = b - a
                    t1 = B["T1"][:, :, 0:n * 32].rearrange("p t (h d) -> p t h d", h=n)
                    t2 = B["T2"][:, :, 0:n * 32].rearrange("p t (h d) -> p t h d", h=n)
                    cb, sb_ = cos.to_broadcast([P, TT, n, 32]), sin.to_broadcast([P, TT, n, 32])
                    for half, (f1, f2, op) in enumerate(((cb, sb_, ALU.subtract), (sb_, cb, ALU.add))):
                        nc.vector.tensor_tensor(t1, q1, f1, ALU.mult)
                        link(nc.vector.tensor_tensor(t2, q2, f2, ALU.mult))
                        if a == 0:
                            dst = [B["QR"][:, :, 0:QW].rearrange("p t (h d) -> p t h d", h=n)[:, :, :, half * 32:half * 32 + 32]]
                        else:
                            dst = [kdst[:, :, :, c, half * 32:half * 32 + 32] for c in range(2)]
                        for d in dst:
                            ins = nc.vector.tensor_tensor(d, t1, t2, op)
                        link(ins)
            else:
                nc.vector.tensor_copy(B["QR"][:, :, 0:QW], B["PROJ"][:, :, 0:QW])
                for c in range(2):
                    ins = nc.vector.tensor_copy(kdst[:, :, :, c, :], B["PROJ"][:, :, QW:QW + KVW].rearrange("p t (h d) -> p t h d", h=KVH))
                link(ins)
            v0 = TT if latent else 0
            link(nc.vector.tensor_copy(B["V"][:, v0:v0 + TT, :], B["PROJ"][:, :, QW + KVW:QKV2]))
            if latent:
                for h in range(KVH):
                    nc.vector.tensor_copy(B["KT"][:, h, 0:S], KTC[:].rearrange("p l h s -> p (l h) s")[:, bass.ds(l * KVH + h, 1), :].rearrange("p o s -> p (o s)"))
                link(nc.vector.tensor_copy(B["V"][:, 0:TT, :], VC[:].rearrange("p l t n -> p l (t n)")[:, bass.ds(l, 1), :].rearrange("p o n -> p (o n)").rearrange("p (t n) -> p t n", t=TT)))
            dve.sem_inc(rot_ready, 1)
            nk = 2 * S if latent else S
            dve.wait_ge(conv_in_ready, 8)
            nc.vector.tensor_tensor(B["PAD"][:, :, HALO:HALO + S], B["U"][:, 0:4, :], B["U"][:, 4:8, :], ALU.mult).then_inc(pad_ready, 1)
            dve.wait_ge(pad_ready, 1)
            n = TT * QH

            def tap_step(k):
                for j in range(3):
                    tap = B["COLC"][:, j, k:k + 1]
                    if k == 0:
                        ins = nc.vector.tensor_scalar(B["U"][:, j, :], B["PAD"][:, j, 0:S], tap, B["COLC"][:, j, TAPS2:TAPS2 + 1], ALU.mult, ALU.add)
                    else:
                        ins = nc.vector.scalar_tensor_tensor(B["U"][:, j, :], B["PAD"][:, j, k:k + S], tap, B["U"][:, j, :], ALU.mult, ALU.add)
                if k < TAPS2 - 1:
                    link(ins)
                else:
                    ins.then_inc(conv_ready, 1)

            def conv_norm(step):
                if step == 0:
                    for t in range(TT):
                        dve.wait_ge(groups_done, groups.of("convT", t))
                        link(nc.vector.bn_stats(B["BN"][:, t, 0:6], PS[:, groups.at["convT", t, "bank"], :]))
                        link(nc.vector.bn_aggr(B["BN"][:, t, 6:8], B["BN"][:, t, 0:6]))
                    statistic(nc.vector.tensor_copy(st[:, 0, 0:TT], B["BN"][:, :, 7]))
                elif step == 1:
                    r = inverse(2, TT)
                    for t in range(TT):
                        nc.vector.tensor_scalar(B["Y"][:, t, :], PS[:, groups.at["convT", t, "bank"], :], B["BN"][:, t, 6:7], r[:, t:t + 1],
                                                ALU.subtract, ALU.mult).then_inc(conv_read, 1)
                else:
                    dve.wait_ge(conv_read, TT)
                    link(nc.vector.tensor_tensor(B["Y"], B["Y"], B["LNR"][:, 0:1, :].to_broadcast([P, TT, CW2]), ALU.mult))
                    nc.vector.tensor_tensor(B["Y"], B["Y"], B["LNR"][:, 1:2, :].to_broadcast([P, TT, CW2]), ALU.add).then_inc(act_in_ready, 1)

            for i in range(n):
                dve.wait_ge(groups_done, groups.of("score", i))
                nc.vector.tensor_reduce(B["NMAX"][:, i:i + 1], PS[:, groups.at["score", i, "bank"], 0:nk], AX, ALU.max,
                                        negate=True).then_inc(max_ready, 1)
                for k in range(3 * i, min(3 * i + 3, TAPS2)):
                    tap_step(k)
                if CONV_STEP <= i < CONV_STEP + 3:
                    conv_norm(i - CONV_STEP)
            if not latent:
                dve.wait_ge(qkT_ready, 3)
                nc.vector.tensor_copy(KTC[:, 0], B["KT"][:, :, 0:S])
                nc.vector.tensor_copy(VC[:, 0], B["V"][:, 0:TT, :])
            dve.wait_ge(act_out_ready, 1)
            statistic(sum_squares(lambda t: B["Y"][:, t, :], CW2))
            dve.wait_ge(groups_done, groups.of("pv", n - 1))
            link(nc.vector.reciprocal(B["SUM"][:, 1, :], B["SUM"][:, 0, :]))
            for t in range(TT):
                ins = nc.vector.tensor_tensor(B["O"][:, t, :].rearrange("p (h d) -> p h d", h=QH),
                                              PS[:, 6 + t, :].rearrange("p (h d) -> p h d", h=QH),
                                              B["SUM"][:, 1, t * QH:(t + 1) * QH].rearrange("p (h o) -> p h o", o=1).to_broadcast([P, QH, HD]), ALU.mult)
            link(ins)
            r = inverse(3, TT)
            for t in range(TT):
                ins = nc.vector.tensor_scalar(B["Y"][:, t, :], B["Y"][:, t, :], r[:, t:t + 1], None, ALU.mult)
            ins.then_inc(merged_ready, 1)
            r = inverse_root(TT, sum_squares(lambda t: B["O"][:, t, :], QW))
            for t in range(TT):
                ins = nc.vector.tensor_scalar(B["O"][:, t, :], B["O"][:, t, :], r[:, t:t + 1], None, ALU.mult)
            ins.then_inc(merged_ready, 1)
            for t in range(TT):
                for c in range(2):
                    dve.wait_ge(groups_done, groups.of("mix", c, t))
                    cols = slice(c * 512, (c + 1) * 512)
                    nc.vector.tensor_tensor(H[:, t, cols], PS[:, groups.at["mix", c, t, "bank"], :], B["ROW"][0][:, cols], ALU.mult
                                            ).then_inc(mix_read, 1)
                dve.wait_ge(mix_read, 2 * t + 2)
                nc.vector.tensor_tensor(SRC[:, t, :], SRC[:, t, :], H[:, t, :], ALU.add).then_inc(merged_ready, 1)
                dve.wait_ge(merged_ready, 3 + t)
                r = inverse_root(1, sum_squares(lambda _: SRC[:, t, :], D, 1))
                link(nc.vector.scalar_tensor_tensor(H[:, t, :], SRC[:, t, :], r[:, 0:1], B["ROW"][2], ALU.mult, ALU.mult))
                nc.vector.tensor_tensor(H[:, t, :], H[:, t, :], B["ROW"][1], ALU.add).then_inc(h_ready, 1)


            def best(vals, idx, src, these):
                for rnd in range(2):
                    o = slice(8 * rnd, 8 * rnd + 8)
                    for g in these:
                        ins = nc.vector.max(vals[:, g, o], src[:, g, :])
                    link(ins)
                    for g in these:
                        ins = nc.vector.max_index(idx[:, g, o], vals[:, g, o], src[:, g, :])
                    link(ins)
                    if rnd == 0:
                        for g in these:
                            ins = nc.vector.match_replace(src[:, g, :], vals[:, g, o], src[:, g, :], LOW)
                        link(ins)

            def search_keys(t, h0, h1):
                dve.wait_ge(score_read, 4 * t + h1 // 2)
                best(B["TV"], B["TI"], B["SC"][t].rearrange("p (g k) -> p g k", k=EK), range(2 * h0, 2 * h1))
                link(nc.vector.tensor_copy(B["TF"][:, 2 * h0:2 * h1, :], B["TI"][:, 2 * h0:2 * h1, :]))

            def search_pairs(t, h0, h1):
                n, heads, picks = h1 - h0, slice(h0, h1), slice(h0 * TOPK, h1 * TOPK)
                tv = B["TV"][:].rearrange("p (h c) k -> p h c k", c=2)[:, heads]
                tf = B["TF"][:].rearrange("p (h c) k -> p h c k", c=2)[:, heads]
                cand = B["CAND"].rearrange("p (h a b) -> p h a b", h=EH, a=TOPK)[:, heads]
                link(nc.vector.tensor_tensor(cand, tv[:, :, 0, :].rearrange("p h (k o) -> p h k o", o=1).to_broadcast([P, n, TOPK, TOPK]),
                                             tv[:, :, 1:2, :].to_broadcast([P, n, TOPK, TOPK]), ALU.add))
                best(B["BV"], B["BJ"], B["CAND"].rearrange("p (h n) -> p h n", h=EH), range(h0, h1))
                bj = B["BJ"][:].rearrange("p h k -> p (h k)")[:, picks]
                nc.vector.tensor_scalar(B["J"][:, 0, picks], bj, 4, None, ALU.logical_shift_right)
                link(nc.vector.tensor_scalar(B["J"][:, 1, picks], bj, TOPK - 1, None, ALU.bitwise_and))
                link(nc.vector.tensor_copy(B["JF"][:, :, picks], B["J"][:, :, picks]))
                hot = B["HOT"].rearrange("p (h a b) -> p h a b", h=EH, a=TOPK)[:, heads]
                hotf = B["HOT"].rearrange("p (n b) -> p n b", b=TOPK)[:, picks]
                for c in range(2):
                    link(nc.vector.tensor_tensor(hotf, B["JF"][:, c, picks].rearrange("p (n o) -> p n o", o=1).to_broadcast([P, n * TOPK, TOPK]),
                                                 iota16.rearrange("p (o k) -> p o k", o=1).to_broadcast([P, n * TOPK, TOPK]), ALU.is_equal))
                    link(nc.vector.tensor_tensor(hot, hot, tf[:, :, c:c + 1, :].to_broadcast([P, n, TOPK, TOPK]), ALU.mult))
                    link(nc.vector.tensor_reduce(B["EI"][:, c, picks], hotf, AX, ALU.add))
                link(nc.vector.scalar_tensor_tensor(B["EI"][:, 0, picks], B["EI"][:, 0, picks], float(EK), B["EI"][:, 1, picks], ALU.mult, ALU.add))
                nc.vector.tensor_scalar(IDX[:, t, picks], B["EI"][:, 0, picks], BASE[:, 0:1], None, ALU.add).then_inc(picks_ready, 1)
                ei = B["EI"][:, 2 + t, picks].rearrange("p (h k) -> p h k", h=n)
                ins = nc.vector.tensor_tensor(ei, B["BV"][:, heads], B["BV"][:, heads, 0:1].to_broadcast([P, n, TOPK]), ALU.subtract)
                if h1 == EH:
                    ins.then_inc(act_in_ready, 1)

            def softmax_tail(t):
                dve.wait_ge(act_out_ready, 2 + t)
                ei = B["EI"][:, 2 + t, :].rearrange("p (h k) -> p h k", h=EH)
                link(nc.vector.tensor_reduce(B["SUM"][:, 0, 0:EH], ei, AX, ALU.add))
                link(nc.vector.reciprocal(B["SUM"][:, 1, 0:EH], B["SUM"][:, 0, 0:EH]))
                link(nc.vector.tensor_tensor(WGT[:, t, :].rearrange("p (h k) -> p h k", h=EH), ei,
                                             B["SUM"][:, 1, 0:EH].rearrange("p (h o) -> p h o", o=1).to_broadcast([P, EH, TOPK]), ALU.mult))

            return search_keys, search_pairs, softmax_tail, statistic, inverse

        with ExitStack() as ph:
            B = stream_buffers(ph, False)
            CX = sbuf("CX", [P, TT, D], at=ph)
            with nc.Block() as block:
                groups = Groups()

                @block.tensor
                def _(pe):
                    banks = stream_pe(pe, groups, B, False)
                    mod_pe(pe, banks, groups, len(CHUNKS2))

                @block.sync
                def _(sp):
                    sp.dma_start(CX[:], ctx_dram).then_inc(consts_loaded, 16)
                    stream_sp(sp, groups, B, 0, 1)
                    sp.wait_ge(merged_ready, 4)
                    sp.dma_start(cx_dram, CX[:].rearrange("p t d -> p (t d)")).then_inc(stored, 16)
                    used = {8: ("mix", 0, 1), 9: ("mix", 1, 1), 10: ("pq", 1, 0), 11: ("pq", 1, 1)}
                    mod_sp(sp, 1, len(CHUNKS2), lambda c: groups.of(*used[c]) if c in used else groups.of("mod", c - len(CHUNKS2) - WS),
                           lambda: groups.of("pq", TT - 1, 1))
                    sp.wait_ge(stored, 16)

                @block.scalar
                def _(act):
                    stream_act(act, groups, B, 0, False)
                    mod_act(act, groups, 16 * (NPIECE // 2))
                    for t in range(TT):
                        softmax_act(act, B, t)

                @block.vector
                def _(dve):
                    dve.wait_ge(consts_loaded, 16)
                    search_keys, search_pairs, softmax_tail, _, _ = stream_dve(dve, dve_chain(dve), groups, B, CX, 0, False)
                    for t in range(TT):
                        search_keys(t, 0, EH)
                        search_pairs(t, 0, EH)
                    for t in range(TT):
                        softmax_tail(t)

                @block.gpsimd
                def _(pool):
                    stream_pool(pool, groups, B)
                    mod_pool(pool, 1, 16 * (NPIECE // 2))
            phase_end()

        with ExitStack() as ph:
            PROJ = sbuf("PROJ1", [P, TT, QKV1], at=ph)
            DEC = sbuf("DEC", [P, RET_H, 3 * P], at=ph)
            BIAS = sbuf("BIAS", [P, MOBA_H, 3 * P], at=ph)
            PP = sbuf("PP", [P, 4 * 3 * P], at=ph)
            CF = sbuf("CF", [P, 6 * S], at=ph)
            GP = sbuf("GP", [P, 2, S + 2], at=ph)
            RAW = sbuf("RAW", [3 * FT + 6, P], at=ph)
            COLS = sbuf("COLS", [P, 3 * FT + 6], at=ph)
            ALPHAI = sbuf("ALPHAI", [P, P], at=ph)
            NM = sbuf("NM1", [P, 2 * MOBA_H], at=ph)
            SUM = sbuf("SUM1", [P, 2, 2 * MOBA_H], at=ph)
            BN = sbuf("BN1", [P, TT, 14], at=ph)
            RQ, RV, RG, MQ, MV = 0, 2 * RW, 3 * RW, 4 * RW, 4 * RW + 2 * MW
            QROT = CT[:].rearrange("p k s -> p (k s)")[:, 0:TT * 2 * RW].rearrange("p (t n) -> p t n", t=TT)
            SQ = CT[:].rearrange("p k s -> p (k s)")[:, 0:TT * RW].rearrange("p (t n) -> p t n", t=TT)
            RT = XT

            def MT(k):
                return PROJ[:, k // 3, (k % 3) * S:(k % 3 + 1) * S]

            T1 = PP[:, 0:768].rearrange("p (t h d) -> p t h d", t=TT, h=12)
            T2 = PP[:, 768:1536].rearrange("p (t h d) -> p t h d", t=TT, h=12)
            PR = PP[:, 0:768].rearrange("p (i n) -> p i n", i=2)
            PT = PP[:, 768:1536].rearrange("p (i n) -> p i n", i=2)
            YR = PROJ[:, :, MQ:MQ + RW]
            YM = PROJ[:, :, MQ + RW:MQ + RW + MW]
            CONV = CF[:].rearrange("p (j s) -> p j s", j=6)
            APAD = CF[:, 0:4 * (S + 2)].rearrange("p (i j s) -> p i j s", i=2, j=2)
            HC = PP[:, 0:1024].rearrange("p (i j s) -> p i j s", i=2, j=2)
            HG = [PP[:, 1024:1536].rearrange("p (j s) -> p j s", j=2), PROJ[:, 0, 2048:2560].rearrange("p (j s) -> p j s", j=2)]
            PAIRS = FT // 2
            PROJ_CH = [(o, min(512, QKV1 - o)) for o in range(0, QKV1, 512)]
            CONV_CH = [(QKV1, 512), (QKV1 + 512, 256)]
            IN_CH = PROJ_CH + CONV_CH
            NPC = len(PROJ_CH)
            V_ROUNDS = PICKS // RING

            with nc.Fori(0, L) as l:
                with nc.Block() as block:
                    groups = Groups()
                    taken = {}

                    @block.tensor
                    def _(pe):
                        banks = Banks(pe, [0, 1, 2, 3])
                        pe.wait_ge(inputs_loaded, 16 * 2)
                        b = banks.take(cols_ready, 1)
                        nc.tensor.transpose(PS[:, b, 0:3 * FT + 6], RAW[:], ident[0:3 * FT + 6, 0:3 * FT + 6]).then_inc(
                            groups_done, groups.mark("cols"))
                        transposes(pe, banks, groups, "xT", lambda t, k: X[:, t, k * P:(k + 1) * P], DK, xT_ready, 0)
                        pe.wait_ge(xT_ready, 4)
                        for c, (o, n) in enumerate(PROJ_CH):
                            weights_in(pe, c)
                            for t in range(TT):
                                b = banks.take(proj_ready, c * TT + t + 1)
                                matmul_rows(pe, b, (0, n), lambda k: XT[:, k, t * P:(t + 1) * P],
                                            lambda k: wslot(c % WS, DK, n)[:, k, :], DK).then_inc(
                                    groups_done, groups.mark("proj", c, t))
                                groups.at["proj", c, t, "bank"] = b
                        for j in range(6):
                            c = NPC + j // 4
                            if j % 4 == 0:
                                weights_in(pe, c)
                            n = IN_CH[c][1]
                            b = banks.take(conv_in_ready, j + 1)
                            matmul_rows(pe, b, (0, S), lambda k: wslot(c % WS, DK, n)[:, k, (j % 4) * P:(j % 4 + 1) * P],
                                        lambda k: XT[:, k, :], DK).then_inc(groups_done, groups.mark("u", j))
                            groups.at["u", j, "bank"] = b
                        pe.wait_ge(proj_ready, TT * NPC)
                        transposes(pe, banks, groups, "mqk", lambda t, k: PROJ[:, t, MQ + k * P:MQ + (k + 1) * P], 6, qkT_ready, 0)
                        pe.wait_ge(rot_ready, 1)
                        transposes(pe, banks, groups, "rqk", lambda t, k: QROT[:, t, k * P:(k + 1) * P], 6, qkT_ready, 3)
                        pe.wait_ge(qkT_ready, 6)
                        for h in range(RET_H + 1):
                            if h < RET_H:
                                q0, pair = HD * (h % 2), h // 2
                                b = banks.take(ret_ready, h + 1)
                                nc.tensor.matmul(PS[:, b, 0:S], RT[q0:q0 + HD, 3 + pair, 0:P], RT[q0:q0 + HD, pair, :], start=True, stop=True)
                                nc.tensor.matmul(PS[:, b, S:3 * P], RT[q0:q0 + HD, 3 + pair, P:S], RT[q0:q0 + HD, pair, P:S], start=True, stop=True
                                                 ).then_inc(groups_done, groups.mark("rs", h))
                                groups.at["rs", h, "bank"] = b
                            if h >= 1:
                                g = h - 1
                                pe.wait_ge(ret_ready, g + 1)
                                w = PT[:, g % 2, :]
                                cols = slice(g * HD, (g + 1) * HD)
                                v = [PROJ[:, t, RV + g * HD:RV + (g + 1) * HD] for t in range(TT)]
                                nc.tensor.matmul(PS[:, 4, cols], w[:, 0:P], v[0], start=True, stop=True)
                                nc.tensor.matmul(PS[:, 5, cols], w[:, P:S], v[0], start=True, stop=False)
                                nc.tensor.matmul(PS[:, 5, cols], w[:, S:3 * P], v[1], start=False, stop=True
                                                 ).then_inc(groups_done, groups.mark("rpv", g))
                        for i in range(MOBA_H + 2):
                            if i < MOBA_H:
                                q0, pair = HD * (i % 2), i // 2
                                b = banks.take(act_in_ready, i + 1)
                                nc.tensor.matmul(PS[:, b, 0:P], MT(pair)[q0:q0 + HD, 0:P], MT(3 + pair)[q0:q0 + HD, 0:P], start=True, stop=True)
                                nc.tensor.matmul(PS[:, b, P:3 * P], MT(pair)[q0:q0 + HD, P:S], MT(3 + pair)[q0:q0 + HD, :], start=True, stop=True
                                                 ).then_inc(groups_done, groups.mark("ms", i))
                                groups.at["ms", i, "bank"] = b
                            if 1 <= i <= MOBA_H:
                                j = i - 1
                                pe.wait_ge(probs_ready, j + 1)
                                b = banks.take(probsT_ready, j + 1)
                                for kb in range(3):
                                    ins = nc.tensor.transpose(PS[:, b, kb * P:(kb + 1) * P], PR[:, j % 2, kb * P:(kb + 1) * P], ident)
                                ins.then_inc(groups_done, groups.mark("pT", j))
                                groups.at["pT", j, "bank"] = b
                            if i >= 2:
                                j = i - 2
                                pe.wait_ge(probsT_ready, j + 1)
                                w = PT[:, j % 2, :]
                                cols = slice(j * HD, (j + 1) * HD)
                                v = [PROJ[:, t, MV + j * HD:MV + (j + 1) * HD] for t in range(TT)]
                                nc.tensor.matmul(PS[:, 6, cols], w[:, 0:P], v[0], start=True, stop=True)
                                nc.tensor.matmul(PS[:, 7, cols], w[:, P:S], v[0], start=True, stop=False)
                                nc.tensor.matmul(PS[:, 7, cols], w[:, S:3 * P], v[1], start=False, stop=True
                                                 ).then_inc(groups_done, groups.mark("pv", j))
                        pe.wait_ge(merged_ready, 1)
                        transposes(pe, banks, groups, "yT", lambda t, k: YR[:, t, k * P:(k + 1) * P], 3, catT_ready, 0)
                        pe.wait_ge(merged_ready, 2)
                        transposes(pe, banks, groups, "oT", lambda t, k: YM[:, t, k * P:(k + 1) * P], 3, catT_ready, 2)
                        pe.wait_ge(catT_ready, 4)
                        pe.wait_ge(conv_ready, 1)
                        for c in range(2):
                            weights_in(pe, 8 + c)
                            for t in range(TT):
                                b = banks.take(mix_read, c * TT + t + 1)
                                matmul_rows(pe, b, (0, 512), lambda k: CT[:, k, t * P:(t + 1) * P],
                                            lambda k: wslot(c, DK, 512)[:, k, :], DK).then_inc(
                                    groups_done, groups.mark("mix", c, t))
                                groups.at["mix", c, t, "bank"] = b
                        pe.wait_ge(h_ready, 1)
                        transposes(pe, banks, groups, "x1T", lambda t, k: X[:, t, k * P:(k + 1) * P], DK, xT_ready, 4)
                        for t in range(TT):
                            for n in range(2):
                                nc.tensor.matmul(PS[:, 4 + 2 * t + n, :], ALPHAI[:], X[:, t, n * 512:(n + 1) * 512], start=True,
                                                 stop=False, skip_group_check=True)
                        pe.wait_ge(xT_ready, 8)

                        def up(i, r, lap):
                            pe.wait_ge(up_loaded[r], 32 * (i // 2 + 1) + lap * 16)
                            if i >= 2:
                                pe.wait_ge(up_read, i - 1 + lap)
                                pe.wait_ge(hidden_ready, i - 1 + lap)
                            for half in range(2):
                                for j in range(2):
                                    for k in range(DK):
                                        c = half * 2 * P + j * P
                                        ins = nc.tensor.matmul(PS[:, 2 * r + half, j * S:(j + 1) * S], wslot(r, DK, 512)[:, k, c:c + P],
                                                               XT[:, k, :], start=(k == 0), stop=(k == DK - 1))
                                ins.then_inc(groups_done, groups.mark("up", i, half))

                        def down(i, r, lap, last=False):
                            pe.wait_ge(down_loaded[r], 16 * (i // 2 + 1) + lap * 8)
                            pe.wait_ge(hidden_ready, i + 1 + lap)
                            for j in range(2):
                                for t in range(TT):
                                    for n in range(2):
                                        ins = nc.tensor.matmul(PS[:, 4 + 2 * t + n, :], HG[r][:, j, t * P:(t + 1) * P],
                                                               wslot(2 + r, 2, D)[:, j, n * 512:(n + 1) * 512], start=False,
                                                               stop=last and j == 1, skip_group_check=True)
                            ins.then_inc(groups_done, groups.mark("down", i))

                        up(0, 0, 0)
                        up(1, 1, 0)
                        down(0, 0, 0)
                        at_loop = groups.n
                        with pe.Fori(0, (PAIRS - 3) // 2) as it:
                            for i in (2, 3):
                                up(i, i % 2, it * 2)
                                down(i - 1, (i - 1) % 2, it * 2)
                        taken["per"] = groups.n - at_loop
                        groups.n += taken["per"] * ((PAIRS - 3) // 2 - 1)
                        up(PAIRS - 1, 0, 0)
                        down(PAIRS - 2, 1, 0)
                        down(PAIRS - 1, 0, 0, last=True)

                    @block.sync
                    def _(sp):
                        sp.dma_start(RAW[0:3 * FT, :], A["ffn_conv_w"].rearrange("l k (f p) -> l (k f) p", p=P)[l]).then_inc(inputs_loaded, 16)
                        sp.dma_start(RAW[3 * FT:3 * FT + 6, :], A["conv_w"].rearrange("l k (f p) -> l (k f) p", p=P)[l]).then_inc(inputs_loaded, 16)

                        def load(c):
                            name, o, n = ("w_in", *IN_CH[c]) if c < 8 else ("w_out", (c - 8) * 512, 512)
                            sp.dma_start(wslot(c % WS, DK, n), wview(name, l)[:, :, o:o + n]).then_inc(weights_loaded[c % WS], 16)

                        last = [("proj", c, 1) for c in range(NPC)]
                        for c in range(4):
                            load(c)
                        sp.dma_start(DEC[:].rearrange("p h n -> p (h n)"), A["decay"]).then_inc(consts_loaded, 16)
                        sp.dma_start(BIAS[:].rearrange("p h n -> p (h n)"), bias_dram).then_inc(consts_loaded, 16)
                        for c in range(4, 10):
                            sp.wait_ge(groups_done, groups.of(*last[c - 4]))
                            load(c)

                        up_v = A["w_up"].rearrange("l (k p) (h f n) -> l f h p k n", p=P, h=2, n=2 * P)[l]
                        down_v = A["w_down"].rearrange("l (f j p) n -> l f p j n", p=P, j=2)[l]

                        def load_up(i, r):
                            for half in range(2):
                                sp.dma_start(wslot(r, DK, 512)[:, :, half * 2 * P:(half + 1) * 2 * P], up_v[i, half]
                                             ).then_inc(up_loaded[r], 16)

                        def load_down(i, r):
                            sp.dma_start(wslot(2 + r, 2, D), down_v[i]).then_inc(down_loaded[r], 16)

                        sp.wait_ge(groups_done, groups.of("u", 3))
                        load_down(0, 0)
                        sp.wait_ge(groups_done, groups.of("u", 5))
                        load_down(1, 1)
                        sp.wait_ge(groups_done, groups.of("ms", MOBA_H - 1))
                        for i, name in enumerate(("ln1_g", "ln1_b")):
                            sp.dma_start(PROJ[:, i, 0:D], A[name].rearrange("(o l) n -> l o n", o=1)[l].to_broadcast([P, D])
                                         ).then_inc(late_rows_loaded, 16)
                        sp.wait_ge(groups_done, groups.of("mix", 0, 1))
                        load_up(0, 0)
                        sp.wait_ge(groups_done, groups.of("mix", 1, 1))
                        load_up(1, 1)
                        for i, name in enumerate(("ln2_g", "ln2_b")):
                            sp.dma_start(PROJ[:, i, D:2 * D], A[name].rearrange("(o l) n -> l o n", o=1)[l].to_broadcast([P, D])
                                         ).then_inc(rows_loaded, 16)
                        per = taken["per"]
                        sp.wait_ge(groups_done, groups.of("up", 0, 1))
                        load_up(2, 0)
                        sp.wait_ge(groups_done, groups.of("down", 0))
                        load_down(2, 0)
                        with sp.Fori(0, (PAIRS - 3) // 2) as it:
                            sp.wait_ge(groups_done, it * per + groups.of("up", 1, 1))
                            load_up(it * 2 + 3, 1)
                            sp.wait_ge(groups_done, it * per + groups.of("down", 1))
                            load_down(it * 2 + 3, 1)
                            sp.wait_ge(groups_done, it * per + groups.of("up", 2, 1))
                            load_up(it * 2 + 4, 0)
                            sp.wait_ge(groups_done, it * per + groups.of("down", 2))
                            load_down(it * 2 + 4, 0)
                        sp.wait_ge(rows_used, RING + 2 * PICKS)
                        sp.dma_start(cs_dram[l], PROD[:]).then_inc(stored, 16)
                        sp.wait_ge(stored, 16)

                    @block.scalar
                    def _(act):
                        def bank(*name):
                            act.wait_ge(groups_done, groups.of(*name))
                            return groups.at[name + ("bank",)]

                        for j in range(DK // 2):
                            b = bank("xT", j)
                            nc.scalar.copy(XT[:, 2 * j:2 * j + 2, :].rearrange("p k s -> p (k s)"), PS[:, b, :]).then_inc(xT_ready, 1)
                        for c, (o, n) in enumerate(PROJ_CH):
                            for t in range(TT):
                                b = bank("proj", c, t)
                                nc.scalar.copy(PROJ[:, t, o:o + n], PS[:, b, 0:n]).then_inc(proj_ready, 1)
                        for j in range(6):
                            b = bank("u", j)
                            nc.scalar.copy(CONV[:, j, :], PS[:, b, 0:S]).then_inc(conv_in_ready, 1)
                        act.wait_ge(proj_ready, TT * NPC)
                        nc.scalar.activation(PROJ[:, :, RG:RG + RW], PROJ[:, :, RG:RG + RW], ACT.Silu).then_inc(silu_ready, 1)
                        act.wait_ge(rot_ready, 1)
                        for j in range(3):
                            b = bank("mqk", j)
                            nc.scalar.copy(MT(2 * j), PS[:, b, 0:S])
                            nc.scalar.copy(MT(2 * j + 1), PS[:, b, S:2 * S]).then_inc(qkT_ready, 1)
                        for j in range(3):
                            b = bank("rqk", j)
                            nc.scalar.copy(RT[:, 2 * j:2 * j + 2, :].rearrange("p k s -> p (k s)"), PS[:, b, :]).then_inc(qkT_ready, 1)
                        root(act, TT * RET_H, 0, 1.0 / HD, 0)
                        for i in range(MOBA_H):
                            act.wait_ge(max_ready, i + 1)
                            nc.scalar.activation(PR[:, i % 2, 0:P], PR[:, i % 2, 0:P], ACT.Exp, bias=NM[:, 2 * i:2 * i + 1],
                                                 accum_out=SUM[:, 0, i:i + 1])
                            nc.scalar.activation(PR[:, i % 2, P:3 * P], PR[:, i % 2, P:3 * P], ACT.Exp, bias=NM[:, 2 * i + 1:2 * i + 2],
                                                 accum_out=SUM[:, 0, MOBA_H + i:MOBA_H + i + 1]).then_inc(probs_ready, 1)
                        for name, k0 in (("yT", 0), ("oT", 3)):
                            for j in range(2):
                                b = bank(name, j)
                                n = 2 - j
                                nc.scalar.copy(CT[:, k0 + 2 * j:k0 + 2 * j + n, :].rearrange("p k s -> p (k s)"), PS[:, b, 0:n * S]).then_inc(catT_ready, 1)
                        root(act, TT, 1, 1.0, 0)
                        for j in range(DK // 2):
                            b = bank("x1T", j)
                            nc.scalar.copy(XT[:, 2 * j:2 * j + 2, :].rearrange("p k s -> p (k s)"), PS[:, b, :]).then_inc(xT_ready, 1)
                        act.wait_ge(dots_ready, 1)
                        nc.scalar.activation(DOT[:, 0, :], DOT[:, 0, :], ACT.Gelu).then_inc(gelu_ready, 1)
                        per = taken["per"]

                        def hidden(i, r, lap, glap):
                            act.wait_ge(groups_done, groups.of("up", i, 0) + glap)
                            if i >= 2:
                                act.wait_ge(conv_done, i + lap)
                            nc.scalar.copy(APAD[:, r, :, 2:2 + S], PS[:, 2 * r, :].rearrange("p (j s) -> p j s", j=2)).then_inc(up_read, 1)
                            act.wait_ge(conv_done, i + 2 + lap)
                            nc.scalar.activation(HC[:, r], HC[:, r], ACT.Gelu).then_inc(gelu_done, 1)

                        act.wait_ge(conv_done, 1)
                        hidden(0, 0, 0, 0)
                        hidden(1, 1, 0, 0)
                        with act.Fori(0, (PAIRS - 3) // 2) as it:
                            hidden(2, 0, it * 2, it * per)
                            hidden(3, 1, it * 2, it * per)
                        hidden(PAIRS - 1, 0, 0, 0)
                        root(act, TT, 2, 1.0, 0)

                    @block.vector
                    def _(dve):
                        link = dve_chain(dve)
                        dve.sem_inc(rows_used, RING)
                        link(nc.vector.tensor_copy(PROD[:], H[:].rearrange("p t d -> p (t d)")[:, bass.ts(l, D)]))
                        link(nc.vector.tensor_copy(COEF[:, 1, :], WGT[:].rearrange("p t d -> p (t d)")[:, bass.ts(l, PICKS)]))
                        nc.vector.tensor_scalar(ALPHAI[:], ident, ALPHA, None, ALU.mult)
                        link(nc.vector.memset(GP[:, :, 0:2], 0.0))
                        dve.wait_ge(groups_done, groups.of("cols"))
                        nc.vector.tensor_copy(COLS[:], PS[:, 0, 0:3 * FT + 6]).then_inc(cols_ready, 1)
                        before = l * 2 * V_ROUNDS
                        EARLY, PER_HEAD, LATE = 4, 4, 3
                        with dve.Fori(0, EARLY) as e:
                            link.count.enter(e, 1)
                            dot_round(dve, BESIDE, PROD[:], DOT[:, 0, bass.ts(e, RING)], e, before, link)
                        link.count.leave(EARLY)
                        taken["dots"] = EARLY * RING

                        def dots(n):
                            for _ in range(n):
                                e, k = divmod(taken["dots"], RING)
                                dot_step(dve, BESIDE, PROD[:], k, e, before)
                                if k == RING - 1:
                                    dots_out(dve, BESIDE, DOT[:, 0, e * RING:(e + 1) * RING], e, link)
                                taken["dots"] += 1

                        dve.wait_ge(proj_ready, TT * NPC)
                        cos, sin = (angles(c).to_broadcast([P, TT, 12, 32]) for c in (C_COS1, C_SIN1))
                        qk = PROJ[:, :, 0:2 * RW].rearrange("p t (h d) -> p t h d", h=12)
                        qr = QROT.rearrange("p t (h d) -> p t h d", h=12)
                        for half, (f1, f2, op) in enumerate(((cos, sin, ALU.subtract), (sin, cos, ALU.add))):
                            nc.vector.tensor_tensor(T1, qk[:, :, :, 0:32], f1, ALU.mult)
                            link(nc.vector.tensor_tensor(T2, qk[:, :, :, 32:64], f2, ALU.mult))
                            ins = nc.vector.tensor_tensor(qr[:, :, :, half * 32:half * 32 + 32], T1, T2, op)
                            if half == 0:
                                link(ins)
                        ins.then_inc(rot_ready, 1)
                        dve.wait_ge(conv_in_ready, 6)
                        dve.wait_ge(rot_ready, 1)
                        link(nc.vector.tensor_tensor(GP[:, :, 2:2 + S], CONV[:, 2:4, :], CONV[:, 4:6, :], ALU.mult))
                        for k in range(3):
                            for j in range(2):
                                tap = COLS[:, 3 * FT + 2 * k + j:3 * FT + 2 * k + j + 1]
                                if k == 0:
                                    ins = nc.vector.tensor_scalar(CT[:, 6 + j, :], GP[:, j, 0:S], tap, None, ALU.mult)
                                else:
                                    ins = nc.vector.scalar_tensor_tensor(CT[:, 6 + j, :], GP[:, j, k:k + S], tap, CT[:, 6 + j, :], ALU.mult, ALU.add)
                            link(ins)
                        nc.vector.tensor_tensor(CT[:, 6:8, :], CT[:, 6:8, :], CONV[:, 0:2, :], ALU.mult).then_inc(conv_ready, 1)
                        dve.wait_ge(consts_loaded, 32)
                        for h in range(RET_H):
                            dve.wait_ge(groups_done, groups.of("rs", h))
                            if h >= 2:
                                dve.wait_ge(groups_done, groups.of("rpv", h - 2))
                            nc.vector.tensor_tensor(PT[:, h % 2, :], PS[:, groups.at["rs", h, "bank"], 0:3 * P], DEC[:, h, :], ALU.mult
                                                    ).then_inc(ret_ready, 1)
                            dots(PER_HEAD)
                        dve.wait_ge(groups_done, groups.of("rpv", RET_H - 1))

                        def heads(ap):
                            return ap.rearrange("p t (h d) -> p (t h) d", h=RET_H)

                        def spread(ap):
                            return ap.rearrange("p (t h o) -> p t h o", t=TT, o=1).to_broadcast([P, TT, RET_H, HD])

                        raw = PS[:, 4:6, 0:RW].rearrange("p t (h d) -> p t h d", h=RET_H)
                        yr = YR.rearrange("p t (h d) -> p t h d", h=RET_H)
                        link(nc.vector.tensor_reduce(NM[:, 0:12].rearrange("p (t h) -> p t h", t=TT), raw, AX, ALU.add))
                        link(nc.vector.tensor_scalar(NM[:, 0:12], NM[:, 0:12], 1.0 / HD, None, ALU.mult))
                        link(nc.vector.tensor_tensor(yr, raw, spread(NM[:, 0:12]), ALU.subtract))
                        link(nc.vector.tensor_tensor(SQ, YR, YR, ALU.mult))
                        nc.vector.tensor_reduce(st[:, 0, 0:12].rearrange("p (t h) -> p t h", t=TT),
                                                SQ.rearrange("p t (h d) -> p t h d", h=RET_H), AX, ALU.add).then_inc(stat_ready, 1)

                        def scores(i):
                            dve.wait_ge(groups_done, groups.of("ms", i))
                            if i >= 2:
                                dve.wait_ge(groups_done, groups.of("pT", i - 2))
                            ins = nc.vector.scalar_tensor_tensor(PR[:, i % 2, :], PS[:, groups.at["ms", i, "bank"], 0:3 * P], HD ** -0.5,
                                                                 BIAS[:, i, :], ALU.mult, ALU.add)
                            ins.then_inc(act_in_ready, 1)
                            dve.wait_ge(act_in_ready, i + 1)
                            nc.vector.tensor_reduce(NM[:, 2 * i:2 * i + 1], PR[:, i % 2, 0:P], AX, ALU.max, negate=True)
                            nc.vector.tensor_reduce(NM[:, 2 * i + 1:2 * i + 2], PR[:, i % 2, P:3 * P], AX, ALU.max, negate=True
                                                    ).then_inc(max_ready, 1)

                        scores(0)
                        dve.wait_ge(root_ready, 1)
                        link(nc.vector.reciprocal(ri[:, 0, 0:12], rt[:, 0, 0:12]))
                        link(nc.vector.tensor_tensor(yr, yr, spread(ri[:, 0, 0:12]), ALU.mult))
                        dve.wait_ge(silu_ready, 1)
                        nc.vector.tensor_tensor(YR, YR, PROJ[:, :, RG:RG + RW], ALU.mult).then_inc(merged_ready, 1)
                        for i in range(MOBA_H):
                            if i + 1 < MOBA_H:
                                scores(i + 1)
                            dve.wait_ge(groups_done, groups.of("pT", i))
                            if i >= 2:
                                dve.wait_ge(groups_done, groups.of("pv", i - 2))
                            nc.vector.tensor_copy(PT[:, i % 2, :], PS[:, groups.at["pT", i, "bank"], 0:3 * P]).then_inc(probsT_ready, 1)
                            dots(PER_HEAD)
                        link(nc.vector.reciprocal(SUM[:, 1, :], SUM[:, 0, :]))
                        dve.wait_ge(groups_done, groups.of("pv", MOBA_H - 1))
                        nc.vector.tensor_tensor(YM.rearrange("p t (h d) -> p t h d", h=MOBA_H),
                                                PS[:, 6:8, 0:MW].rearrange("p t (h d) -> p t h d", h=MOBA_H),
                                                spread(SUM[:, 1, :]), ALU.mult).then_inc(merged_ready, 1)
                        dots(LATE * RING)
                        for c in range(2):
                            for t in range(TT):
                                dve.wait_ge(groups_done, groups.of("mix", c, t))
                                cols = slice(c * 512, (c + 1) * 512)
                                nc.vector.scalar_tensor_tensor(X[:, t, cols], X[:, t, cols], ALPHA, PS[:, groups.at["mix", c, t, "bank"], :],
                                                               ALU.mult, ALU.add).then_inc(mix_read, 1)
                        dve.wait_ge(mix_read, 4)

                        def norm(halves, i, rows):
                            for t in range(TT):
                                nc.vector.bn_stats(BN[:, t, 0:6], halves(t, 0))
                                link(nc.vector.bn_stats(BN[:, t, 6:12], halves(t, 1)))
                                link(nc.vector.bn_aggr(BN[:, t, 12:14], BN[:, t, 0:12]))
                            nc.vector.tensor_copy(st[:, i % 2, 0:TT], BN[:, :, 13]).then_inc(stat_ready, 1)
                            dve.wait_ge(root_ready, i + 1)
                            link(nc.vector.reciprocal(ri[:, i % 2, 0:TT], rt[:, i % 2, 0:TT]))
                            for t in range(TT):
                                for n in range(2):
                                    ins = nc.vector.tensor_scalar(X[:, t, n * 512:(n + 1) * 512], halves(t, n), BN[:, t, 12:13],
                                                                  ri[:, i % 2, t:t + 1], ALU.subtract, ALU.mult)
                            link(ins)
                            link(nc.vector.tensor_tensor(X[:], X[:], PROJ[:, 0:1, rows:rows + D].to_broadcast([P, TT, D]), ALU.mult))
                            nc.vector.tensor_tensor(X[:], X[:], PROJ[:, 1:2, rows:rows + D].to_broadcast([P, TT, D]), ALU.add).then_inc(h_ready, 1)

                        dve.wait_ge(late_rows_loaded, 32)
                        norm(lambda t, n: X[:, t, n * 512:(n + 1) * 512], 1, 0)
                        dve.wait_ge(catT_ready, 4)
                        nc.vector.memset(APAD[:, :, :, 0:2], 0.0).then_inc(conv_done, 1)
                        dots(PICKS - taken["dots"])
                        dve.sem_inc(dots_ready, 1)
                        dve.wait_ge(gelu_ready, 1)
                        link(nc.vector.tensor_tensor(COEF[:, 0, :], DOT[:, 0, :], COEF[:, 1, :], ALU.mult))
                        link(nc.vector.memset(PROD[:], 0.0))
                        per = taken["per"]

                        def sum_rows(m):
                            sum_round(dve, BESIDE, PROD[:], lambda k: COEF[:, 0, m * RING + k:m * RING + k + 1] if isinstance(m, int)
                                      else COEF[:, 0, bass.ds(m * RING + k, 1)], m + V_ROUNDS, before)

                        sum_rows(0)

                        def hidden(i, r, pair, lap, glap, rounds, n8):
                            dve.wait_ge(up_read, i + 1 + lap)
                            for k in range(3):
                                for j in range(2):
                                    c = k * FT + j
                                    tap = COLS[:, 2 * i + c:2 * i + c + 1] if pair is None else COLS[:, bass.ds(pair * 2 + c, 1)]
                                    if k == 0:
                                        ins = nc.vector.tensor_scalar(HC[:, r, j, :], APAD[:, r, j, 0:S], tap, None, ALU.mult)
                                    else:
                                        ins = nc.vector.scalar_tensor_tensor(HC[:, r, j, :], APAD[:, r, j, k:k + S], tap, HC[:, r, j, :], ALU.mult, ALU.add)
                                if k < 2:
                                    link(ins)
                            ins.then_inc(conv_done, 1)
                            for v in range(rounds):
                                sum_rows(n8 + v)
                            dve.wait_ge(gelu_done, i + 1 + lap)
                            dve.wait_ge(groups_done, groups.of("up", i, 1) + glap)
                            if i >= 2:
                                down_before = groups.of("down", 0) if i == 2 else groups.of("down", 1)
                                if i == PAIRS - 1:
                                    down_before = groups.of("down", 2) + per * ((PAIRS - 3) // 2 - 1)
                                dve.wait_ge(groups_done, down_before + glap)
                            nc.vector.tensor_tensor(HG[r], HC[:, r], PS[:, 2 * r + 1, :].rearrange("p (j s) -> p j s", j=2), ALU.mult
                                                    ).then_inc(hidden_ready, 1)

                        hidden(0, 0, None, 0, 0, 0, 1)
                        hidden(1, 1, None, 0, 0, 1, 1)
                        with dve.Fori(0, (PAIRS - 3) // 2) as it:
                            link.count.enter(it, 4)
                            hidden(2, 0, it * 2 + 2, it * 2, it * per, 2, it * 3 + 2)
                            hidden(3, 1, it * 2 + 3, it * 2, it * per, 1, it * 3 + 4)
                        link.count.leave((PAIRS - 3) // 2)
                        hidden(PAIRS - 1, 0, None, 0, 0, 1, 14)
                        sum_rows(V_ROUNDS - 1)
                        dve.wait_ge(groups_done, groups.of("down", PAIRS - 1))
                        dve.wait_ge(rows_loaded, 32)
                        norm(lambda t, n: PS[:, 4 + 2 * t + n, :], 2, D)

                    @block.gpsimd
                    def _(pool):
                        idx = IDX[:].rearrange("p t n -> p (t n)")
                        for i, table in enumerate(("peer_u_2", "peer_v_2")):
                            gather_rows(pool, BESIDE, table, lambda e: idx[:, bass.ds(l * PICKS + e * RING, RING)], i * PICKS)
                phase_end()

        AR = ROWS[:].rearrange("p k d -> p (k d)")
        KX = AR[:, 0:2 * D].rearrange("p (t d) -> p t d", t=TT)
        KS = AR[:, 2 * D:4 * D].rearrange("p (t d) -> p t d", t=TT)
        KGATE = AR[:, 4 * D:5 * D]
        KVS = AR[:, 5 * D:5 * D + TT * 2 * KVW].rearrange("p (t n) -> p t n", t=TT)
        KD = AR[:, 6 * D:6 * D + TT * 2 * KVW].rearrange("p (t h c d) -> p t h c d", t=TT, h=KVH, c=2)
        KW = CT

        def keys_pe(pe, banks, groups, B):
            pe.wait_ge(keys_loaded, 16 * 6)
            b = banks.take(cols_ready, 2)
            nc.tensor.transpose(PS[:, b, 0:16], B["MODR"][:], ident[0:16, 0:16]).then_inc(groups_done, groups.mark("kcols"))
            groups.at["kcols", "bank"] = b
            pe.wait_ge(norm_ready, 2 * TT)
            transposes(pe, banks, groups, "kxT", lambda t, k: KS[:, t, k * P:(k + 1) * P], DK, xT_ready, 8)
            pe.wait_ge(xT_ready, 12)
            for t in range(TT):
                b = banks.take(proj_ready, 4 + t + 1)
                matmul_rows(pe, b, (0, 2 * KVW), lambda k: XT[:, k, t * P:(t + 1) * P], lambda k: KW[:, k, :], DK).then_inc(
                    groups_done, groups.mark("kproj", t))
                groups.at["kproj", t, "bank"] = b
            pe.wait_ge(rot_ready, 2)
            transposes(pe, banks, groups, "kT", lambda t, k: KD[:, t, k].rearrange("p c d -> p (c d)"), KVH, qkT_ready, 3)

        def keys_sp(sp, B):
            sp.wait_ge(picks_ready, 2 * TT)
            for dst, src in ((KX, cx_dram.rearrange("p (t d) -> p t d", t=TT)), (KS, cs_dram.rearrange("t p d -> p t d")),
                             (KGATE, mod_dram[0, 1:2, 5 * D:6 * D].to_broadcast([P, D])),
                             (B["GAIN"][:, 1, :], A["k_gain_2"][1:2, :].to_broadcast([P, HD])),
                             (B["MODR"][:], mod_dram[1, 1:2, 0:2 * D].rearrange("o (k p) -> (o k) p", p=P)),
                             (KW[:], wview("w_in_2", 1)[:, :, QW:QKV2])):
                sp.dma_start(dst, src).then_inc(keys_loaded, 16)

        def keys_act(act, groups, B):
            root(act, TT, 7, 1.0 / D, 1)
            act.wait_ge(cols_ready, 2)
            for j in range(DK // 2):
                act.wait_ge(groups_done, groups.of("kxT", j))
                for k in range(2):
                    ins = nc.scalar.activation(XT[:, 2 * j + k, :], PS[:, groups.at["kxT", j, "bank"], k * S:(k + 1) * S], ACT.Identity,
                                               bias=B["MODC"][:, 2 * j + k:2 * j + k + 1], scale=B["MODC"][:, 8 + 2 * j + k:9 + 2 * j + k])
                ins.then_inc(xT_ready, 1)
            for t in range(TT):
                act.wait_ge(groups_done, groups.of("kproj", t))
                nc.scalar.copy(KVS[:, t, :], PS[:, groups.at["kproj", t, "bank"], 0:2 * KVW]).then_inc(proj_ready, 1)
            root(act, TT * KVH, 8, 1.0 / HD, 1)
            act.wait_ge(groups_done, groups.of("kT", 0))
            nc.scalar.copy(KTC[:, 1], PS[:, groups.at["kT", 0, "bank"], :].rearrange("p (k s) -> p k s", k=KVH)).then_inc(qkT_ready, 1)

        def keys_dve(dve, link, groups, B, statistic, inverse, step):
            k4 = KVS[:, :, 0:KVW].rearrange("p t (h d) -> p t h d", h=KVH)
            if step == 0:
                dve.wait_ge(keys_loaded, 16 * 6)
                link(nc.vector.tensor_tensor(KS, KS, KGATE.rearrange("p (o d) -> p o d", o=1).to_broadcast([P, TT, D]), ALU.mult))
                link(nc.vector.tensor_tensor(KX, KX, KS, ALU.add))
                for t in range(TT):
                    ins = nc.vector.tensor_tensor_reduce(PROD[:], KX[:, t, :], KX[:, t, :], 1.0, 0.0, ALU.mult, ALU.add, st[:, 1, t:t + 1])
                    if t == 0:
                        link(ins)
                statistic(ins)
            elif step == 1:
                r = inverse(7, TT)
                for t in range(TT):
                    nc.vector.tensor_scalar(KS[:, t, :], KX[:, t, :], r[:, t:t + 1], None, ALU.mult).then_inc(norm_ready, 1)
                dve.wait_ge(groups_done, groups.of("kcols"))
                b = groups.at["kcols", "bank"]
                nc.vector.tensor_copy(B["MODC"][:, 0:8], PS[:, b, 0:8])
                nc.vector.tensor_scalar(B["MODC"][:, 8:16], PS[:, b, 8:16], 1.0, None, ALU.add).then_inc(cols_ready, 1)
            elif step == 2:
                dve.wait_ge(proj_ready, 4 + TT)
                nc.vector.tensor_copy(VC[:, 1], KVS[:, :, KVW:2 * KVW])
                sq = PROD[:, 0:TT * KVW].rearrange("p (t h d) -> p t h d", t=TT, h=KVH)
                link(nc.vector.tensor_tensor(sq, k4, k4, ALU.mult))
                statistic(nc.vector.tensor_reduce(st[:, 0, 0:4].rearrange("p (t h) -> p t h", t=TT), sq, AX, ALU.add))
            else:
                r = inverse(8, TT * KVH)
                link(nc.vector.tensor_tensor(k4, k4, r[:, 0:4].rearrange("p (t h o) -> p t h o", t=TT, o=1).to_broadcast([P, TT, KVH, HD]), ALU.mult))
                for c in range(2):
                    ins = nc.vector.tensor_tensor(KD[:, :, :, c, :], k4, B["GAIN"][:, 1:2, :].rearrange("p (t o) d -> p t o d", t=1).to_broadcast([P, TT, KVH, HD]), ALU.mult)
                ins.then_inc(rot_ready, 1)

        with ExitStack() as ph:
            B = stream_buffers(ph, True)
            for l in range(L):
                with nc.Block() as block:
                    groups = Groups()

                    @block.tensor
                    def _(pe):
                        banks = stream_pe(pe, groups, B, True)
                        if l == 0:
                            keys_pe(pe, banks, groups, B)

                    @block.sync
                    def _(sp):
                        stream_sp(sp, groups, B, l, 0)
                        sp.wait_ge(h_ready, TT)
                        sp.dma_start(B["ROW"][2], mod_dram[l][0:1, 5 * D:6 * D].to_broadcast([P, D])).then_inc(rows_loaded, 16)
                        if l == 0:
                            keys_sp(sp, B)

                    @block.scalar
                    def _(act):
                        stream_act(act, groups, B, l, True)
                        for t in range(TT):
                            softmax_act(act, B, t)
                            if l == 0 and t == 1:
                                keys_act(act, groups, B)
                            act.wait_ge(dots_ready, t + 1)
                            nc.scalar.activation(DOT[:, t, :], DOT[:, t, :], ACT.Gelu).then_inc(gelu_ready, 1)

                    @block.vector
                    def _(dve):
                        link = dve_chain(dve)
                        search_keys, search_pairs, softmax_tail, statistic, inverse = stream_dve(dve, link, groups, B, X, l, True)
                        dve.sem_inc(rows_used, RING2)
                        rounds = PICKS // RING2
                        before = l * 2 * TT * rounds
                        for h in (0, EH // 2):
                            search_keys(0, h, h + EH // 2)
                            search_pairs(0, h, h + EH // 2)
                        link(nc.vector.memset(ACC[:], 0.0))

                        def dot_rounds(t, first, n):
                            with dve.Fori(first, first + n) as e:
                                link.count.enter(e - first, 1)
                                dot_round(dve, ALONE, H[:, t, :], DOT[:, t, bass.ts(e, RING2)], e + 2 * t * rounds, before, link)
                            link.count.leave(n)

                        def sum_rounds(t, first, n):
                            with dve.Fori(first, first + n) as e:
                                sum_round(dve, ALONE, ACC[:, t, :], lambda k: COEF[:, t, bass.ds(e * RING2 + k, 1)], e + (2 * t + 1) * rounds, before)

                        def coefficients(t):
                            dve.sem_inc(dots_ready, 1)
                            softmax_tail(t)
                            dve.wait_ge(gelu_ready, t + 1)
                            link(nc.vector.tensor_tensor(COEF[:, t, :], DOT[:, t, :], WGT[:, t, :], ALU.mult))

                        def onto_stream(t):
                            dve.wait_ge(rows_used, RING2 + 2 * (t + 1) * PICKS)
                            dve.wait_ge(rows_loaded, 16 * 6)
                            link(nc.vector.tensor_tensor(ACC[:, t, :], ACC[:, t, :], B["ROW"][2], ALU.mult))
                            link(nc.vector.tensor_tensor(X[:, t, :], X[:, t, :], ACC[:, t, :], ALU.add))

                        dot_rounds(0, 0, 2)
                        search_keys(1, 0, EH // 2)
                        dot_rounds(0, 2, 2)
                        search_pairs(1, 0, EH // 2)
                        dot_rounds(0, 4, 4)
                        coefficients(0)
                        sum_rounds(0, 0, 2)
                        search_keys(1, EH // 2, EH)
                        sum_rounds(0, 2, 2)
                        search_pairs(1, EH // 2, EH)
                        sum_rounds(0, 4, 4)
                        onto_stream(0)
                        if l == 0:
                            for step in range(4):
                                dot_rounds(1, 2 * step, 2)
                                keys_dve(dve, link, groups, B, statistic, inverse, step)
                        else:
                            dot_rounds(1, 0, rounds)
                        coefficients(1)
                        sum_rounds(1, 0, rounds)
                        onto_stream(1)
                        nc.vector.tensor_scalar(BASE[:], BASE[:], float(N_EXP), None, ALU.add)

                    @block.gpsimd
                    def _(pool):
                        stream_pool(pool, groups, B)
                        pool.wait_ge(groups_done, groups.of("pq", TT - 1, 1))
                        half = PICKS // 2
                        for t in range(TT):
                            for i in range(2):
                                pool.wait_ge(picks_ready, 2 * t + i + 1)
                                gather_rows(pool, ALONE, "peer_u_2", lambda e: IDX[:, t, bass.ds(e * RING2 + i * half, RING2)],
                                            2 * t * PICKS + i * half, half)
                            gather_rows(pool, ALONE, "peer_v_2", lambda e: IDX[:, t, bass.ds(e * RING2, RING2)], (2 * t + 1) * PICKS)
                phase_end()

        with ExitStack() as ph:
            FG = sbuf("FG", [P, D], at=ph)
            with nc.Block() as block:

                @block.sync
                def _(sp):
                    sp.dma_start(FG[:], A["final_g_2"].rearrange("(o n) -> o n", o=1).to_broadcast([P, D])).then_inc(rows_loaded, 16)
                    for t in range(TT):
                        sp.wait_ge(norm_ready, t + 1)
                        sp.dma_start(out_dram[:, t, :], X[:, t, :]).then_inc(stored, 16)
                    sp.wait_ge(stored, 16 * TT)

                @block.scalar
                def _(act):
                    root(act, TT, 0, 1.0 / D, 1)

                @block.vector
                def _(dve):
                    link = dve_chain(dve)
                    for t in range(TT):
                        ins = nc.vector.tensor_tensor_reduce(H[:, t, :], X[:, t, :], X[:, t, :], 1.0, 0.0, ALU.mult, ALU.add, st[:, 0, t:t + 1])
                    ins.then_inc(stat_ready, 1)
                    dve.wait_ge(root_ready, 1)
                    link(nc.vector.reciprocal(ri[:, 0, 0:TT], rt[:, 0, 0:TT]))
                    dve.wait_ge(rows_loaded, 16)
                    for t in range(TT):
                        nc.vector.scalar_tensor_tensor(X[:, t, :], X[:, t, :], ri[:, 0, t:t + 1], FG[:], ALU.mult, ALU.mult
                                                       ).then_inc(norm_ready, 1)


def constants():
    c = np.zeros((P, C_END), np.float32)
    c[:, C_ID:C_ID + P] = np.eye(P)
    c[:, C_FLIP:C_FLIP + P] = np.eye(P)[::-1]
    c[:, C_IOTA:C_IOTA + TOPK] = np.arange(TOPK)
    pos = np.arange(S, dtype=np.float32)
    inv1 = np.float32(10000.0) ** (-np.arange(0, HD, 2, dtype=np.float32) / np.float32(HD))
    ang1 = pos[:, None] * inv1[None, :].astype(np.float32)
    n = HD // 4
    inv2 = np.float32(10000.0) ** (-np.arange(n, dtype=np.float32) / np.float32(n))
    row, col = np.arange(S) // 64, np.arange(S) % 64
    ang2 = np.concatenate([row[:, None].astype(np.float32) * inv2, col[:, None].astype(np.float32) * inv2], -1)
    for c0, table in ((C_COS1, np.cos(ang1.astype(np.float64))), (C_SIN1, np.sin(ang1.astype(np.float64))),
                      (C_COS2, np.cos(ang2.astype(np.float64))), (C_SIN2, np.sin(ang2.astype(np.float64)))):
        c[:, c0:c0 + TT * 32] = table.reshape(TT, P, 32).transpose(1, 0, 2).reshape(P, TT * 32)
    dist = S - 1 - np.arange(2 * S - 1)
    exact = REL_BUCKETS // 2
    nf = np.maximum(dist, 1).astype(np.float32)
    large = exact + (np.log(nf / np.float32(exact)) / np.float32(np.log(REL_MAX / exact))
                     * np.float32(REL_BUCKETS - exact)).astype(np.int32)
    bucket = np.where(dist < exact, np.maximum(dist, 0), np.minimum(large, REL_BUCKETS - 1))
    buckets = np.zeros((REL_BUCKETS + 1, 2 * S - 1), np.float32)
    ok = dist >= 0
    buckets[bucket[ok], np.nonzero(ok)[0]] = 1.0
    buckets[REL_BUCKETS, ~ok] = MASKED
    e, q = np.arange(P)[:, None], np.arange(S)[None, :]
    decay = np.zeros((P, RET_H, 3 * P), np.float32)
    for h in range(RET_H):
        log_g = np.log(np.float32(1.0) - np.float32(2.0) ** np.float32(-5.0 - h)).astype(np.float64)
        d = q - e
        full = np.where(d >= 0, np.exp(np.maximum(d, 0) * log_g), 0.0) * HD ** -0.5
        decay[:, h, 0:S] = full
        decay[:, h, S:] = full[:, 0:P]
    return {"consts": c, "buckets": buckets, "decay": decay.reshape(P, RET_H * 3 * P)}


_INS = ["x", "w_in", "conv_w", "w_out", "ln1_g", "ln1_b", "w_up", "ffn_conv_w", "w_down", "ln2_g", "ln2_b",
        "rel_bias", "c_2", "ctx_2", "c_ctx_2", "w_mod_2", "b_mod_2", "w_in_2", "q_gain_2", "k_gain_2",
        "conv_w_2", "conv_b_2", "ln_g_2", "ln_b_2", "beta_attn_2", "beta_conv_2", "w_o_2", "peer_wq_2",
        "peer_keys_2", "peer_u_2", "peer_v_2", "final_g_2"]


def kernel(**inputs):
    import concourse.bacc as bacc
    from concourse.bass_utils import run_bass_kernel_spmd

    nc = bacc.Bacc("TRN2", target_bir_lowering=False, num_devices=1)
    arrays, aps = {}, {}
    given = {n: np.ascontiguousarray(inputs[n]) for n in _INS}
    given.update(constants())
    for name, a in given.items():
        arrays[f"in_{name}"] = a
        aps[name] = nc.dram_tensor(f"in_{name}", a.shape, mybir.dt.from_np(a.dtype), kind="ExternalInput").ap()
    out = nc.dram_tensor("out", (1, S, D), F32, kind="ExternalOutput").ap()
    program(nc, aps, out)
    r = run_bass_kernel_spmd(nc, [arrays], core_ids=[0])
    return r.results[0]["out"]
```
